# Optimizing a Trainium2 kernel written in Bass

```python
import math
import jax, jax.numpy as jnp
from jax import lax
import numpy as np

D_MODEL = 1024
BATCH = 1
SEQ = 2048
DEPTH = 1
DEC_BATCH = 8
DEC_SEQ = 8
PAST_LEN = 16384
PAGE_SIZE = 128

N_GLA_HEADS = 4
GLA_VAL_W = D_MODEL // 2
GLA_KEY_W = GLA_VAL_W // 2
GLA_DK = GLA_KEY_W // N_GLA_HEADS
GLA_DV = GLA_VAL_W // N_GLA_HEADS
GATE_RANK = 16
GATE_NORMALIZER = 16.0
GLA_CHUNK = 64
POOL_WINDOWS = (2, 4, 8, 16)
POOL_W = D_MODEL - GLA_VAL_W
POOL_GROUP = POOL_W // len(POOL_WINDOWS)
POOL_BUF = max(POOL_WINDOWS) - 1
MIX_W = GLA_VAL_W + POOL_W
IN_COLS = 2 * GLA_KEY_W + 2 * GLA_VAL_W + GATE_RANK + POOL_W
N_EXPERTS = 32
TOP_K = 4
D_FF = D_MODEL
SWIGLU_LIMIT = 7.0
SWIGLU_ALPHA = 1.702
EPS = 1e-5

kernel_name = "hybrid_gla_pool_moe_decode_step"

def rmsnorm(x, w):
    xf = x.astype(jnp.float32)
    y = xf * lax.rsqrt(jnp.mean(xf * xf, axis=-1, keepdims=True) + EPS)
    return (y * w.astype(jnp.float32)).astype(x.dtype)

def gla_scan(q, k, v, g, s0):
    B, L, H, _ = q.shape
    C = math.gcd(L, GLA_CHUNK)
    n = L // C

    def to_chunks(t):
        return t.astype(jnp.float32).reshape(B, n, C, H, t.shape[-1]).transpose(1, 0, 3, 2, 4)

    causal = jnp.tril(jnp.ones((C, C), dtype=bool))

    def step(S, inp):
        qc, kc, vc, gc = inp
        G = jnp.cumsum(gc, axis=2)
        o_inter = jnp.einsum('bhck,bhkv->bhcv', qc * jnp.exp(G), S)
        diff = G[:, :, :, None, :] - G[:, :, None, :, :]
        decay = jnp.exp(jnp.where(causal[:, :, None], diff, -jnp.inf))
        A = jnp.einsum('bhik,bhjk,bhijk->bhij', qc, kc, decay)
        o = o_inter + jnp.einsum('bhij,bhjv->bhiv', A, vc)
        G_last = G[:, :, -1:, :]
        S_new = jnp.exp(G_last[:, :, 0, :])[..., None] * S + jnp.einsum(
            'bhck,bhcv->bhkv', kc * jnp.exp(G_last - G), vc)
        return S_new, o

    S_fin, o = lax.scan(step, s0.astype(jnp.float32), (to_chunks(q), to_chunks(k), to_chunks(v), to_chunks(g)))
    o = o.transpose(1, 0, 3, 2, 4).reshape(B, L, H, v.shape[-1])
    return o, S_fin

def pool_mix(u, buf, start_pos, w_pool, pool_scale):
    B, L, _ = u.shape
    ext = jnp.concatenate([buf.astype(jnp.float32), u.astype(jnp.float32)], axis=1)
    cs = jnp.concatenate([jnp.zeros((B, 1, POOL_W), jnp.float32), jnp.cumsum(ext, axis=1)], axis=1)
    end = cs[:, POOL_BUF + 1:]
    pos = start_pos + jnp.arange(L)
    means = []
    for gi, w in enumerate(POOL_WINDOWS):
        sl = slice(gi * POOL_GROUP, (gi + 1) * POOL_GROUP)
        s = end[..., sl] - cs[:, POOL_BUF + 1 - w:POOL_BUF + 1 - w + L, sl]
        cnt = jnp.minimum(w, pos + 1).astype(jnp.float32)[None, :, None]
        means.append(s / cnt)
    d = (jnp.concatenate(means, axis=-1) - ext[:, POOL_BUF:]).reshape(B, L, len(POOL_WINDOWS), POOL_GROUP)
    z = jnp.einsum('blgc,gcd->blgd', d, w_pool.astype(jnp.float32)).reshape(B, L, POOL_W)
    z = z * pool_scale.astype(jnp.float32)
    return z.astype(u.dtype), ext[:, -POOL_BUF:].astype(u.dtype)

def mixer(xn, s0, buf, start_pos, w_in, w_gk2, b_gk, gla_norm, w_pool, pool_scale, w_o):
    B, L, _ = xn.shape
    p = xn @ w_in
    o0 = 0
    q = p[..., o0:o0 + GLA_KEY_W]; o0 += GLA_KEY_W
    k = p[..., o0:o0 + GLA_KEY_W]; o0 += GLA_KEY_W
    v = p[..., o0:o0 + GLA_VAL_W]; o0 += GLA_VAL_W
    og = p[..., o0:o0 + GLA_VAL_W]; o0 += GLA_VAL_W
    glr = p[..., o0:o0 + GATE_RANK]; o0 += GATE_RANK
    u = p[..., o0:o0 + POOL_W]
    gk = jax.nn.log_sigmoid((glr @ w_gk2).astype(jnp.float32) + b_gk.astype(jnp.float32)) / GATE_NORMALIZER
    q = q.reshape(B, L, N_GLA_HEADS, GLA_DK) * (GLA_DK ** -0.5)
    k = k.reshape(B, L, N_GLA_HEADS, GLA_DK)
    v = v.reshape(B, L, N_GLA_HEADS, GLA_DV)
    gk = gk.reshape(B, L, N_GLA_HEADS, GLA_DK)
    o, s_new = gla_scan(q, k, v, gk, s0)
    o = rmsnorm(o, gla_norm) * jax.nn.silu(og.astype(jnp.float32)).reshape(B, L, N_GLA_HEADS, GLA_DV)
    o = o.reshape(B, L, GLA_VAL_W).astype(xn.dtype)
    z, buf_new = pool_mix(u, buf, start_pos, w_pool, pool_scale)
    mix = jnp.concatenate([o, z], axis=-1) @ w_o
    return mix, s_new.astype(s0.dtype), buf_new

def moe(h, w_r, b_r, w_gu, b_gu, w_down, b_down):
    B, L, D = h.shape
    T = B * L
    x = h.reshape(T, D)
    logits = (x @ w_r).astype(jnp.float32) + b_r.astype(jnp.float32)
    top_v, top_i = lax.top_k(logits, TOP_K)
    gates = jax.nn.softmax(top_v, axis=-1)
    flat_e = top_i.reshape(-1)
    order = jnp.argsort(flat_e)
    e_sorted = flat_e[order]
    tok = order // TOP_K
    sizes = jnp.bincount(flat_e, length=N_EXPERTS).astype(jnp.int32)
    xs = x[tok]
    gu = lax.ragged_dot(xs, w_gu, sizes) + b_gu[e_sorted]
    gate = jnp.minimum(gu[:, :D_FF].astype(jnp.float32), SWIGLU_LIMIT)
    up = jnp.clip(gu[:, D_FF:].astype(jnp.float32), -SWIGLU_LIMIT, SWIGLU_LIMIT)
    act = ((up + 1.0) * gate * jax.nn.sigmoid(SWIGLU_ALPHA * gate)).astype(x.dtype)
    out = lax.ragged_dot(act, w_down, sizes) + b_down[e_sorted]
    out = (out.astype(jnp.float32) * gates.reshape(-1)[order][:, None]).astype(x.dtype)
    y = jax.ops.segment_sum(out, tok, num_segments=T)
    return y.reshape(B, L, D)

def setup_inputs(seed: int = 0) -> dict:
    key = jax.random.key(seed)
    ks = jax.random.split(key, 20)
    f = jnp.float32
    nrm = lambda k, shape, s: jax.random.normal(k, shape, f) * s
    return {
        "x_prompt": nrm(ks[0], (BATCH, SEQ, D_MODEL), 1.0),
        "x_sample": nrm(ks[1], (DEC_BATCH, DEC_SEQ, D_MODEL), 1.0),
        "state_gla": nrm(ks[2], (DEPTH, DEC_BATCH, N_GLA_HEADS, GLA_DK, GLA_DV), 0.5),
        "state_pool": nrm(ks[3], (DEPTH, DEC_BATCH, POOL_BUF, POOL_W), 1.0),
        "norm1": 1.0 + nrm(ks[4], (DEPTH, D_MODEL), 0.02),
        "w_in": nrm(ks[5], (DEPTH, D_MODEL, IN_COLS), D_MODEL ** -0.5),
        "w_gk2": nrm(ks[6], (DEPTH, GATE_RANK, GLA_KEY_W), GATE_RANK ** -0.5),
        "b_gk": nrm(ks[7], (DEPTH, GLA_KEY_W), 0.1),
        "gla_norm": 1.0 + nrm(ks[8], (DEPTH, GLA_DV), 0.02),
        "w_pool": nrm(ks[9], (DEPTH, len(POOL_WINDOWS), POOL_GROUP, POOL_GROUP), POOL_GROUP ** -0.5),
        "pool_scale": 1.0 + nrm(ks[10], (DEPTH, POOL_W), 0.02),
        "w_o": nrm(ks[11], (DEPTH, MIX_W, D_MODEL), MIX_W ** -0.5),
        "norm2": 1.0 + nrm(ks[12], (DEPTH, D_MODEL), 0.02),
        "w_router": nrm(ks[13], (DEPTH, D_MODEL, N_EXPERTS), D_MODEL ** -0.5),
        "b_router": nrm(ks[14], (DEPTH, N_EXPERTS), 0.01),
        "w_gate_up": nrm(ks[15], (DEPTH, N_EXPERTS, D_MODEL, 2 * D_FF), D_MODEL ** -0.5),
        "b_gate_up": nrm(ks[16], (DEPTH, N_EXPERTS, 2 * D_FF), 0.02),
        "w_down": nrm(ks[17], (DEPTH, N_EXPERTS, D_FF, D_MODEL), D_FF ** -0.5),
        "b_down": nrm(ks[18], (DEPTH, N_EXPERTS, D_MODEL), 0.02),
        "final_norm": 1.0 + nrm(ks[19], (D_MODEL,), 0.02),
    }

def reference(x_prompt, x_sample, state_gla, state_pool, norm1, w_in, w_gk2, b_gk, gla_norm,
              w_pool, pool_scale, w_o, norm2, w_router, b_router, w_gate_up, b_gate_up,
              w_down, b_down, final_norm):
    xp, xs = x_prompt, x_sample
    gla_p, pool_p, gla_s, pool_s = [], [], [], []
    for l in range(DEPTH):
        lw = (w_in[l], w_gk2[l], b_gk[l], gla_norm[l], w_pool[l], pool_scale[l], w_o[l])
        mw = (w_router[l], b_router[l], w_gate_up[l], b_gate_up[l], w_down[l], b_down[l])
        s0_p = jnp.zeros((BATCH, N_GLA_HEADS, GLA_DK, GLA_DV), state_gla.dtype)
        buf0_p = jnp.zeros((BATCH, POOL_BUF, POOL_W), xp.dtype)
        mix_p, sp, bp = mixer(rmsnorm(xp, norm1[l]), s0_p, buf0_p, 0, *lw)
        xp = xp + mix_p
        xp = xp + moe(rmsnorm(xp, norm2[l]), *mw)
        mix_s, ss, bs = mixer(rmsnorm(xs, norm1[l]), state_gla[l], state_pool[l], PAST_LEN, *lw)
        xs = xs + mix_s
        xs = xs + moe(rmsnorm(xs, norm2[l]), *mw)
        gla_p.append(sp); pool_p.append(bp); gla_s.append(ss); pool_s.append(bs)
    y_prompt = rmsnorm(xp, final_norm)
    y_sample = rmsnorm(xs, final_norm)
    new_gla_prompt = jnp.stack(gla_p, axis=0)
    new_pool_prompt = jnp.stack(pool_p, axis=0)
    new_gla_sample = jnp.stack(gla_s, axis=0)
    new_pool_sample = jnp.stack(pool_s, axis=0)
    return (y_prompt, y_sample, new_gla_prompt, new_pool_prompt, new_gla_sample, new_pool_sample)


_drawn_inputs = setup_inputs


def setup_inputs(seed=0):
    import zlib

    import numpy as np

    out = dict(_drawn_inputs(seed))
    spreads = {}
    factors = {'b_gate_up': 6.111, 'b_down': 7.073, 'final_norm': 2.839}
    for name, (base, spread) in spreads.items():
        noise = np.random.default_rng([zlib.crc32(name.encode()), seed]).standard_normal(out[name].shape)
        drawn = base * np.exp(spread * noise) if base else spread * noise
        out[name] = __import__('jax').numpy.asarray(drawn.astype(out[name].dtype))
    for name, factor in factors.items():
        out[name] = (out[name] * factor).astype(out[name].dtype)
    return out
```

```python
from contextlib import ExitStack

import numpy as np

import concourse.bass as bass
from concourse import mybir

F32 = mybir.dt.float32
F32R = mybir.dt.float32r
I32 = mybir.dt.int32
U32 = mybir.dt.uint32
ALU = mybir.AluOpType
ACT = mybir.ActivationFunctionType
AX = mybir.AxisListType.X

P = 128
D = 1024
KD = D // P
SEQ = 2048
NSEQ, LSEQ = 8, 8
NS = NSEQ * LSEQ
PT = SEQ // P
NT = PT + 1
TOK = SEQ + NS
H, DK, DV = 4, 64, 128
QK = H * DK
VW = H * DV
RANK = 16
GATE_DIV = 16.0
C = 64
NC = P // C
PW = 512
NG = 4
BUF = 15
O_Q, O_K, O_V, O_OG, O_GLR, O_U = 0, QK, 2 * QK, 2 * QK + VW, 2 * QK + 2 * VW, 2 * QK + 2 * VW + RANK
IN_COLS = O_U + PW
NE = 32
TOPK = 4
FF = D
EPS = 1e-5
LIMIT = 7.0
ALPHA = 1.702
CHUNK = 320
SUBS = [(0, 128), (128, 128), (256, 64)]
CPE = -(-TOK // CHUNK)
REGION = CPE * CHUNK
SLOTS = NE * REGION
MAXC = TOK * TOPK // CHUNK + NE
NTAB = 64
ROWS = TOK + CHUNK
PIECE = 4096
assert MAXC + 1 <= NTAB

def constants():
    p = np.arange(P)
    c = {}
    c["ident"] = np.eye(P, dtype=np.float32)
    c["before"] = (p[:, None] < p[None, :]).astype(np.float32)
    c["ones"] = np.ones((P, P), np.float32)
    c["scan_p"] = np.tile((np.arange(P) % C != 0).astype(np.float32), (P, 2))
    c["scan_s"] = np.tile((np.arange(NS) % LSEQ != 0).astype(np.float32), (P, 2))
    c["causal_p"] = np.tile((np.arange(C)[None, :] >= (p % C)[:, None]).astype(np.int32), (1, H))
    j, i = np.arange(NS)[:, None], np.arange(NS)[None, :]
    c["causal_s"] = np.tile(((i >= j) & (i // LSEQ == j // LSEQ)).astype(np.int32), (1, H))
    c["seq_of"] = (np.arange(NS)[:, None] // LSEQ == np.arange(NSEQ)[None, :]).astype(np.float32)
    c["expert_no"] = np.tile(np.arange(NE, dtype=np.float32), (P, TOPK))
    c["token_no"] = (p[:, None] + P * np.arange(NT)[None, :]).astype(np.int32)
    w = np.array([2, 4, 8, 16])
    first = 1.0 / np.minimum(w[:, None], np.arange(P)[None, :] + 1)
    c["inv_first"] = np.tile(first.astype(np.float32).reshape(1, -1), (P, 1))
    c["inv_rest"] = np.tile(np.repeat(1.0 / w, BUF).astype(np.float32)[None, :], (P, 1))
    slot = np.arange(SLOTS)
    c["empty_slots"] = np.stack([TOK + slot % CHUNK, 0 * slot], 1).astype(np.int32)
    c["chunk_no"] = np.repeat(np.arange(NTAB, dtype=np.float32), NE)[None, :]
    c["zero_rows"] = np.zeros((CHUNK, D), np.float32)
    return c

class Event:

    def __init__(self, ctx, nc, name, per=1):
        self.sem = ctx.enter_context(nc.semaphore(name))
        self.per = per

    def done(self, ins):
        ins.then_inc(self.sem, 1)

    def wait(self, eng, t, k=None):
        if isinstance(t, int) and t < 0:
            return
        eng.wait_ge(self.sem, t * self.per + (self.per if k is None else k))

class Tile:

    def __init__(self, pair, par, kind="p"):
        self.t = pair * 2 + par
        self.pair, self.par, self.kind = pair, par, kind
        self.n = P if kind == "p" else NS
        self.static = isinstance(self.t, int)

def mixer(nc, I, O, X, tab, ctab, eps_rows):
    with ExitStack() as ctx:
        def sb(name, shape, dt=F32):
            return ctx.enter_context(nc.sbuf_tensor(name, shape, dt))

        def sem(name):
            return ctx.enter_context(nc.semaphore(name))

        def ev(name, per=1):
            return Event(ctx, nc, name, per)

        bank = [ctx.enter_context(nc.psum_tensor(f"bank{b}", [P, 512], F32)) for b in range(8)]
        w_in = sb("w_in_sb", [P, KD, IN_COLS])
        w_o = sb("w_o_sb", [P, KD, D])
        w_r = sb("w_r_sb", [P, KD, NE])
        w_gk = sb("w_gk_sb", [RANK, QK])
        w_pool = sb("w_pool_sb", [P, NG, P])
        b_gk = sb("b_gk_sb", [P, 2])
        glan = sb("glan_sb", [P, 1])
        n1 = sb("norm1_rows", [P, D])
        n2 = sb("norm2_rows", [P, D])
        b_r = sb("b_r_rows", [P, NE])
        ident = sb("ident", [P, P])
        before = sb("before", [P, P])
        ones = sb("ones", [P, P])
        scan_p = sb("scan_p", [P, 2 * P])
        scan_s = sb("scan_s", [P, 2 * NS])
        causal_p = sb("causal_p", [P, H * C], I32)
        causal_s = sb("causal_s", [NS, H * NS], I32)
        seq_of = sb("seq_of", [NS, NSEQ])
        expert_no = sb("expert_no", [P, TOPK * NE])
        token_no = sb("token_no", [P, NT], I32)
        inv = sb("inv_count", [P, NG, P])
        inv_rest = sb("inv_rest", [P, NG * BUF])
        ss1, ms1, rs1 = sb("ss1", [P, 1]), sb("ms1", [P, 1]), sb("rs1", [P, 1])
        ss2, ms2, rs2 = sb("ss2", [P, 1]), sb("ms2", [P, 1]), sb("rs2", [P, 1])
        neghalf = sb("neghalf", [P, 4])
        x = [sb(f"x{b}", [P, D]) for b in range(2)]
        xn = sb("xn", [P, D])
        xT = sb("xT", [P, KD, P])
        qks = sb("qks", [P, 4, P])
        ux = [sb(f"ux{b}", [P, NG, BUF + P]) for b in range(2)]
        uxs = sb("uxs", [P, NG, NSEQ, BUF + LSEQ])
        uc = sb("uc", [P, NG, NS])
        glrs = sb("glrs", [RANK, P])
        zz, az, G, Dm = (sb(n, [P, 2 * P]) for n in ("zz", "az", "G", "Dm"))
        e1 = l1 = az
        gk = zz
        eq, ek = sb("eq", [P, 2 * P]), sb("ek", [P, 2 * P])
        lr = sb("lr", [P, 4])
        esm = [sb(f"esm{b}", [P, 3, 4]) for b in range(2)]
        els = sb("els", [P, 2 * NSEQ])
        qdz = [sb(f"qdz{b}", [P, H, P]) for b in range(2)]
        kd = [sb(f"kd{b}", [P, 2, P]) for b in range(2)]
        vs = [sb(f"vs{b}", [P, VW]) for b in range(2)]
        eog = sb("eog", [P, VW])
        dog = eog
        sg = [sb(f"sg{b}", [P, VW]) for b in range(2)]
        pscale = sg[0]
        pa, pb = sb("pa", [P, NG, 8 * 23]), sb("pb", [P, NG, 8 * 23])
        dT = [sb(f"dT{b}", [P, NG, P]) for b in range(2)]
        ATs = sb("ATs", [P, H, P])
        kdTz = sb("kdTz", [P, NC, 2 * P])
        S, Sm, Pt = sb("S", [P, 2, DV]), sb("Sm", [P, 2, DV]), sb("Pt", [P, 2, DV])
        Sp = [sb(f"Sp{b}", [P, 2, DV]) for b in range(2)]
        os_, osq = sb("os", [P, VW]), sb("osq", [P, VW])
        so, mso, rso = sb("so", [P, H]), sb("mso", [P, H]), sb("rso", [P, H])
        cat = sb("cat", [P, KD, P])
        h = sb("h", [P, D])
        hT = sb("hT", [P, KD, P])
        lg = sb("lg", [P, NE])
        top = sb("top", [P, 8])
        idx = sb("idx", [P, 8], U32)
        idf = sb("idf", [P, TOPK])
        ng = sb("ng", [P, 1])
        e4, sum4, rs4 = sb("e4", [P, TOPK]), sb("sum4", [P, 1]), sb("rs4", [P, 1])
        oh, ohr = sb("oh", [P, TOPK, NE]), sb("ohr", [P, TOPK, NE])
        sel, selsum = sb("sel", [P, NE]), sb("selsum", [P, NE])
        r4, slotf = sb("r4", [P, TOPK]), sb("slotf", [P, TOPK])
        slot = [sb(f"slot{b}", [P, TOPK], U32) for b in range(2)]
        meta = [sb(f"meta{b}", [P, TOPK, 2], I32) for b in range(2)]
        Q8 = w_in[:, 0, 0:2048].rearrange("p (a b n) -> p a b n", a=H, b=NSEQ)
        kdT8 = w_in[0:NS, 1, 0:2048].rearrange("p (b n) -> p b n", b=NSEQ)
        ge = w_in[0:1, 2, 0:2048].rearrange("p (i e) -> p i e", e=NE)
        geb = w_in[0:1, 3, 0:2048].rearrange("p (i e) -> p i e", e=NE)
        chunk_no = w_in[0:1, 4, 0:2048]
        S0 = w_in[:, 5, 0:2048].rearrange("p (b a v) -> p b a v", b=NSEQ, a=2)
        pool_old = sb("pool_old", [NSEQ * BUF, PW])
        last_rows = sg[1][0:BUF, :]
        os_new = vs[1][0:NS, :]

        w_sem, wo_sem, c_sem = sem("w_loaded"), sem("wo_loaded"), sem("consts_loaded")
        init_sem = sem("dram_init")
        x_in = [sem("x_in0"), sem("x_in1")]
        y_st, h_st = [sem("y_stored0")], [sem("h_stored0")]
        slot_st = [sem("slots_scattered0"), sem("slots_scattered1")]
        old_st = sem("states_stored")
        s0_in = sem("sampled_states_loaded")
        no_sem = sem("chunk_numbers_loaded")
        memo = ev("cleared")
        E = {n: ev(n, per) for n, per in dict(
            ss1=1, ms1=1, rs1=1, xn=1, trA=1, trB=1, xTe=2, glr=1, qk=1, u=1, z=1, v=1, og=1,
            qks=1, uxe=1, glrs=1, vse=1, eog=1, e1=1, l1=1, zz=2, az=1, gk=1, G=1, Dm=1, lr=1,
            eqk=2, esm=3, dog=1, rog=1, sg=1, qdz=2, kd=1, hist=1, pool=5, mean=2, dT=1,
            AT=1, kdT=1, ATs=2, kdTz=2, Sp=2, Pc=2, Pt=4, Sm=2, S=2, zp=1, zpe=1, o=1, os=1, osq=1,
            so=1, mso=1, rso=1, on1=1, on=1, oT=1, oTe=1, mix=2, x1=2, ss2=1, ms2=1, rs2=1, h=1,
            hA=1, hB=1, hTe=2, lgp=1, lg=1, top=1, idx=1, idf=1, ng=1, e4=1, rs4=1, gate=1, oh=1,
            sel=1, rank=1, ohr=1, r4=1, slotf=1, slot=1, tokid=1, selsum=1).items()}
        s_misc = ev("sample_steps")
        s_misc2 = ev("sample_inputs_kept")
        s_S8, s_P8, s_T8 = ev("s_S8"), ev("s_P8"), ev("s_T8")
        s_tab = ev("table_steps")
        s_cnt = ev("counted")
        s_old, s_olde, s_newt, s_newe, s_pnt, s_pne = (ev(n) for n in (
            "old_rows_turned", "old_rows_kept", "new_rows_turned", "new_rows_kept",
            "prompt_rows_turned", "prompt_rows_kept"))
        N_W, N_C = 8, 16

        block = ctx.enter_context(nc.Block())
        xp, xs = I["x_prompt"][0], I["x_sample"].rearrange("b l d -> (b l) d")

        def rows_of(ap, T):
            return ap[SEQ:TOK, :] if T.kind == "s" else ap[bass.ds(T.t * P, P), :]

        def wv(E_, eng, T, k=None, back=0):
            E[E_].wait(eng, T.t - back, k)

        def waitx(eng, T):
            eng.wait_ge(x_in[T.par], T.pair * 16 + 16)

        @block.sync
        def _(sp):
            def c_load(dst, src):
                sp.dma_start(dst, src).then_inc(c_sem, 16)

            def load_x(T):
                if T.t > 1:
                    sp.wait_ge(y_st[0], 16 * (T.t - 1))
                wv("h", sp, T, back=2)
                src = xs if T.kind == "s" else xp[bass.ds(T.t * P, P), :]
                sp.dma_start(x[T.par][0:T.n, :], src).then_inc(x_in[T.par], 16)

            def store(T):
                wv("x1", sp, T)
                sp.dma_start(rows_of(X["y"], T), x[T.par][0:T.n, :]).then_inc(y_st[0], 16)
                wv("h", sp, T)
                sp.dma_start(rows_of(X["h"], T), h[0:T.n, :]).then_inc(h_st[0], 16)

            load_x(Tile(0, 0))
            c_load(n1[:, :], I["norm1"].partition_broadcast(P))
            c_load(ident[:, :], I["ident"])
            win = I["w_in"][0].rearrange("(k p) n -> p k n", p=P)
            for k0 in range(0, KD, 4):
                sp.dma_start(w_in[:, k0:k0 + 4, :], win[:, k0:k0 + 4, :]).then_inc(w_sem, 16)
            sp.dma_start(w_gk[:, :], I["w_gk2"][0]).then_inc(w_sem, 16)
            load_x(Tile(0, 1))
            for dst, src in ((b_gk, I["b_gk"][0].rearrange("(a p) -> p a", p=P)),
                             (glan, I["gla_norm"].rearrange("a p -> p a")),
                             (n2, I["norm2"].partition_broadcast(P)),
                             (b_r, I["b_router"].partition_broadcast(P)),
                             (before, I["before"]), (ones, I["ones"]), (scan_p, I["scan_p"]),
                             (causal_p, I["causal_p"]), (expert_no, I["expert_no"]),
                             (token_no, I["token_no"]), (inv_rest, I["inv_rest"])):
                with nc.allow_non_contiguous_dma(reason="a few hundred bias elements"):
                    c_load(dst[:, :], src)
            c_load(inv[:, :, :].rearrange("p g t -> p (g t)"), I["inv_first"])
            c_load(pscale[:, :], I["pool_scale"].partition_broadcast(P))
            sp.dma_start(w_pool[:, :, :], I["w_pool"][0].rearrange("g c e -> c g e")).then_inc(w_sem, 16)
            wo = I["w_o"][0].rearrange("(k p) n -> p k n", p=P)
            for k0 in range(0, KD, 4):
                sp.dma_start(w_o[:, k0:k0 + 4, :], wo[:, k0:k0 + 4, :]).then_inc(wo_sem, 16)
            sp.dma_start(w_r[:, :, :], I["w_router"][0].rearrange("(k p) n -> p k n", p=P)).then_inc(wo_sem, 16)
            sp.dma_start(X["slots"][:, :], I["empty_slots"]).then_inc(init_sem, 16)
            sp.dma_start(X["h"][TOK:ROWS, :], I["zero_rows"]).then_inc(init_sem, 16)
            sp.dma_start(X["y"][TOK:ROWS, :], I["zero_rows"]).then_inc(init_sem, 16)
            for dst, src in ((scan_s, I["scan_s"]), (causal_s, I["causal_s"]), (seq_of, I["seq_of"])):
                c_load(dst[:, :], src)
            c_load(pool_old[:, :], I["state_pool"][0].rearrange("b r c -> (b r) c"))
            sp.dma_start(O["pool_s"][0, :, 0:BUF - LSEQ, :],
                         I["state_pool"][0, :, LSEQ:BUF, :]).then_inc(old_st, 16)
            for t in range(2):
                store(Tile(0, t))
                load_x(Tile(1, t))
            with sp.Fori(1, PT // 2 - 1) as i:
                for t in range(2):
                    store(Tile(i, t))
                    sp.wait_ge(y_st[0], 16 * (i * 2 + t + 1))
                    wv("h", sp, Tile(i, t))
                    sp.dma_start(x[t][:, :], xp[bass.ds((i * 2 + t + 2) * P, P), :]).then_inc(x_in[t], 16)
            store(Tile(PT // 2 - 1, 0))
            load_x(Tile(PT // 2, 0, "s"))
            store(Tile(PT // 2 - 1, 1))
            E["S"].wait(sp, PT - 1)
            for c in range(2):
                sp.dma_start(O["gla_p"][0, 0].rearrange("(a c) k v -> c k a v", c=2)[c],
                             S[c * DK:(c + 1) * DK, :, :]).then_inc(old_st, 16)
            s_pne.wait(sp, 0)
            sp.dma_start(O["pool_p"][0, 0], last_rows).then_inc(old_st, 16)
            E["og"].wait(sp, PT)
            sg_in = I["state_gla"][0].rearrange("b (a c) k v -> c k b a v", c=2)
            for c in range(2):
                for a in range(2):
                    sp.dma_start(S0[c * DK:(c + 1) * DK, :, a, :], sg_in[c, :, :, a, :]).then_inc(s0_in, 16)
            sp.dma_start(chunk_no, I["chunk_no"]).then_inc(no_sem, 16)
            store(Tile(PT // 2, 0, "s"))
            s_newe.wait(sp, 0)
            for b in range(NSEQ):
                sp.dma_start(O["pool_s"][0, b, BUF - LSEQ:BUF, :],
                             os_new[b * LSEQ:(b + 1) * LSEQ, :]).then_inc(old_st, 16)
            s_S8.wait(sp, 0, NSEQ)
            sg_out = O["gla_s"][0].rearrange("b (a c) k v -> c k b a v", c=2)
            for c in range(2):
                for a in range(2):
                    sp.dma_start(sg_out[c, :, :, a, :], S0[c * DK:(c + 1) * DK, :, a, :]).then_inc(old_st, 16)
            sp.wait_ge(old_st, 16 * (1 + 2 + 1 + NSEQ + 4))
            sp.wait_ge(y_st[0], 16 * NT)
            sp.wait_ge(h_st[0], 16 * NT)
            sp.wait_ge(init_sem, 48)
            sp.wait_ge(slot_st[0], 64 * ((NT + 1) // 2))
            sp.wait_ge(slot_st[1], 64 * (NT // 2))

        @block.tensor
        def _(pe):
            B = bank

            def turn(src, b, ks, n, e):
                for q, k in enumerate(ks):
                    ins = pe.transpose(B[b][:, q * n:(q + 1) * n], src[0:n, k * P:(k + 1) * P], ident[0:n, 0:n])
                E[e].done(ins)

            def proj_T(b, cols, n, e, m=P):
                for q, c0 in enumerate(cols):
                    for k in range(KD):
                        ins = pe.matmul(B[b][0:m, q * n:(q + 1) * n], w_in[:, k, c0:c0 + m], xT[:, k, 0:n],
                                        start=(k == 0), stop=(k == KD - 1))
                E[e].done(ins)

            def proj(b, c0, n, e):
                for k in range(KD):
                    ins = pe.matmul(B[b][0:n, :], xT[:, k, 0:n], w_in[:, k, c0:c0 + 512],
                                    start=(k == 0), stop=(k == KD - 1))
                E[e].done(ins)

            def f_turn(T):
                wv("xn", pe, T)
                wv("vse", pe, T, back=1)
                turn(xn, 0, range(4), T.n, "trA")
                wv("sg", pe, T, back=1)
                turn(xn, 1, range(4, 8), T.n, "trB")

            def f_glr(T):
                wv("xTe", pe, T)
                wv("zz", pe, T, back=1)
                proj_T(7, [O_GLR], T.n, "glr", RANK)

            def f_qk(T):
                wv("qks", pe, T, back=1)
                proj_T(2, [O_Q, O_Q + P, O_K, O_K + P], T.n, "qk")

            def f_z(T):
                wv("glrs", pe, T)
                for a in range(2):
                    ins = pe.matmul(B[7][:, a * T.n:(a + 1) * T.n], w_gk[:, a * P:(a + 1) * P],
                                    glrs[:, 0:T.n], start=True, stop=True)
                E["z"].done(ins)

            def f_u(T):
                wv("uxe", pe, T, back=1)
                proj_T(3, [O_U + g * P for g in range(NG)], T.n, "u")

            def f_v(T):
                proj(0, O_V, T.n, "v")

            def f_og(T):
                proj(1, O_OG, T.n, "og")

            def m_AT(T):
                wv("qdz", pe, T)
                wv("kd", pe, T)
                wv("hTe", pe, T, back=1)
                for a in range(H):
                    for c in range(NC):
                        ins = pe.matmul(B[4][c * C:(c + 1) * C, a * C:(a + 1) * C],
                                        kd[T.par][:, a // 2, c * C:(c + 1) * C],
                                        qdz[T.par][:, a, c * C:(c + 1) * C], start=True, stop=True,
                                        skip_group_check=True)
                E["AT"].done(ins)
                for a in range(2):
                    ins = pe.transpose(B[4][:, 256 + a * P:256 + (a + 1) * P], kd[T.par][:, a, :], ident[:, :])
                E["kdT"].done(ins)

            def m_o0(T):
                wv("ATs", pe, T)
                wv("vse", pe, T)
                wv("lg", pe, T, back=1)
                for a in range(H):
                    pe.matmul(B[5][:, a * DV:(a + 1) * DV], ATs[:, a, :], vs[T.par][:, a * DV:(a + 1) * DV],
                              start=(a == 0), stop=False, skip_group_check=True)
                wv("Sp", pe, T, 1)
                m_inter(T, 0)

            def m_inter(T, c):
                for a in range(H):
                    ins = pe.matmul(B[5][c * C:(c + 1) * C, a * DV:(a + 1) * DV],
                                    qdz[T.par][:, a, c * C:(c + 1) * C], Sp[c][:, a // 2, :],
                                    start=False, stop=(a == H - 1), skip_group_check=True)
                if c == NC - 1:
                    E["o"].done(ins)

            def m_P(T, c):
                wv("kdTz", pe, T)
                if c == 0:
                    wv("ohr", pe, T, back=1)
                else:
                    wv("Pt", pe, T, 2)
                for a in range(2):
                    ins = pe.matmul(B[6][:, a * 256:(a + 1) * 256], kdTz[:, c, a * P:(a + 1) * P],
                                    vs[T.par][:, a * 256:(a + 1) * 256], start=True, stop=True)
                E["Pc"].done(ins)

            def m_pool(T):
                wv("dT", pe, T)
                wv("kdTz", pe, T)
                for g in range(NG):
                    ins = pe.matmul(B[4][:, g * T.n:(g + 1) * T.n], w_pool[:, g, :], dT[T.par][:, g, 0:T.n],
                                    start=True, stop=True)
                E["zp"].done(ins)

            def m_oT(T):
                wv("on", pe, T)
                if T.kind == "p":
                    wv("Pt", pe, T)
                for a in range(H):
                    ins = pe.transpose(B[6][:, a * T.n:(a + 1) * T.n], osq[0:T.n, a * P:(a + 1) * P],
                                       ident[0:T.n, 0:T.n])
                E["oT"].done(ins)

            def b_mix(T):
                wv("oTe", pe, T)
                wv("zpe", pe, T)
                wv("os", pe, T)
                for half in range(2):
                    for k in range(KD):
                        ins = pe.matmul(B[4 + half][0:T.n, :], cat[:, k, 0:T.n],
                                        w_o[:, k, half * 512:(half + 1) * 512],
                                        start=(k == 0), stop=(k == KD - 1))
                    E["mix"].done(ins)

            def b_hT(T):
                wv("h", pe, T)
                turn(h, 6, range(4), T.n, "hA")
                turn(h, 4, range(4, 8), T.n, "hB")

            def b_router(T):
                wv("hTe", pe, T)
                for k in range(KD):
                    ins = pe.matmul(B[5][0:T.n, 0:NE], hT[:, k, 0:T.n], w_r[:, k, :],
                                    start=(k == 0), stop=(k == KD - 1))
                E["lgp"].done(ins)

            def b_rank(T):
                wv("sel", pe, T)
                pe.matmul(B[6][0:T.n, 0:NE], before[0:T.n, 0:T.n], sel[0:T.n, :], start=True, stop=False)
                wv("selsum", pe, T, back=1)
                ins = pe.matmul(B[6][0:T.n, 0:NE], ones[:, 0:T.n], selsum[:, :], start=False, stop=True)
                E["rank"].done(ins)

            def front(T):
                f_turn(T)
                f_glr(T)
                f_qk(T)
                f_z(T)
                f_u(T)
                f_v(T)
                f_og(T)

            def back(T):
                m_AT(T)
                m_o0(T)
                m_P(T, 0)
                m_pool(T)
                wv("Sp", pe, T, 2)
                m_inter(T, 1)
                m_P(T, 1)
                m_oT(T)
                b_mix(T)
                b_hT(T)
                b_router(T)
                b_rank(T)

            pe.wait_ge(c_sem, 16 * N_CONST)
            pe.wait_ge(w_sem, 16 * 4)
            pe.wait_ge(wo_sem, 16 * 3)
            memo.wait(pe, 0, 7)
            for t in range(2):
                front(Tile(0, t))
                back(Tile(0, t))
            with pe.Fori(1, PT // 2) as i:
                for t in range(2):
                    front(Tile(i, t))
                    back(Tile(i, t))
            E["hTe"].wait(pe, PT - 1)
            for g in range(NG):
                ins = pe.transpose(B[4][0:BUF, g * P:(g + 1) * P], ux[1][:, g, P:P + BUF], ident[:, :])
            s_pnt.done(ins)
            T = Tile(PT // 2, 0, "s")
            s_pne.wait(pe, 0)
            for g in range(NG):
                ins = pe.transpose(B[4][:, g * 120:(g + 1) * 120], pool_old[:, g * P:(g + 1) * P],
                                   ident[0:120, 0:120])
            s_old.done(ins)
            front(T)
            E["uxe"].wait(pe, PT)
            s_olde.wait(pe, 0)
            for g in range(NG):
                ins = pe.transpose(B[4][0:NS, g * P:(g + 1) * P], uc[:, g, :], ident[:, :])
            s_newt.done(ins)
            wv("qdz", pe, T)
            wv("kd", pe, T)
            s_newe.wait(pe, 0)
            for a in range(H):
                ins = pe.matmul(B[4][0:NS, a * NS:(a + 1) * NS], kd[0][:, a // 2, 0:NS], qdz[0][:, a, 0:NS],
                                start=True, stop=True, skip_group_check=True)
            E["AT"].done(ins)
            for a in range(2):
                ins = pe.transpose(B[4][0:NS, 256 + a * P:256 + (a + 1) * P], kd[0][:, a, 0:NS], ident[:, :])
            E["kdT"].done(ins)
            wv("ATs", pe, T)
            wv("vse", pe, T)
            wv("lg", pe, T, back=1)
            for a in range(H):
                pe.matmul(B[5][0:NS, a * DV:(a + 1) * DV], ATs[0:NS, a, 0:NS], vs[0][0:NS, a * DV:(a + 1) * DV],
                          start=(a == 0), stop=False, skip_group_check=True)
            pe.wait_ge(s0_in, 64)
            s_misc.wait(pe, 0, NSEQ)
            for b in range(NSEQ):
                for a in range(H):
                    ins = pe.matmul(B[5][0:NS, a * DV:(a + 1) * DV], Q8[:, a, b, :], S0[:, b, a // 2, :],
                                    start=False, stop=(b == NSEQ - 1), skip_group_check=True)
            E["o"].done(ins)
            wv("ohr", pe, T, back=1)
            for b in range(NSEQ):
                s_T8.wait(pe, 0, b + 1)
                if b:
                    s_S8.wait(pe, 0, b)
                for a in range(2):
                    ins = pe.matmul(B[6][:, a * 256:(a + 1) * 256], kdT8[:, b, a * P:(a + 1) * P],
                                    vs[0][0:NS, a * 256:(a + 1) * 256], start=True, stop=True)
                s_P8.done(ins)
            s_T8.wait(pe, 0, NSEQ)
            wv("dT", pe, T)
            for g in range(NG):
                ins = pe.matmul(B[4][:, g * NS:(g + 1) * NS], w_pool[:, g, :], dT[0][:, g, 0:NS],
                                start=True, stop=True)
            E["zp"].done(ins)
            s_S8.wait(pe, 0, NSEQ)
            m_oT(T)
            b_mix(T)
            b_hT(T)
            b_router(T)
            b_rank(T)
            E["selsum"].wait(pe, PT)
            E["ohr"].wait(pe, PT)
            s_cnt.done(pe.matmul(B[6][:, 0:NE], ones[:, :], selsum[:, :], start=True, stop=True))

        @block.scalar
        def _(act):
            B = bank

            def f_ss(T):
                waitx(act, T)
                wv("trB", act, T, back=1)
                E["ss1"].done(act.activation(xn[0:T.n, :], x[T.par][0:T.n, :], ACT.Square,
                                             accum_out=ss1[0:T.n, :]))

            def f_xT(T):
                for half, e in enumerate(("trA", "trB")):
                    wv(e, act, T)
                    if half == 0:
                        wv("og", act, T, back=1)
                    E["xTe"].done(act.activation(
                        xT[:, 4 * half:4 * half + 4, 0:T.n],
                        B[half][:, 0:4 * T.n].rearrange("p (k n) -> p k n", k=4), ACT.Copy))

            def f_glr(T):
                wv("glr", act, T)
                E["glrs"].done(act.activation(glrs[:, 0:T.n], B[7][0:RANK, 0:T.n], ACT.Copy))

            def f_qk(T):
                wv("qk", act, T)
                wv("kd", act, T, back=1)
                E["qks"].done(act.activation(qks[:, :, 0:T.n], B[2][:, 0:4 * T.n].rearrange(
                    "p (k n) -> p k n", k=4), ACT.Copy))

            def f_gate(T):
                wv("az", act, T)
                E["e1"].done(act.activation(e1[:, 0:2 * T.n], az[:, 0:2 * T.n], ACT.Exp, scale=-1.0))
                wv("e1", act, T)
                E["l1"].done(act.activation(l1[:, 0:2 * T.n], e1[:, 0:2 * T.n], ACT.Ln, bias=1.0))

            def f_u(T):
                wv("u", act, T)
                src = B[3][:, 0:4 * T.n]
                if T.kind == "p":
                    wv("dT", act, T, back=2)
                    wv("hist", act, T, back=1)
                    E["uxe"].done(act.activation(ux[T.par][:, :, BUF:], src.rearrange("p (g n) -> p g n", g=NG),
                                                 ACT.Copy))
                else:
                    s_misc2.done(act.activation(uxs[:, :, :, BUF:], src.rearrange(
                        "p (g s l) -> p g s l", g=NG, l=LSEQ), ACT.Copy))
                    E["uxe"].done(act.activation(uc[:, :, :], src.rearrange("p (g n) -> p g n", g=NG), ACT.Copy))

            def f_v(T):
                wv("v", act, T)
                wv("Pc", act, T, back=2)
                E["vse"].done(act.activation(vs[T.par][0:T.n, :], B[0][0:T.n, :], ACT.Copy))

            def f_og(T):
                wv("og", act, T)
                E["eog"].done(act.activation(eog[0:T.n, :], B[1][0:T.n, :], ACT.Exp, scale=-1.0))

            def f_decay(T):
                wv("Dm", act, T)
                wv("qdz", act, T, back=1)
                E["eqk"].done(act.activation(eq[:, 0:2 * T.n], Dm[:, 0:2 * T.n], ACT.Exp, scale=1 / GATE_DIV))
                wv("kd", act, T, back=1)
                E["eqk"].done(act.activation(ek[:, 0:2 * T.n], Dm[:, 0:2 * T.n], ACT.Exp, scale=-1 / GATE_DIV))

            def f_small(T):
                wv("Pt", act, T, back=2)
                Gc = G[:, :].rearrange("p (q c) -> p q c", c=C)
                E["esm"].done(act.activation(esm[T.par][:, 0, :], Gc[:, :, C // 2 - 1], ACT.Exp, scale=1 / GATE_DIV))
                E["esm"].done(act.activation(esm[T.par][:, 1, :], Gc[:, :, C - 1], ACT.Exp, scale=1 / GATE_DIV))
                wv("lr", act, T)
                E["esm"].done(act.activation(esm[T.par][:, 2, :], lr[:, :], ACT.Exp, scale=1 / GATE_DIV))

            def m_os(T):
                wv("o", act, T)
                wv("on", act, T, back=1)
                E["os"].done(act.activation(os_[0:T.n, :], B[5][0:T.n, :], ACT.Copy))

            def m_pool(T):
                wv("zp", act, T)
                wv("mix", act, T, back=1)
                E["zpe"].done(act.activation(cat[:, NG:, 0:T.n], B[4][:, 0:4 * T.n].rearrange(
                    "p (g n) -> p g n", g=NG), ACT.Copy))

            def m_oT(T):
                wv("oT", act, T)
                E["oTe"].done(act.activation(cat[:, 0:H, 0:T.n], B[6][:, 0:4 * T.n].rearrange(
                    "p (g n) -> p g n", g=H), ACT.Copy, scale=glan[:, 0:1]))

            def b_ss(T):
                wv("x1", act, T)
                wv("hB", act, T, back=1)
                if not (T.static and T.t == 0):
                    act.wait_ge(h_st[0], T.t * 16)
                E["ss2"].done(act.activation(h[0:T.n, :], x[T.par][0:T.n, :], ACT.Square, accum_out=ss2[0:T.n, :]))

            def b_hT(T):
                for half, e in enumerate(("hA", "hB")):
                    wv(e, act, T)
                    b = (6, 4)[half]
                    E["hTe"].done(act.activation(hT[:, 4 * half:4 * half + 4, 0:T.n],
                                                 B[b][:, 0:4 * T.n].rearrange("p (k n) -> p k n", k=4), ACT.Copy))

            def b_gates(T):
                wv("ng", act, T)
                E["e4"].done(act.activation(e4[0:T.n, :], top[0:T.n, 0:TOPK], ACT.Exp, bias=ng[0:T.n, 0:1],
                                            accum_out=sum4[0:T.n, :]))

            def front(T):
                f_ss(T)
                f_xT(T)
                f_glr(T)
                f_qk(T)
                f_gate(T)
                f_u(T)
                f_decay(T)
                f_small(T)
                f_v(T)
                f_og(T)

            def back(T):
                m_pool(T)
                m_os(T)
                m_oT(T)
                b_ss(T)
                b_hT(T)
                b_gates(T)

            act.wait_ge(c_sem, 16 * N_CONST)
            for t in range(2):
                front(Tile(0, t))
                back(Tile(0, t))
            with act.Fori(1, PT // 2) as i:
                for t in range(2):
                    front(Tile(i, t))
                    back(Tile(i, t))
            s_pnt.wait(act, 0)
            E["on1"].wait(act, PT - 1)
            s_pne.done(act.activation(last_rows.rearrange("r (g c) -> r g c", g=NG), B[4][0:BUF, :].rearrange("r (g c) -> r g c", g=NG),
                                      ACT.Copy))
            s_old.wait(act, 0)
            s_olde.done(act.activation(uxs[:, :, :, 0:BUF], B[4][:, 0:480].rearrange(
                "p (g s r) -> p g s r", g=NG, s=NSEQ), ACT.Copy))
            T = Tile(PT // 2, 0, "s")
            f_ss(T)
            f_xT(T)
            f_glr(T)
            f_qk(T)
            f_gate(T)
            f_u(T)
            wv("G", act, T)
            E["eqk"].done(act.activation(eq[:, 0:2 * NS], G[:, 0:2 * NS], ACT.Exp, scale=1 / GATE_DIV))
            E["eqk"].done(act.activation(ek[:, 0:2 * NS], G[:, 0:2 * NS], ACT.Exp, scale=-1 / GATE_DIV))
            E["esm"].done(act.activation(els[:, :], G[:, 0:2 * NS].rearrange("p (q l) -> p q l", l=LSEQ)[:, :, LSEQ - 1],
                                         ACT.Exp, scale=1 / GATE_DIV))
            f_v(T)
            f_og(T)
            s_newt.wait(act, 0)
            s_newe.done(act.activation(os_new, B[4][0:NS, :], ACT.Copy))
            m_os(T)
            m_pool(T)
            m_oT(T)
            b_ss(T)
            b_hT(T)
            b_gates(T)

        @block.vector
        def _(dve):
            B = bank

            def tt(e, out, a, b, op):
                E[e].done(dve.tensor_tensor(out, a, b, op))

            def f_ms(T):
                wv("ss1", dve, T)
                E["ms1"].done(dve.tensor_scalar(ms1[0:T.n, :], ss1[0:T.n, :], 1.0 / D, EPS, ALU.mult, ALU.add))
                wv("rs1", dve, T)
                waitx(dve, T)
                wv("trB", dve, T, back=1)
                E["xn"].done(dve.scalar_tensor_tensor(xn[0:T.n, :], x[T.par][0:T.n, :], rs1[0:T.n, 0:1],
                                                      n1[0:T.n, :], ALU.mult, ALU.mult))

            def f_gate(T):
                n2_ = 2 * T.n
                wv("z", dve, T)
                for a in range(2):
                    E["zz"].done(dve.tensor_scalar(zz[:, a * T.n:(a + 1) * T.n], B[7][:, a * T.n:(a + 1) * T.n],
                                                   b_gk[:, a:a + 1], None, ALU.add))
                wv("zz", dve, T)
                E["az"].done(dve.scalar_tensor_tensor(az[:, 0:n2_], zz[:, 0:n2_], -1.0, zz[:, 0:n2_],
                                                      ALU.mult, ALU.max))
                wv("l1", dve, T)
                E["gk"].done(dve.scalar_tensor_tensor(gk[:, 0:n2_], zz[:, 0:n2_], 0.0, l1[:, 0:n2_],
                                                      ALU.min, ALU.subtract))
                wv("gk", dve, T)
                mask = scan_p if T.kind == "p" else scan_s
                wv("esm", dve, T, back=1)
                E["G"].done(dve.tensor_tensor_scan(G[:, 0:n2_], mask[:, 0:n2_], gk[:, 0:n2_], 0.0,
                                                   ALU.mult, ALU.add))
                wv("G", dve, T)
                if T.kind == "p":
                    Gc = G[:, :].rearrange("p (q c) -> p q c", c=C)
                    wv("eqk", dve, T, back=1)
                    tt("Dm", Dm[:, :].rearrange("p (q c) -> p q c", c=C), Gc,
                       Gc[:, :, C // 2 - 1:C // 2].to_broadcast([P, 4, C]), ALU.subtract)
                    tt("lr", lr[:, :], Gc[:, :, C - 1], Gc[:, :, C // 2 - 1], ALU.subtract)

            def f_og(T):
                wv("eog", dve, T)
                E["dog"].done(dve.tensor_scalar(dog[0:T.n, :], eog[0:T.n, :], 1.0, None, ALU.add))
                wv("dog", dve, T)
                E["rog"].done(dve.reciprocal(dog[0:T.n, :], dog[0:T.n, :]))
                wv("rog", dve, T)
                tt("sg", sg[T.par][0:T.n, :], B[1][0:T.n, :], dog[0:T.n, :], ALU.mult)

            def f_qd(T):
                n = T.n
                wv("qks", dve, T)
                wv("eqk", dve, T)
                wv("o", dve, T, back=2)
                eqv = eq[:, 0:2 * n].rearrange("p (a n) -> p a n", a=2)
                ekv = ek[:, 0:2 * n].rearrange("p (a n) -> p a n", a=2)
                for r in range(2):
                    s = slice(r * DK, (r + 1) * DK)
                    E["qdz"].done(dve.scalar_tensor_tensor(qdz[T.par][s, r::2, 0:n], qks[s, 0:2, 0:n], DK ** -0.5,
                                                           eqv[s], ALU.mult, ALU.mult))
                wv("kdT", dve, T, back=2)
                tt("kd", kd[T.par][:, :, 0:n], qks[:, 2:4, 0:n], ekv, ALU.mult)

            def m_AT(T):
                wv("kdT", dve, T)
                wv("o", dve, T, back=1)
                for c in range(NC):
                    s = slice(c * C, (c + 1) * C)
                    E["kdTz"].done(dve.tensor_copy(kdTz[s, c, :], B[4][s, 256:512]))
                for c in range(NC):
                    s = slice(c * C, (c + 1) * C)
                    E["ATs"].done(dve.copy_predicated(
                        ATs[s, :, s], causal_p[s, :].rearrange("p (a i) -> p a i", a=H),
                        B[4][s, 0:H * C].rearrange("p (a i) -> p a i", a=H)))

            def small(T, k, c, s=slice(0, P)):
                return esm[T.par][s, k, c::NC].unsqueeze(2).to_broadcast([s.stop - s.start, 2, DV])

            def m_Sp(T, c):
                if c == 0:
                    wv("esm", dve, T)
                    wv("S", dve, T, back=1)
                else:
                    wv("S", dve, T, 1)
                tt("Sp", Sp[c][:, :, :], S[:, :, :], small(T, 0, c), ALU.mult)

            def m_S(T, c):
                tt("Sm", Sm[:, :, :], S[:, :, :], small(T, 1, c), ALU.mult)
                wv("Pc", dve, T, c + 1)
                for r in range(2):
                    s = slice(r * DK, (r + 1) * DK)
                    src = B[6][s, :].rearrange("p (a b v) -> p a b v", a=2, b=2)[:, :, r, :]
                    tt("Pt", Pt[s, :, :], src, small(T, 2, c, s), ALU.mult)
                wv("Sm", dve, T, c + 1)
                wv("Pt", dve, T, 2 * c + 2)
                tt("S", S[:, :, :], Sm[:, :, :], Pt[:, :, :], ALU.add)

            def m_o(T):
                n = T.n
                wv("os", dve, T)
                wv("oT", dve, T, back=1)
                tt("osq", osq[0:n, :], os_[0:n, :], os_[0:n, :], ALU.mult)
                wv("osq", dve, T)
                E["so"].done(dve.tensor_reduce(so[0:n, :], osq[0:n, :].rearrange("p (a v) -> p a v", a=H), AX, ALU.add))
                wv("so", dve, T)
                E["mso"].done(dve.tensor_scalar(mso[0:n, :], so[0:n, :], 1.0 / DV, EPS, ALU.mult, ALU.add))
                wv("sg", dve, T)
                tt("on1", os_[0:n, :], os_[0:n, :], sg[T.par][0:n, :], ALU.mult)
                wv("rso", dve, T)
                wv("on1", dve, T)
                tt("on", osq[0:n, :].rearrange("p (a v) -> p a v", a=H),
                   os_[0:n, :].rearrange("p (a v) -> p a v", a=H),
                   rso[0:n, :].unsqueeze(2).to_broadcast([n, H, DV]), ALU.mult)

            def b_x1(T):
                for half in range(2):
                    c = slice(half * 512, (half + 1) * 512)
                    wv("mix", dve, T, half + 1)
                    tt("x1", x[T.par][0:T.n, c], B[4 + half][0:T.n, :], x[T.par][0:T.n, c], ALU.add)

            def b_h(T):
                wv("ss2", dve, T)
                E["ms2"].done(dve.tensor_scalar(ms2[0:T.n, :], ss2[0:T.n, :], 1.0 / D, EPS, ALU.mult, ALU.add))
                wv("rs2", dve, T)
                wv("x1", dve, T)
                E["h"].done(dve.scalar_tensor_tensor(h[0:T.n, :], x[T.par][0:T.n, :], rs2[0:T.n, 0:1], n2[0:T.n, :],
                                                     ALU.mult, ALU.mult))

            def b_top(T):
                n = T.n
                wv("lgp", dve, T)
                tt("lg", lg[0:n, :], B[5][0:n, 0:NE], b_r[0:n, :], ALU.add)
                pairs = T.pair * 64
                if not (isinstance(pairs, int) and pairs == 0):
                    dve.wait_ge(slot_st[T.par], pairs)
                wv("lg", dve, T)
                tok = token_no[:, PT:NT] if T.kind == "s" else token_no[:, bass.ds(T.t, 1)]
                E["tokid"].done(dve.tensor_copy(meta[T.par][0:n, :, 0], tok[0:n, :].to_broadcast([n, TOPK])))
                E["top"].done(dve.max(top[0:n, :], lg[0:n, :]))
                wv("top", dve, T)
                E["ng"].done(dve.tensor_scalar(ng[0:n, :], top[0:n, 0:1], -1.0, None, ALU.mult))
                E["idx"].done(dve.max_index(idx[0:n, :], top[0:n, :], lg[0:n, :]))
                wv("idx", dve, T)
                E["idf"].done(dve.tensor_copy(idf[0:n, :], idx[0:n, 0:TOPK]))
                wv("idf", dve, T)
                tt("oh", oh[0:n, :, :], expert_no[0:n, :].rearrange("p (k e) -> p k e", k=TOPK),
                   idf[0:n, :].unsqueeze(2).to_broadcast([n, TOPK, NE]), ALU.is_equal)
                wv("oh", dve, T)
                wv("rank", dve, T, back=1)
                E["sel"].done(dve.tensor_reduce(sel[0:n, :], oh[0:n, :, :].rearrange("p k e -> p e k"), AX, ALU.add))

            def b_gates(T):
                n = T.n
                wv("e4", dve, T)
                E["rs4"].done(dve.reciprocal(rs4[0:n, :], sum4[0:n, :]))
                wv("rs4", dve, T)
                E["gate"].done(dve.tensor_scalar(meta[T.par][0:n, :, 1].bitcast(F32), e4[0:n, :], rs4[0:n, 0:1],
                                                 None, ALU.mult))

            def b_slot(T):
                n = T.n
                wv("rank", dve, T)
                tt("ohr", ohr[0:n, :, :], B[6][0:n, 0:NE].unsqueeze(1).to_broadcast([n, TOPK, NE]), oh[0:n, :, :],
                   ALU.mult)
                wv("sel", dve, T)
                tt("selsum", selsum[0:n, :], selsum[0:n, :], sel[0:n, :], ALU.add)
                wv("ohr", dve, T)
                E["r4"].done(dve.tensor_reduce(r4[0:n, :], ohr[0:n, :, :], AX, ALU.add))
                wv("r4", dve, T)
                E["slotf"].done(dve.scalar_tensor_tensor(slotf[0:n, :], idf[0:n, :], float(REGION), r4[0:n, :],
                                                         ALU.mult, ALU.add))
                wv("slotf", dve, T)
                E["slot"].done(dve.tensor_copy(slot[T.par][0:n, :], slotf[0:n, :]))

            def front(T):
                f_ms(T)
                f_gate(T)
                f_qd(T)
                f_og(T)

            def back(T):
                m_Sp(T, 0)
                m_AT(T)
                m_S(T, 0)
                m_Sp(T, 1)
                m_S(T, 1)
                m_o(T)
                b_x1(T)
                b_h(T)
                b_top(T)
                b_gates(T)
                b_slot(T)

            dve.wait_ge(c_sem, 16 * N_CONST)
            for buf in (S, selsum, ATs, kdTz, qdz[0], qdz[1]):
                memo.done(dve.memset(buf[tuple([slice(None)] * len(buf.shape))], 0.0))
            dve.wait_ge(w_sem, 16 * 4)
            memo.done(dve.tensor_tensor(w_pool[:, :, :].rearrange("p g e -> p (g e)"),
                                        w_pool[:, :, :].rearrange("p g e -> p (g e)"), pscale[:, :], ALU.mult))
            memo.wait(dve, 0, 7)
            for t in range(2):
                front(Tile(0, t))
                back(Tile(0, t))
            with dve.Fori(1, PT // 2) as i:
                for t in range(2):
                    front(Tile(i, t))
                    back(Tile(i, t))
            T = Tile(PT // 2, 0, "s")
            front(T)
            wv("qdz", dve, T)
            wv("og", dve, T)
            memo.done(dve.memset(Q8, 0.0))
            memo.wait(dve, 0, 8)
            for b in range(NSEQ):
                s_misc.done(dve.tensor_copy(Q8[:, :, b, b * LSEQ:(b + 1) * LSEQ],
                                            qdz[0][:, :, b * LSEQ:(b + 1) * LSEQ]))
            wv("kdT", dve, T)
            wv("o", dve, T, back=1)
            s_misc.done(dve.memset(ATs[0:NS, :, 0:NS], 0.0))
            s_misc.wait(dve, 0, NSEQ + 1)
            for s in (slice(0, NS // 2), slice(NS // 2, NS)):
                E["ATs"].done(dve.copy_predicated(ATs[s, :, 0:NS],
                                                  causal_s[s, :].rearrange("p (a i) -> p a i", a=H),
                                                  B[4][s, 0:H * NS].rearrange("p (a i) -> p a i", a=H)))
            for b in range(NSEQ):
                s_T8.done(dve.tensor_scalar(kdT8[:, b, :], B[4][0:NS, 256:512], seq_of[:, b:b + 1], None, ALU.mult))
            wv("esm", dve, T, 1)
            wv("o", dve, T)
            for b in range(NSEQ):
                s_P8.wait(dve, 0, b + 1)
                for r in range(2):
                    s = slice(r * DK, (r + 1) * DK)
                    src = B[6][s, :].rearrange("p (a b v) -> p a b v", a=2, b=2)[:, :, r, :]
                    s_misc.done(dve.tensor_tensor(S0[s, b, :, :], src, S0[s, b, :, :], ALU.add))
                s_misc.wait(dve, 0, NSEQ + 3 + 2 * b)
                el = els[:, b::NSEQ].unsqueeze(2).to_broadcast([P, 2, DV])
                s_S8.done(dve.tensor_tensor(S0[:, b, :, :], S0[:, b, :, :], el, ALU.mult))
            m_o(T)
            b_x1(T)
            b_h(T)
            b_top(T)
            b_gates(T)
            b_slot(T)
            s_cnt.wait(dve, 0)
            step = [0]

            def chain(ins):
                step[0] += 1
                s_tab.done(ins)
                s_tab.wait(dve, 0, step[0])

            cnt, nch, end = ctab["cnt"], ctab["nch"], ctab["end"]
            dve.wait_ge(no_sem, 16)
            chain(dve.tensor_copy(cnt[0:1, :], B[6][0:1, 0:NE]))
            chain(dve.tensor_scalar(nch[0:1, :], cnt[0:1, :], 0.0, None, ALU.is_gt))
            for m in range(1, CPE):
                chain(dve.scalar_tensor_tensor(nch[0:1, :], cnt[0:1, :], float(m * CHUNK), nch[0:1, :],
                                               ALU.is_gt, ALU.add))
            chain(dve.tensor_tensor_scan(end[0:1, :], ones[0:1, 0:NE], nch[0:1, :], 0.0, ALU.mult, ALU.add))
            def bc(a):
                return a[0:1, :].unsqueeze(1).to_broadcast([1, NTAB, NE])
            cn = chunk_no.rearrange("o (i e) -> o i e", e=NE)
            chain(dve.tensor_tensor(ge, cn, bc(end), ALU.is_ge))
            chain(dve.tensor_tensor(geb, ge, bc(nch), ALU.mult))
            ex, bs = ctab["ex"], ctab["bs"]
            chain(dve.tensor_reduce(ex[0:1, :], ge, AX, ALU.add))
            chain(dve.tensor_reduce(bs[0:1, :], geb, AX, ALU.add))
            chain(dve.tensor_scalar(ex[0:1, :], ex[0:1, :], float(NE - 1), None, ALU.min))
            chain(dve.tensor_tensor(bs[0:1, :], cn[:, :, 0], bs[0:1, :], ALU.subtract))
            chain(dve.tensor_scalar(bs[0:1, :], bs[0:1, :], float(CPE - 1), float(CHUNK), ALU.min, ALU.mult))
            chain(dve.scalar_tensor_tensor(bs[0:1, :], ex[0:1, :], float(REGION), bs[0:1, :], ALU.mult, ALU.add))
            chain(dve.tensor_copy(tab[0:1, 0:NTAB], ex[0:1, :]))
            chain(dve.tensor_copy(tab[0:1, NTAB:2 * NTAB], bs[0:1, :]))
            chain(dve.tensor_copy(tab[0:1, 2 * NTAB:2 * NTAB + 1], end[0:1, NE - 1:NE]))

        @block.gpsimd
        def _(pool):
            def root(T, src, dst, e_in, e, m):
                wv(e_in, pool, T)
                E[e].done(pool.tensor_tensor(dst[0:T.n, :], src[0:T.n, :], neghalf[0:T.n, 0:m], ALU.pow))

            one = ones[:, 0:NG * BUF].rearrange("p (g r) -> p g r", g=NG)

            def f_pool(T):
                n = T.n
                if T.kind == "p":
                    cur = ux[T.par]
                    if T.static and T.t == 0:
                        E["hist"].done(pool.memset(cur[:, :, 0:BUF], 0.0))
                    else:
                        wv("uxe", pool, T, back=1)
                        last = ux[1 - T.par][:, :, P:P + BUF]
                        E["hist"].done(pool.tensor_tensor(cur[:, :, 0:BUF], last, one, ALU.mult))
                    wv("uxe", pool, T)
                    wv("hist", pool, T)
                    L, s = P, 1
                    src = cur[:, :, :].unsqueeze(2)
                else:
                    s_olde.wait(pool, 0)
                    s_misc2.wait(pool, 0)
                    L, s = LSEQ, NSEQ
                    src = uxs[:, :, :, :]
                W = BUF + L
                A = pa[:, :, 0:s * W].rearrange("p g (s w) -> p g s w", s=s)
                B_ = pb[:, :, 0:s * W].rearrange("p g (s w) -> p g s w", s=s)

                def grow(dst, a, g0, lo, step, k):
                    E["pool"].done(pool.tensor_tensor(dst[:, g0:, :, lo:W], a[:, g0:, :, lo:W],
                                                      a[:, g0:, :, lo - step:W - step], ALU.add))
                    wv("pool", pool, T, k)

                grow(A, src, 0, 1, 1, 1)
                grow(B_, A, 1, 3, 2, 2)
                grow(A, B_, 2, 7, 4, 3)
                grow(B_, A, 3, 15, 8, 4)
                wv("zp", pool, T, back=2)
                d4 = dT[T.par][:, :, 0:n].rearrange("p g (s l) -> p g s l", s=s)
                i4 = inv[:, :, 0:n].rearrange("p g (s l) -> p g s l", s=s)
                for q, a in enumerate((A, B_)):
                    E["mean"].done(pool.tensor_tensor(d4[:, q::2], a[:, q::2, :, BUF:], i4[:, q::2], ALU.mult))
                wv("mean", pool, T)
                E["dT"].done(pool.tensor_tensor(d4, d4, src[:, :, :, BUF:], ALU.subtract))
                rest = inv_rest[:, :].rearrange("p (g r) -> p g r", g=NG)
                E["pool"].done(pool.tensor_tensor(inv[:, :, 0:BUF], rest, one, ALU.mult))
                wv("pool", pool, T)

            def b_routed(T, back=0):
                wv("slot", pool, T, back=back)
                wv("gate", pool, T, back=back)
                wv("tokid", pool, T, back=back)

            def b_scatter(par, n):
                for k in range(TOPK):
                    pool.indirect_dma_start(
                        X["slots"][:, :], bass.IndirectOffsetOnAxis(slot[par][0:n, k:k + 1], 0),
                        meta[par][0:n, k, :], None).then_inc(slot_st[par], 16)

            def tile(T):
                root(T, ms1, rs1, "ms1", "rs1", 1)
                f_pool(T)
                b_routed(T, back=1)
                root(T, mso, rso, "mso", "rso", 4)
                if not (T.static and T.t == 0):
                    b_scatter(1 - T.par, P)
                root(T, ms2, rs2, "ms2", "rs2", 1)

            neg = ev("neghalf_set")
            neg.done(pool.memset(neghalf[:, :], -0.5))
            neg.wait(pool, 0)
            pool.wait_ge(c_sem, 16 * N_CONST)
            pool.wait_ge(init_sem, 48)
            for t in range(2):
                tile(Tile(0, t))
            with pool.Fori(1, PT // 2) as i:
                for t in range(2):
                    tile(Tile(i, t))
            T = Tile(PT // 2, 0, "s")
            tile(T)
            b_routed(T)
            b_scatter(0, NS)

N_CONST = 2 + 11 + 2 + 3 + 1

def experts(nc, I, X, tab):
    with ExitStack() as ctx:
        def sb(name, shape, dt=F32):
            return ctx.enter_context(nc.sbuf_tensor(name, shape, dt))

        def sem(name):
            return ctx.enter_context(nc.semaphore(name))

        def ev(name, per=1):
            return Event(ctx, nc, name, per)

        B = [ctx.enter_context(nc.psum_tensor(f"ebank{b}", [P, 512], F32)) for b in range(7)]
        raw = [sb(f"raw{b}", [P, PIECE]) for b in range(2)]
        wh = [sb(f"wh{b}", [P, PIECE], F32R) for b in range(2)]
        wl = [sb(f"wl{b}", [P, PIECE], F32R) for b in range(2)]
        xg = sb("xg", [P, 3, D])
        xh = sb("xh", [P, KD, CHUNK], F32R)
        xl = sb("xl", [P, KD, CHUNK], F32R)
        ah = sb("ah", [P, KD, CHUNK], F32R)
        al = sb("al", [P, KD, CHUNK], F32R)
        g_, u_, u2, gu_, sg_ = (sb(n, [P, CHUNK]) for n in ("gate", "up", "up1", "gateup", "sig"))
        a_ = [sb(f"act{b}", [P, CHUNK]) for b in range(2)]
        osb = sb("osb", [P, 3, D])
        bd = sb("b_down_rows", [P, D])
        ident = sb("eident", [P, P])
        bgu_rows = sb("bgu_rows", [NE, 2 * FF])
        bgu = sb("bgu", [P, 2 * KD, NE])
        bcur = sb("bcur", [P, 2 * KD])
        mnx = sb("slots_next", [P, 3, 2], I32)
        mcur = sb("slots_now", [P, 3, 2], I32)

        raw_in = [sem("raw_in0"), sem("raw_in1")]
        ld, meta_in, x_in, bd_in, sc = (sem(n) for n in ("loaded", "slots_in", "rows_in", "b_down_in", "rows_added"))
        bturn, bkept = ev("bias_turned"), ev("bias_kept")
        hi, lo = ev("w_hi", 6), ev("w_lo", 6)
        trx, xhe, xle = ev("x_turned", 8), ev("x_hi", 8), ev("x_lo", 8)
        gu, dn = ev("gate_up_done", 8), ev("down_done", 6)
        mc, bc = ev("slots_now_set", 2), ev("bias_now_set")
        g1, u1, u1b, gm, ac = (ev(n, 8) for n in ("gate_clamped", "up_clamped", "up_plus1", "gate_times_up", "act_done"))
        sgm, ahe, ale = ev("sigmoid_done", 8), ev("act_hi", 8), ev("act_lo", 8)
        ob, osc = ev("out_biased", 6), ev("out_scaled", 6)
        mc0, last = ev("first_slots_set"), ev("last_rows_scaled")
        carry = sb("carry", [1, 1])

        wgu = I["w_gate_up"][0].rearrange("e (k p) n -> e p k n", p=P)
        wdn = I["w_down"][0].rearrange("e (k p) n -> e p k n", p=P)

        def n_chunks(eng):
            return eng.value_load(tab[0:1, 2 * NTAB:2 * NTAB + 1], min_val=1, max_val=MAXC)

        def expert_of(eng, i):
            return eng.value_load(tab[0:1, bass.ds(i, 1)], min_val=0, max_val=NE - 1)

        block = ctx.enter_context(nc.Block())

        @block.sync
        def _(sp):
            def piece(e, i, p):
                sp.wait_ge(lo.sem, i * 6 + (p + 1))
                s = p % 2
                if p < 4:
                    v = raw[s][:, :].rearrange("p (g k c) -> p g k c", g=2, k=KD)
                    for g in range(2):
                        sp.dma_start(v[:, g], wgu[e, :, :, g * FF + p * 256:g * FF + (p + 1) * 256]).then_inc(raw_in[s], 16)
                else:
                    v = raw[s][:, :].rearrange("p (k c) -> p k c", k=KD)
                    for q in range(2):
                        sp.dma_start(v[:, 4 * q:4 * q + 4], wdn[e, :, 4 * q:4 * q + 4, (p - 4) * 512:(p - 3) * 512]).then_inc(raw_in[s], 16)

            sp.dma_start(ident[:, :], I["ident"]).then_inc(ld, 16)
            sp.dma_start(bgu_rows[:, :], I["b_gate_up"][0]).then_inc(ld, 16)
            n = n_chunks(sp)
            with sp.Fori(0, n) as i:
                e = expert_of(sp, i)
                for p in range(6):
                    piece(e, i, p)
                    if p == 2:
                        ob.wait(sp, i, 3)
                        sp.dma_start(bd[:, :], I["b_down"][0, bass.ds(e, 1), :].to_broadcast([P, D])).then_inc(bd_in, 16)
            e = expert_of(sp, n)
            for p in range(2):
                piece(e, n, p)

        @block.tensor
        def _(pe):
            def turn_x(i, k):
                for s0, m in SUBS:
                    ins = pe.transpose(B[k % 4][:, s0:s0 + m], xg[0:m, s0 // P, k * P:(k + 1) * P], ident[0:m, 0:m])
                trx.done(ins)

            def gate_up(i, j):
                p, jj = j // 2, j % 2
                if jj == 0:
                    pe.wait_ge(lo.sem, i * 6 + (p + 3))
                if j >= 2:
                    u1.wait(pe, i, j - 1)
                h_, l_ = (w[p % 2][:, :].rearrange("p (g k c) -> p g k c", g=2, k=KD) for w in (wh, wl))
                for g in range(2):
                    out = B[2 * jj + g][:, 0:CHUNK]
                    for k in range(KD):
                        c = slice(jj * P, (jj + 1) * P)
                        pe.matmul(out, h_[:, g, k, c], xh[:, k, :], start=(k == 0), stop=False)
                        pe.matmul(out, h_[:, g, k, c], xl[:, k, :], start=False, stop=False)
                        ins = pe.matmul(out, l_[:, g, k, c], xh[:, k, :], start=False, stop=(k == KD - 1))
                gu.done(ins)

            def down(i, half, s):
                s0, m = SUBS[s]
                if s == 0:
                    pe.wait_ge(lo.sem, i * 6 + (4 + half + 3))
                pe.wait_ge(ob.sem, i * 6 + (3 * half + s + 1))
                h_, l_ = (w[half][:, :].rearrange("p (k c) -> p k c", k=KD) for w in (wh, wl))
                out = B[4 + s][0:m, :]
                for k in range(KD):
                    pe.matmul(out, ah[:, k, s0:s0 + m], h_[:, k, :], start=(k == 0), stop=False)
                    pe.matmul(out, ah[:, k, s0:s0 + m], l_[:, k, :], start=False, stop=False)
                    ins = pe.matmul(out, al[:, k, s0:s0 + m], h_[:, k, :], start=False, stop=(k == KD - 1))
                dn.done(ins)

            pe.wait_ge(ld, 32)
            for q in range(2):
                for jj in range(8):
                    ins = pe.transpose(B[4 + q][:, jj * NE:(jj + 1) * NE],
                                       bgu_rows[:, (8 * q + jj) * P:(8 * q + jj + 1) * P], ident[0:NE, 0:NE])
                bturn.done(ins)
            pe.wait_ge(x_in, 48)
            for k in range(KD):
                if k >= 4:
                    xle.wait(pe, 0, k - 3)
                turn_x(0, k)
            bkept.wait(pe, 0, 2)
            n = n_chunks(pe)
            with pe.Fori(0, n) as i:
                xle.wait(pe, i)
                for j in range(8):
                    gate_up(i, j)
                ale.wait(pe, i)
                for s in range(3):
                    down(i, 0, s)
                u1.wait(pe, i)
                pe.wait_ge(x_in, i * 48 + 96)
                for k in range(4):
                    turn_x(i + 1, k)
                down(i, 1, 0)
                for k in range(4, 8):
                    xle.wait(pe, i + 1, k - 3)
                    turn_x(i + 1, k)
                down(i, 1, 1)
                down(i, 1, 2)

        @block.scalar
        def _(act):
            def w_hi(i, p):
                if p >= 2:
                    if p - 2 < 4:
                        gu.wait(act, i, 2 * (p - 2) + 2)
                act.wait_ge(raw_in[p % 2], i * 96 + 32 * (p // 2 + 1))
                hi.done(act.activation(wh[p % 2][:, :], raw[p % 2][:, :], ACT.Copy))

            def x_hi(i, k):
                trx.wait(act, i, k + 1)
                xhe.done(act.activation(xh[:, k, :], B[k % 4][:, 0:CHUNK], ACT.Copy))

            def swiglu(i, j):
                g1.wait(act, i, j + 1)
                if j == 0:
                    ob.wait(act, i, 3)
                else:
                    ac.wait(act, i, j)
                sgm.done(act.activation(sg_[:, :], g_[:, :], ACT.Sigmoid, scale=ALPHA))
                ac.wait(act, i, j + 1)
                ahe.done(act.activation(ah[:, j, :], a_[j % 2][:, :], ACT.Copy))

            def scale(i, half, s):
                s0, m = SUBS[s]
                ob.wait(act, i, 3 * half + s + 4)
                v = osb[0:m, s, half * 512:(half + 1) * 512]
                osc.done(act.activation(v, v, ACT.Copy, scale=mcur[0:m, s, 1:2].bitcast(F32)))

            w_hi(0, 0)
            w_hi(0, 1)
            for k in range(KD):
                x_hi(0, k)
            mc0.wait(act, 0, 4)
            osc.done(act.activation(carry[:, :], carry[:, :], ACT.Copy))
            osc.wait(act, 0, 1)
            n = n_chunks(act)
            with act.Fori(0, n) as i:
                for p in range(4):
                    swiglu(i, 2 * p)
                    swiglu(i, 2 * p + 1)
                    w_hi(i, p + 2)
                for s in range(3):
                    scale(i, 0, s)
                dn.wait(act, i, 3)
                w_hi(i + 1, 0)
                for k in range(4):
                    x_hi(i + 1, k)
                scale(i, 1, 0)
                for k in range(4, 8):
                    x_hi(i + 1, k)
                scale(i, 1, 1)
                scale(i, 1, 2)
                dn.wait(act, i, 6)
                w_hi(i + 1, 1)

        @block.vector
        def _(dve):
            def w_lo(i, p):
                hi.wait(dve, i, p + 1)
                lo.done(dve.tensor_tensor(wl[p % 2][:, :], raw[p % 2][:, :], wh[p % 2][:, :].bitcast(F32), ALU.subtract))

            def x_lo(i, k):
                xhe.wait(dve, i, k + 1)
                xle.done(dve.tensor_tensor(xl[:, k, :], B[k % 4][:, 0:CHUNK], xh[:, k, :].bitcast(F32), ALU.subtract))

            def clamp(i, j):
                G, U = B[2 * (j % 2)][:, 0:CHUNK], B[2 * (j % 2) + 1][:, 0:CHUNK]
                gu.wait(dve, i, j + 1)
                g1.done(dve.tensor_scalar(g_[:, :], G, bcur[:, j:j + 1], LIMIT, ALU.add, ALU.min))
                u1.done(dve.tensor_scalar(u_[:, :], U, bcur[:, KD + j:KD + j + 1], LIMIT, ALU.add, ALU.min))
                u1.wait(dve, i, j + 1)
                u1b.done(dve.tensor_scalar(u2[:, :], u_[:, :], -LIMIT, 1.0, ALU.max, ALU.add))
                g1.wait(dve, i, j + 1)
                u1b.wait(dve, i, j + 1)
                gm.done(dve.tensor_tensor(gu_[:, :], g_[:, :], u2[:, :], ALU.mult))
                gm.wait(dve, i, j + 1)
                sgm.wait(dve, i, j + 1)
                if j >= 2:
                    ale.wait(dve, i, j - 1)
                ac.done(dve.tensor_tensor(a_[j % 2][:, :], gu_[:, :], sg_[:, :], ALU.mult))

            def out_bias(i, half, s):
                s0, m = SUBS[s]
                c = slice(half * 512, (half + 1) * 512)
                dn.wait(dve, i, 3 * half + s + 1)
                if half == 0 and s == 0:
                    dve.wait_ge(bd_in, i * 16 + 16)
                    dve.wait_ge(sc, i * 48 + 48)
                ob.done(dve.tensor_tensor(osb[0:m, s, c], B[4 + s][0:m, :], bd[0:m, c], ALU.add))

            def take_slots(i):
                dve.wait_ge(meta_in, i * 48 + 48)
                dve.wait_ge(x_in, i * 48 + 48)
                dve.wait_ge(sc, i * 48 + 48)
                mc.done(dve.tensor_copy(mcur[:, 0:2, :], mnx[:, 0:2, :]))
                mc.done(dve.tensor_copy(mcur[0:64, 2, :], mnx[0:64, 2, :]))

            for q in range(2):
                lo.done(dve.memset(u2[:, q:q + 1], 0.0))
            for q in range(2, 5):
                ob.done(dve.memset(u2[:, q:q + 1], 0.0))
            lo.wait(dve, 0, 2)
            for q in range(2):
                bturn.wait(dve, 0, q + 1)
                bkept.done(dve.tensor_copy(bgu[:, 8 * q:8 * q + 8, :],
                                           B[4 + q][:, 0:8 * NE].rearrange("p (j e) -> p j e", j=8)))
            bkept.wait(dve, 0, 2)
            ob.wait(dve, 0, 3)
            w_lo(0, 0)
            w_lo(0, 1)
            for k in range(KD):
                x_lo(0, k)
            dve.wait_ge(meta_in, 48)
            mc0.done(dve.memset(osb[:, :, :], 0.0))
            mc0.done(dve.memset(carry[:, :], 0.0))
            mc0.done(dve.tensor_copy(mcur[:, 0:2, :], mnx[:, 0:2, :]))
            mc0.done(dve.tensor_copy(mcur[0:64, 2, :], mnx[0:64, 2, :]))
            mc0.wait(dve, 0, 4)
            n = n_chunks(dve)
            with dve.Fori(0, n) as i:
                e = expert_of(dve, i)
                bc.done(dve.tensor_copy(bcur[:, :], bgu[:, :, bass.ds(e, 1)].rearrange("p j o -> p (j o)")))
                bc.wait(dve, i)
                for p in range(4):
                    clamp(i, 2 * p)
                    clamp(i, 2 * p + 1)
                    if p == 1:
                        take_slots(i)
                    w_lo(i, p + 2)
                for s in range(3):
                    out_bias(i, 0, s)
                w_lo(i + 1, 0)
                for k in range(4):
                    x_lo(i + 1, k)
                out_bias(i, 1, 0)
                for k in range(4, 8):
                    x_lo(i + 1, k)
                out_bias(i, 1, 1)
                out_bias(i, 1, 2)
                w_lo(i + 1, 1)

        @block.gpsimd
        def _(pool):
            def load_slots(i):
                r = pool.value_load(tab[0:1, bass.ds(i + NTAB, 1)], min_val=0, max_val=SLOTS - CHUNK)
                for s, (s0, m) in enumerate(SUBS):
                    pool.dma_start(mnx[0:m, s, :], X["slots"][bass.ds(r + s0, m), :]).then_inc(meta_in, 16)

            def gather():
                for s, (s0, m) in enumerate(SUBS):
                    pool.indirect_dma_start(
                        xg[0:m, s, :], None, X["h"][:, :],
                        bass.IndirectOffsetOnAxis(mnx[0:m, s, 0:1].bitcast(U32), 0)).then_inc(x_in, 16)

            def act_lo(i, j):
                ahe.wait(pool, i, j + 1)
                ale.done(pool.tensor_tensor(al[:, j, :], a_[j % 2][:, :], ah[:, j, :].bitcast(F32), ALU.subtract))

            def add_rows():
                for s, (s0, m) in enumerate(SUBS):
                    pool.indirect_dma_start(
                        X["y"][:, :], bass.IndirectOffsetOnAxis(mcur[0:m, s, 0:1].bitcast(U32), 0),
                        osb[0:m, s, :], None, compute_op=ALU.add).then_inc(sc, 16)

            load_slots(0)
            pool.wait_ge(meta_in, 48)
            gather()
            mc0.wait(pool, 0, 4)
            n = n_chunks(pool)
            with pool.Fori(0, n) as i:
                osc.wait(pool, i, 1)
                act_lo(i, 0)
                add_rows()
                act_lo(i, 1)
                act_lo(i, 2)
                act_lo(i, 3)
                mc.wait(pool, i)
                act_lo(i, 4)
                load_slots(i + 1)
                act_lo(i, 5)
                pool.wait_ge(meta_in, i * 48 + 96)
                trx.wait(pool, i)
                act_lo(i, 6)
                gather()
                act_lo(i, 7)
            osc.wait(pool, n, 1)
            mc.wait(pool, n - 1)
            last.done(pool.tensor_tensor(carry[:, :], carry[:, :], carry[:, :], ALU.add))
            add_rows()
            pool.wait_ge(sc, n * 48 + 48)
            pool.wait_ge(x_in, n * 48 + 48)

def final(nc, I, O, X):
    with ExitStack() as ctx:
        def sb(name, shape, dt=F32):
            return ctx.enter_context(nc.sbuf_tensor(name, shape, dt))

        def ev(name, per=1):
            return Event(ctx, nc, name, per)

        nf = sb("final_rows", [P, D])
        neghalf = sb("fneghalf", [P, 1])
        y = [sb(f"y{b}", [P, D]) for b in range(2)]
        yo = [sb(f"yo{b}", [P, D]) for b in range(2)]
        junk = sb("fjunk", [P, D])
        ss, ms, rs = ([sb(f"f{n}{b}", [P, 1]) for b in range(2)] for n in ("ss", "ms", "rs"))
        y_in = [ctx.enter_context(nc.semaphore(f"y_in{b}")) for b in range(2)]
        out_st = [ctx.enter_context(nc.semaphore(f"out_stored{b}")) for b in range(2)]
        nf_in = ctx.enter_context(nc.semaphore("final_norm_in"))
        ess, ems, ers, eo = (ev(n) for n in ("f_ss", "f_ms", "f_rs", "f_out"))
        neg = ev("f_neghalf_set")
        block = ctx.enter_context(nc.Block())
        ST = Tile(PT // 2, 0, "s")

        def every(eng, f):
            for t in range(2):
                f(Tile(0, t))
            with eng.Fori(1, PT // 2) as i:
                for t in range(2):
                    f(Tile(i, t))
            f(ST)

        @block.sync
        def _(sp):
            sp.dma_start(nf[:, :], I["final_norm"].partition_broadcast(P)).then_inc(nf_in, 16)

            def load(T):
                eo.wait(sp, T.t - 2)
                src = X["y"][SEQ:TOK, :] if T.kind == "s" else X["y"][bass.ds(T.t * P, P), :]
                sp.dma_start(y[T.par][0:T.n, :], src).then_inc(y_in[T.par], 16)
            every(sp, load)

        @block.scalar
        def _(act):
            def square(T):
                act.wait_ge(y_in[T.par], T.pair * 16 + 16)
                ems.wait(act, T.t - 2)
                ess.wait(act, T.t - 1)
                ess.done(act.activation(junk[0:T.n, :], y[T.par][0:T.n, :], ACT.Square, accum_out=ss[T.par][0:T.n, :]))
                eo.wait(act, T.t - 1)
                if not (T.static and T.t == 0):
                    store(T.t - 1, 1 - T.par, P)

            def store(t, par, n):
                if n == P:
                    dst = O["y_p"][0][bass.ds(t * P, P), :]
                else:
                    dst = O["y_s"].rearrange("b l d -> (b l) d")
                act.dma_start(dst, yo[par][0:n, :]).then_inc(out_st[par], 16)
            every(act, square)
            eo.wait(act, PT)
            store(PT, 0, NS)
            act.wait_ge(out_st[0], 16 * (PT // 2 + 1))
            act.wait_ge(out_st[1], 16 * (PT // 2))

        @block.gpsimd
        def _(pool):
            neg.done(pool.memset(neghalf[:, :], -0.5))
            neg.wait(pool, 0)

            def root(T):
                ems.wait(pool, T.t)
                eo.wait(pool, T.t - 2)
                ers.done(pool.tensor_tensor(rs[T.par][0:T.n, :], ms[T.par][0:T.n, :], neghalf[0:T.n, :], ALU.pow))
            every(pool, root)

        @block.vector
        def _(dve):
            dve.wait_ge(nf_in, 16)

            def norm(T):
                ess.wait(dve, T.t)
                ers.wait(dve, T.t - 2)
                ems.done(dve.tensor_scalar(ms[T.par][0:T.n, :], ss[T.par][0:T.n, :], 1.0 / D, EPS, ALU.mult, ALU.add))
                ers.wait(dve, T.t)
                dve.wait_ge(y_in[T.par], T.pair * 16 + 16)
                if not (T.static and T.pair == 0):
                    dve.wait_ge(out_st[T.par], T.pair * 16)
                eo.done(dve.scalar_tensor_tensor(yo[T.par][0:T.n, :], y[T.par][0:T.n, :], rs[T.par][0:T.n, 0:1],
                                                 nf[0:T.n, :], ALU.mult, ALU.mult))
            every(dve, norm)

def build(nc, I, O):
    X = {
        "slots": nc.dram_tensor("slot_rows", [SLOTS, 2], I32).ap(),
        "h": nc.dram_tensor("h_rows", [ROWS, D], F32).ap(),
        "y": nc.dram_tensor("y_rows", [ROWS, D], F32).ap(),
    }
    with nc.sbuf_tensor("chunk_table", [1, 2 * NTAB + 1], I32) as tab:
        with ExitStack() as ctx:
            ctab = {n: ctx.enter_context(nc.sbuf_tensor("t_" + n, [1, *s], F32)) for n, s in dict(
                cnt=[NE], nch=[NE], end=[NE], ex=[NTAB], bs=[NTAB]).items()}
            mixer(nc, I, O, X, tab, ctab, None)
        experts(nc, I, X, tab)
    final(nc, I, O, X)

_INS = ["x_prompt", "x_sample", "state_gla", "state_pool", "norm1", "w_in", "w_gk2", "b_gk", "gla_norm", "w_pool",
        "pool_scale", "w_o", "norm2", "w_router", "b_router", "w_gate_up", "b_gate_up", "w_down", "b_down",
        "final_norm"]
_OUTS = {"y_p": (1, SEQ, D), "y_s": (NSEQ, LSEQ, D), "gla_p": (1, 1, H, DK, DV), "pool_p": (1, 1, BUF, PW),
         "gla_s": (1, NSEQ, H, DK, DV), "pool_s": (1, NSEQ, BUF, PW)}

def kernel(**inputs):
    import concourse.bacc as _bacc
    from concourse.bass_utils import run_bass_kernel_spmd as _run

    nc = _bacc.Bacc("TRN2", target_bir_lowering=False, num_devices=1)
    arrays = {f"in_{n}": np.ascontiguousarray(inputs[n]) for n in _INS}
    arrays.update({f"in_{n}": a for n, a in constants().items()})
    I = {n[3:]: nc.dram_tensor(n, a.shape, mybir.dt.from_np(a.dtype), kind="ExternalInput").ap()
         for n, a in arrays.items()}
    O = {n: nc.dram_tensor(f"out_{n}", s, F32, kind="ExternalOutput").ap() for n, s in _OUTS.items()}
    build(nc, I, O)
    r = _run(nc, [arrays], core_ids=[0])
    return tuple(r.results[0][f"out_{n}"] for n in _OUTS)
```

```python
from contextlib import ExitStack

import numpy as np

import concourse.bass as bass
from concourse import mybir

F32 = mybir.dt.float32
F32R = mybir.dt.float32r
I32 = mybir.dt.int32
U32 = mybir.dt.uint32
ALU = mybir.AluOpType
ACT = mybir.ActivationFunctionType
AX = mybir.AxisListType.X

P = 128
D = 1024
KD = D // P
SEQ = 2048
NSEQ, LSEQ = 8, 8
NS = NSEQ * LSEQ
PT = SEQ // P
NT = PT + 1
TOK = SEQ + NS
H, DK, DV = 4, 64, 128
QK = H * DK
VW = H * DV
RANK = 16
GATE_DIV = 16.0
C = 64
NC = P // C
PW = 512
NG = 4
BUF = 15
O_Q, O_K, O_V, O_OG, O_GLR, O_U = 0, QK, 2 * QK, 2 * QK + VW, 2 * QK + 2 * VW, 2 * QK + 2 * VW + RANK
IN_COLS = O_U + PW
NE = 32
TOPK = 4
FF = D
EPS = 1e-5
LIMIT = 7.0
ALPHA = 1.702
CHUNK = 320
SUBS = [(0, 128), (128, 128), (256, 64)]
WIDTHS = [256, 272, 288, 304, CHUNK]
CPE = -(-TOK // CHUNK)
REGION = CPE * CHUNK
SLOTS = NE * REGION
MAXC = TOK * TOPK // CHUNK + NE
NTAB = 64
SIZES = 2 * NTAB + 4
ROWS = TOK + CHUNK
PIECE = 4096
assert MAXC + 1 <= NTAB

def constants():
    p = np.arange(P)
    c = {}
    c["ident"] = np.eye(P, dtype=np.float32)
    c["before"] = (p[:, None] < p[None, :]).astype(np.float32)
    c["ones"] = np.ones((P, P), np.float32)
    c["scan_p"] = np.tile((np.arange(P) % C != 0).astype(np.float32), (P, 2))
    c["scan_s"] = np.tile((np.arange(NS) % LSEQ != 0).astype(np.float32), (P, 2))
    c["causal_p"] = np.tile((np.arange(C)[None, :] >= (p % C)[:, None]).astype(np.int32), (1, H))
    j, i = np.arange(NS)[:, None], np.arange(NS)[None, :]
    c["causal_s"] = np.tile(((i >= j) & (i // LSEQ == j // LSEQ)).astype(np.int32), (1, H))
    c["seq_of"] = (np.arange(NS)[:, None] // LSEQ == np.arange(NSEQ)[None, :]).astype(np.float32)
    c["expert_no"] = np.tile(np.arange(NE, dtype=np.float32), (P, TOPK))
    c["token_no"] = (p[:, None] + P * np.arange(NT)[None, :]).astype(np.int32)
    w = np.array([2, 4, 8, 16])
    first = 1.0 / np.minimum(w[:, None], np.arange(P)[None, :] + 1)
    c["inv_first"] = np.tile(first.astype(np.float32).reshape(1, -1), (P, 1))
    c["inv_rest"] = np.tile(np.repeat(1.0 / w, BUF).astype(np.float32)[None, :], (P, 1))
    slot = np.arange(SLOTS)
    c["empty_slots"] = np.stack([TOK + slot % CHUNK, 0 * slot], 1).astype(np.int32)
    c["chunk_no"] = np.repeat(np.arange(NTAB, dtype=np.float32), NE)[None, :]
    c["zero_rows"] = np.zeros((CHUNK, D), np.float32)
    return c

class Event:

    def __init__(self, ctx, nc, name, per=1):
        self.sem = ctx.enter_context(nc.semaphore(name))
        self.per = per

    def done(self, ins):
        ins.then_inc(self.sem, 1)

    def wait(self, eng, t, k=None):
        if isinstance(t, int) and t < 0:
            return
        eng.wait_ge(self.sem, t * self.per + (self.per if k is None else k))

class Tile:

    def __init__(self, pair, par, kind="p"):
        self.t = pair * 2 + par
        self.pair, self.par, self.kind = pair, par, kind
        self.n = P if kind == "p" else NS
        self.static = isinstance(self.t, int)

    def later(self, k):
        par = (self.par + k) % 2
        pair = self.pair + (self.par + k - par) // 2
        if self.static and not 0 <= pair * 2 + par < NT:
            return None
        return Tile(pair, par, "s" if self.static and pair * 2 + par == PT else "p")


def in_order(eng, steps):
    for t in range(2):
        steps(Tile(0, t))
    with eng.Fori(1, PT // 2 - 1) as i:
        for t in range(2):
            steps(Tile(i, t))
    for t in range(2):
        steps(Tile(PT // 2 - 1, t))

def mixer(nc, I, O, X, tab, ctab, eps_rows):
    with ExitStack() as ctx:
        def sb(name, shape, dt=F32):
            return ctx.enter_context(nc.sbuf_tensor(name, shape, dt))

        def sem(name):
            return ctx.enter_context(nc.semaphore(name))

        def ev(name, per=1):
            return Event(ctx, nc, name, per)

        bank = [ctx.enter_context(nc.psum_tensor(f"bank{b}", [P, 512], F32)) for b in range(8)]
        w_in = sb("w_in_sb", [P, KD, IN_COLS])
        w_o = sb("w_o_sb", [P, KD, D])
        w_r = sb("w_r_sb", [P, KD, NE])
        w_gk = sb("w_gk_sb", [RANK, QK])
        w_pool = sb("w_pool_sb", [P, NG, P])
        b_gk = sb("b_gk_sb", [P, 2])
        glan = sb("glan_sb", [P, 1])
        n1 = sb("norm1_rows", [P, D])
        n2 = sb("norm2_rows", [P, D])
        b_r = sb("b_r_rows", [P, NE])
        ident = sb("ident", [P, P])
        before = sb("before", [P, P])
        ones = sb("ones", [P, P])
        scan_p = sb("scan_p", [P, 2 * P])
        scan_s = sb("scan_s", [P, 2 * NS])
        causal_p = sb("causal_p", [P, H * C], I32)
        causal_s = sb("causal_s", [NS, H * NS], I32)
        seq_of = sb("seq_of", [NS, NSEQ])
        expert_no = sb("expert_no", [P, TOPK * NE])
        token_no = sb("token_no", [P, NT], I32)
        inv = sb("inv_count", [P, NG, P])
        inv_rest = sb("inv_rest", [P, NG * BUF])
        ss1, ms1, rs1 = sb("ss1", [P, 1]), sb("ms1", [P, 1]), sb("rs1", [P, 1])
        ss2, ms2, rs2 = sb("ss2", [P, 1]), sb("ms2", [P, 1]), sb("rs2", [P, 1])
        neghalf = sb("neghalf", [P, 4])
        x = [sb(f"x{b}", [P, D]) for b in range(2)]
        xr = sb("x_residual", [P, D])
        xT = sb("xT", [P, KD, P])
        qks = sb("qks", [P, 4, P])
        ux = [sb(f"ux{b}", [P, NG, BUF + P]) for b in range(2)]
        uxs = sb("uxs", [P, NG, NSEQ, BUF + LSEQ])
        uc = sb("uc", [P, NG, NS])
        glrs = sb("glrs", [RANK, P])
        zz, az, G, Dm = (sb(n, [P, 2 * P]) for n in ("zz", "az", "G", "Dm"))
        e1 = l1 = az
        gk = zz
        eq, ek = sb("eq", [P, 2 * P]), sb("ek", [P, 2 * P])
        lr = sb("lr", [P, 4])
        esm = [sb(f"esm{b}", [P, 3, 4]) for b in range(2)]
        els = sb("els", [P, 2 * NSEQ])
        qdz = [sb(f"qdz{b}", [P, H, P]) for b in range(2)]
        kd = [sb(f"kd{b}", [P, 2, P]) for b in range(2)]
        vs = [sb(f"vs{b}", [P, VW]) for b in range(2)]
        eog = sb("eog", [P, VW])
        dog = eog
        sg = [sb(f"sg{b}", [P, VW]) for b in range(2)]
        pscale = sg[0]
        pa, pb = sb("pa", [P, NG, 8 * 23]), sb("pb", [P, NG, 8 * 23])
        dT = [sb(f"dT{b}", [P, NG, P]) for b in range(2)]
        ATs = sb("ATs", [P, H, P])
        kdTz = sb("kdTz", [P, NC, 2 * P])
        S, Sm, Pt = sb("S", [P, 2, DV]), sb("Sm", [P, 2, DV]), sb("Pt", [P, 2, DV])
        Sp = [sb(f"Sp{b}", [P, 2, DV]) for b in range(2)]
        os_, osq = sb("os", [P, VW]), sb("osq", [P, VW])
        so, mso, rso = sb("so", [P, H]), sb("mso", [P, H]), sb("rso", [P, H])
        cat = sb("cat", [P, KD, P])
        h = sb("h", [P, D])
        hT = sb("hT", [P, KD, P])
        lg = sb("lg", [P, NE])
        top = sb("top", [P, 8])
        idx = sb("idx", [P, 8], U32)
        idf = sb("idf", [P, TOPK])
        ng = sb("ng", [P, 1])
        e4, sum4, rs4 = sb("e4", [P, TOPK]), sb("sum4", [P, 1]), sb("rs4", [P, 1])
        oh, ohr = sb("oh", [P, TOPK, NE]), sb("ohr", [P, TOPK, NE])
        sel, selsum = sb("sel", [P, NE]), sb("selsum", [P, NE])
        r4, slotf = sb("r4", [P, TOPK]), sb("slotf", [P, TOPK])
        slot = [sb(f"slot{b}", [P, TOPK], U32) for b in range(2)]
        meta = [sb(f"meta{b}", [P, TOPK, 2], I32) for b in range(2)]
        Q8 = w_in[:, 0, 0:2048].rearrange("p (a b n) -> p a b n", a=H, b=NSEQ)
        kdT8 = w_in[0:NS, 1, 0:2048].rearrange("p (b n) -> p b n", b=NSEQ)
        ge = w_in[0:1, 2, 0:2048].rearrange("p (i e) -> p i e", e=NE)
        geb = w_in[0:1, 3, 0:2048].rearrange("p (i e) -> p i e", e=NE)
        chunk_no = w_in[0:1, 4, 0:2048]
        S0 = w_in[:, 5, 0:2048].rearrange("p (b a v) -> p b a v", b=NSEQ, a=2)
        pool_old = sb("pool_old", [NSEQ * BUF, PW])
        last_rows = sg[1][0:BUF, :]
        os_new = vs[1][0:NS, :]

        w_sem, wo_sem, c_sem = sem("w_loaded"), sem("wo_loaded"), sem("consts_loaded")
        init_sem = sem("dram_init")
        x_in = [sem("x_in0"), sem("x_in1")]
        xr_in = sem("x_residual_in")
        y_st, h_st = [sem("y_stored0")], [sem("h_stored0")]
        slot_st = [sem("slots_scattered0"), sem("slots_scattered1")]
        old_st = sem("states_stored")
        s0_in = sem("sampled_states_loaded")
        no_sem = sem("chunk_numbers_loaded")
        memo = ev("cleared")
        E = {n: ev(n, per) for n, per in dict(
            ss1=1, ms1=1, rs1=1, xn=1, trA=1, trB=1, xTe=2, glr=1, qk=1, u=1, z=1, v=1, og=1,
            qks=1, uxe=1, glrs=1, vse=1, eog=1, e1=1, l1=1, zz=2, az=1, gk=1, G=1, Dm=1, lr=1,
            eqk=2, esm=3, dog=1, rog=1, sg=1, qdz=2, kd=1, hist=1, pool=5, mean=2, dT=1,
            AT=1, kdT=1, ATs=2, kdTz=2, Sp=2, Pc=2, Pt=4, Sm=2, S=2, zp=1, zpe=1, o=1, os=1, osq=1,
            so=1, mso=1, rso=1, on1=1, on=1, oT=1, oTe=1, mix=2, x1=2, ss2=1, ms2=1, rs2=1, h=1,
            hA=1, hB=1, hTe=2, lgp=1, lg=1, top=1, idx=1, idf=1, ng=1, e4=1, rs4=1, gate=1, oh=1,
            sel=1, rank=1, ohr=1, r4=1, slotf=1, slot=1, tokid=1, selsum=1).items()}
        s_misc = ev("sample_steps")
        s_misc2 = ev("sample_inputs_kept")
        s_S8, s_P8, s_T8 = ev("s_S8"), ev("s_P8"), ev("s_T8")
        s_tab = ev("table_steps")
        s_cnt = ev("counted")
        s_old, s_olde, s_newt, s_newe, s_pnt, s_pne = (ev(n) for n in (
            "old_rows_turned", "old_rows_kept", "new_rows_turned", "new_rows_kept",
            "prompt_rows_turned", "prompt_rows_kept"))
        N_W, N_C = 8, 16

        block = ctx.enter_context(nc.Block())
        xp, xs = I["x_prompt"][0], I["x_sample"].rearrange("b l d -> (b l) d")

        def rows_of(ap, T):
            return ap[SEQ:TOK, :] if T.kind == "s" else ap[bass.ds(T.t * P, P), :]

        def wv(E_, eng, T, k=None, back=0):
            E[E_].wait(eng, T.t - back, k)

        def waitx(eng, T):
            eng.wait_ge(x_in[T.par], T.pair * 16 + 16)

        @block.sync
        def _(sp):
            def c_load(dst, src):
                sp.dma_start(dst, src).then_inc(c_sem, 16)

            def load_x(T):
                wv("trB", sp, T, back=2)
                src = xs if T.kind == "s" else xp[bass.ds(T.t * P, P), :]
                sp.dma_start(x[T.par][0:T.n, :], src).then_inc(x_in[T.par], 16)

            def load_residual(T):
                src = xs if T.kind == "s" else xp[bass.ds(T.t * P, P), :]
                sp.dma_start(xr[0:T.n, :], src).then_inc(xr_in, 16)

            def store(T):
                wv("x1", sp, T)
                sp.dma_start(rows_of(X["y"], T), xr[0:T.n, :]).then_inc(y_st[0], 16)
                wv("h", sp, T)
                sp.dma_start(rows_of(X["h"], T), h[0:T.n, :]).then_inc(h_st[0], 16)

            def tile(T):
                if T.later(2):
                    load_x(T.later(2))
                store(T)
                sp.wait_ge(y_st[0], T.t * 16 + 16)
                load_residual(T.later(1))

            load_x(Tile(0, 0))
            c_load(n1[:, :], I["norm1"].partition_broadcast(P))
            c_load(ident[:, :], I["ident"])
            win = I["w_in"][0].rearrange("(k p) n -> p k n", p=P)
            for k0 in range(0, KD, 4):
                sp.dma_start(w_in[:, k0:k0 + 4, :], win[:, k0:k0 + 4, :]).then_inc(w_sem, 16)
            sp.dma_start(w_gk[:, :], I["w_gk2"][0]).then_inc(w_sem, 16)
            load_x(Tile(0, 1))
            load_residual(Tile(0, 0))
            for dst, src in ((b_gk, I["b_gk"][0].rearrange("(a p) -> p a", p=P)),
                             (glan, I["gla_norm"].rearrange("a p -> p a")),
                             (n2, I["norm2"].partition_broadcast(P)),
                             (b_r, I["b_router"].partition_broadcast(P)),
                             (before, I["before"]), (ones, I["ones"]), (scan_p, I["scan_p"]),
                             (causal_p, I["causal_p"]), (expert_no, I["expert_no"]),
                             (token_no, I["token_no"]), (inv_rest, I["inv_rest"])):
                with nc.allow_non_contiguous_dma(reason="a few hundred bias elements"):
                    c_load(dst[:, :], src)
            c_load(inv[:, :, :].rearrange("p g t -> p (g t)"), I["inv_first"])
            c_load(pscale[:, :], I["pool_scale"].partition_broadcast(P))
            sp.dma_start(w_pool[:, :, :], I["w_pool"][0].rearrange("g c e -> c g e")).then_inc(w_sem, 16)
            wo = I["w_o"][0].rearrange("(k p) n -> p k n", p=P)
            for k0 in range(0, KD, 4):
                sp.dma_start(w_o[:, k0:k0 + 4, :], wo[:, k0:k0 + 4, :]).then_inc(wo_sem, 16)
            sp.dma_start(w_r[:, :, :], I["w_router"][0].rearrange("(k p) n -> p k n", p=P)).then_inc(wo_sem, 16)
            sp.dma_start(X["slots"][:, :], I["empty_slots"]).then_inc(init_sem, 16)
            sp.dma_start(X["h"][TOK:ROWS, :], I["zero_rows"]).then_inc(init_sem, 16)
            sp.dma_start(X["y"][TOK:ROWS, :], I["zero_rows"]).then_inc(init_sem, 16)
            for dst, src in ((scan_s, I["scan_s"]), (causal_s, I["causal_s"]), (seq_of, I["seq_of"])):
                c_load(dst[:, :], src)
            c_load(pool_old[:, :], I["state_pool"][0].rearrange("b r c -> (b r) c"))
            sp.dma_start(O["pool_s"][0, :, 0:BUF - LSEQ, :],
                         I["state_pool"][0, :, LSEQ:BUF, :]).then_inc(old_st, 16)
            in_order(sp, tile)
            E["S"].wait(sp, PT - 1)
            for c in range(2):
                sp.dma_start(O["gla_p"][0, 0].rearrange("(a c) k v -> c k a v", c=2)[c],
                             S[c * DK:(c + 1) * DK, :, :]).then_inc(old_st, 16)
            s_pne.wait(sp, 0)
            sp.dma_start(O["pool_p"][0, 0], last_rows).then_inc(old_st, 16)
            E["og"].wait(sp, PT)
            sg_in = I["state_gla"][0].rearrange("b (a c) k v -> c k b a v", c=2)
            for c in range(2):
                for a in range(2):
                    sp.dma_start(S0[c * DK:(c + 1) * DK, :, a, :], sg_in[c, :, :, a, :]).then_inc(s0_in, 16)
            sp.dma_start(chunk_no, I["chunk_no"]).then_inc(no_sem, 16)
            store(Tile(PT // 2, 0, "s"))
            s_newe.wait(sp, 0)
            for b in range(NSEQ):
                sp.dma_start(O["pool_s"][0, b, BUF - LSEQ:BUF, :],
                             os_new[b * LSEQ:(b + 1) * LSEQ, :]).then_inc(old_st, 16)
            s_S8.wait(sp, 0, NSEQ)
            sg_out = O["gla_s"][0].rearrange("b (a c) k v -> c k b a v", c=2)
            for c in range(2):
                for a in range(2):
                    sp.dma_start(sg_out[c, :, :, a, :], S0[c * DK:(c + 1) * DK, :, a, :]).then_inc(old_st, 16)
            sp.wait_ge(old_st, 16 * (1 + 2 + 1 + NSEQ + 4))
            sp.wait_ge(y_st[0], 16 * NT)
            sp.wait_ge(h_st[0], 16 * NT)
            sp.wait_ge(init_sem, 48)
            sp.wait_ge(slot_st[0], 64 * ((NT + 1) // 2))
            sp.wait_ge(slot_st[1], 64 * (NT // 2))

        @block.tensor
        def _(pe):
            B = bank

            def turn(src, b, ks, n, e):
                for q, k in enumerate(ks):
                    ins = pe.transpose(B[b][:, q * n:(q + 1) * n], src[0:n, k * P:(k + 1) * P], ident[0:n, 0:n])
                E[e].done(ins)

            def proj_T(b, cols, n, e, m=P):
                for q, c0 in enumerate(cols):
                    for k in range(KD):
                        ins = pe.matmul(B[b][0:m, q * n:(q + 1) * n], w_in[:, k, c0:c0 + m], xT[:, k, 0:n],
                                        start=(k == 0), stop=(k == KD - 1))
                E[e].done(ins)

            def proj(b, c0, n, e, ks=range(KD)):
                for k in ks:
                    ins = pe.matmul(B[b][0:n, :], xT[:, k, 0:n], w_in[:, k, c0:c0 + 512],
                                    start=(k == 0), stop=(k == KD - 1))
                if k == KD - 1:
                    E[e].done(ins)

            def f_turnA(T):
                wv("xn", pe, T)
                wv("vse", pe, T, back=1)
                turn(x[T.par], 0, range(4), T.n, "trA")

            def f_turnB(T):
                wv("sg", pe, T, back=1)
                turn(x[T.par], 1, range(4, 8), T.n, "trB")

            def f_glr(T):
                wv("xTe", pe, T)
                wv("zz", pe, T, back=1)
                proj_T(7, [O_GLR], T.n, "glr", RANK)

            def f_qk(T):
                wv("qks", pe, T, back=1)
                proj_T(2, [O_Q, O_Q + P, O_K, O_K + P], T.n, "qk")

            def f_z(T):
                wv("glrs", pe, T)
                for a in range(2):
                    ins = pe.matmul(B[7][:, a * T.n:(a + 1) * T.n], w_gk[:, a * P:(a + 1) * P],
                                    glrs[:, 0:T.n], start=True, stop=True)
                E["z"].done(ins)

            def f_u(T):
                wv("uxe", pe, T, back=1)
                proj_T(3, [O_U + g * P for g in range(NG)], T.n, "u")

            def f_v(T):
                proj(0, O_V, T.n, "v")

            def f_og(T, ks):
                proj(1, O_OG, T.n, "og", ks)

            def m_AT(T):
                wv("qdz", pe, T)
                wv("kd", pe, T)
                wv("hTe", pe, T, back=1)
                for a in range(H):
                    for c in range(NC):
                        ins = pe.matmul(B[4][c * C:(c + 1) * C, a * C:(a + 1) * C],
                                        kd[T.par][:, a // 2, c * C:(c + 1) * C],
                                        qdz[T.par][:, a, c * C:(c + 1) * C], start=True, stop=True,
                                        skip_group_check=True)
                E["AT"].done(ins)
                for a in range(2):
                    ins = pe.transpose(B[4][:, 256 + a * P:256 + (a + 1) * P], kd[T.par][:, a, :], ident[:, :])
                E["kdT"].done(ins)

            def m_o0(T):
                wv("ATs", pe, T)
                wv("vse", pe, T)
                wv("lg", pe, T, back=1)
                for a in range(H):
                    pe.matmul(B[5][:, a * DV:(a + 1) * DV], ATs[:, a, :], vs[T.par][:, a * DV:(a + 1) * DV],
                              start=(a == 0), stop=False, skip_group_check=True)
                wv("Sp", pe, T, 1)
                m_inter(T, 0)

            def m_inter(T, c):
                for a in range(H):
                    ins = pe.matmul(B[5][c * C:(c + 1) * C, a * DV:(a + 1) * DV],
                                    qdz[T.par][:, a, c * C:(c + 1) * C], Sp[c][:, a // 2, :],
                                    start=False, stop=(a == H - 1), skip_group_check=True)
                if c == NC - 1:
                    E["o"].done(ins)

            def m_P(T, c):
                wv("kdTz", pe, T)
                if c == 0:
                    wv("ohr", pe, T, back=1)
                else:
                    wv("Pt", pe, T, 2)
                for a in range(2):
                    ins = pe.matmul(B[6][:, a * 256:(a + 1) * 256], kdTz[:, c, a * P:(a + 1) * P],
                                    vs[T.par][:, a * 256:(a + 1) * 256], start=True, stop=True)
                E["Pc"].done(ins)

            def m_pool(T):
                wv("dT", pe, T)
                wv("kdTz", pe, T)
                for g in range(NG):
                    ins = pe.matmul(B[4][:, g * T.n:(g + 1) * T.n], w_pool[:, g, :], dT[T.par][:, g, 0:T.n],
                                    start=True, stop=True)
                E["zp"].done(ins)

            def m_oT(T):
                wv("on", pe, T)
                if T.kind == "p":
                    wv("Pt", pe, T)
                for a in range(H):
                    ins = pe.transpose(B[6][:, a * T.n:(a + 1) * T.n], osq[0:T.n, a * P:(a + 1) * P],
                                       ident[0:T.n, 0:T.n])
                E["oT"].done(ins)

            def b_mix(T):
                wv("zpe", pe, T)
                wv("os", pe, T)
                for half in range(2):
                    for q, k in enumerate([4, 5, 6, 7, 0, 1, 2, 3]):
                        if half == 0 and k == 0:
                            wv("oTe", pe, T)
                        ins = pe.matmul(B[4 + half][0:T.n, :], cat[:, k, 0:T.n],
                                        w_o[:, k, half * 512:(half + 1) * 512],
                                        start=(q == 0), stop=(q == KD - 1))
                    E["mix"].done(ins)

            def b_hT(T):
                wv("h", pe, T)
                turn(h, 6, range(4), T.n, "hA")
                turn(h, 4, range(4, 8), T.n, "hB")

            def b_router(T):
                wv("hTe", pe, T)
                for k in range(KD):
                    ins = pe.matmul(B[5][0:T.n, 0:NE], hT[:, k, 0:T.n], w_r[:, k, :],
                                    start=(k == 0), stop=(k == KD - 1))
                E["lgp"].done(ins)

            def b_rank(T):
                wv("sel", pe, T)
                pe.matmul(B[6][0:T.n, 0:NE], before[0:T.n, 0:T.n], sel[0:T.n, :], start=True, stop=False)
                wv("selsum", pe, T, back=1)
                ins = pe.matmul(B[6][0:T.n, 0:NE], ones[:, 0:T.n], selsum[:, :], start=False, stop=True)
                E["rank"].done(ins)

            def tile(T):
                N, L = T.later(1), T.later(-1)
                f_turnA(N)
                m_AT(T)
                f_turnB(N)
                if L:
                    b_rank(L)
                f_glr(N)
                f_qk(N)
                m_o0(T)
                m_P(T, 0)
                m_pool(T)
                f_z(N)
                f_u(N)
                wv("Sp", pe, T, 2)
                m_inter(T, 1)
                m_P(T, 1)
                f_v(N)
                m_oT(T)
                b_mix(T)
                f_og(N, range(6))
                b_hT(T)
                f_og(N, range(6, KD))
                b_router(T)

            pe.wait_ge(c_sem, 16 * N_CONST)
            for g in range(NG):
                ins = pe.transpose(B[4][:, g * 120:(g + 1) * 120], pool_old[:, g * P:(g + 1) * P],
                                   ident[0:120, 0:120])
            s_old.done(ins)
            pe.wait_ge(w_sem, 16 * 4)
            memo.wait(pe, 0, 7)
            T = Tile(0, 0)
            f_turnA(T)
            f_turnB(T)
            f_glr(T)
            f_qk(T)
            f_z(T)
            f_u(T)
            f_v(T)
            f_og(T, range(KD))
            s_olde.wait(pe, 0)
            pe.wait_ge(wo_sem, 16 * 3)
            in_order(pe, tile)
            b_rank(Tile(PT // 2 - 1, 1))
            E["hTe"].wait(pe, PT - 1)
            for g in range(NG):
                ins = pe.transpose(B[4][0:BUF, g * P:(g + 1) * P], ux[1][:, g, P:P + BUF], ident[:, :])
            s_pnt.done(ins)
            T = Tile(PT // 2, 0, "s")
            s_pne.wait(pe, 0)
            E["uxe"].wait(pe, PT)
            s_olde.wait(pe, 0)
            for g in range(NG):
                ins = pe.transpose(B[4][0:NS, g * P:(g + 1) * P], uc[:, g, :], ident[:, :])
            s_newt.done(ins)
            wv("qdz", pe, T)
            wv("kd", pe, T)
            s_newe.wait(pe, 0)
            for a in range(H):
                ins = pe.matmul(B[4][0:NS, a * NS:(a + 1) * NS], kd[0][:, a // 2, 0:NS], qdz[0][:, a, 0:NS],
                                start=True, stop=True, skip_group_check=True)
            E["AT"].done(ins)
            for a in range(2):
                ins = pe.transpose(B[4][0:NS, 256 + a * P:256 + (a + 1) * P], kd[0][:, a, 0:NS], ident[:, :])
            E["kdT"].done(ins)
            wv("ATs", pe, T)
            wv("vse", pe, T)
            wv("lg", pe, T, back=1)
            for a in range(H):
                pe.matmul(B[5][0:NS, a * DV:(a + 1) * DV], ATs[0:NS, a, 0:NS], vs[0][0:NS, a * DV:(a + 1) * DV],
                          start=(a == 0), stop=False, skip_group_check=True)
            pe.wait_ge(s0_in, 64)
            s_misc.wait(pe, 0, NSEQ)
            for b in range(NSEQ):
                for a in range(H):
                    ins = pe.matmul(B[5][0:NS, a * DV:(a + 1) * DV], Q8[:, a, b, :], S0[:, b, a // 2, :],
                                    start=False, stop=(b == NSEQ - 1), skip_group_check=True)
            E["o"].done(ins)
            wv("ohr", pe, T, back=1)
            for b in range(NSEQ):
                s_T8.wait(pe, 0, b + 1)
                if b:
                    s_S8.wait(pe, 0, b)
                for a in range(2):
                    ins = pe.matmul(B[6][:, a * 256:(a + 1) * 256], kdT8[:, b, a * P:(a + 1) * P],
                                    vs[0][0:NS, a * 256:(a + 1) * 256], start=True, stop=True)
                s_P8.done(ins)
            s_T8.wait(pe, 0, NSEQ)
            wv("dT", pe, T)
            for g in range(NG):
                ins = pe.matmul(B[4][:, g * NS:(g + 1) * NS], w_pool[:, g, :], dT[0][:, g, 0:NS],
                                start=True, stop=True)
            E["zp"].done(ins)
            s_S8.wait(pe, 0, NSEQ)
            m_oT(T)
            b_mix(T)
            b_hT(T)
            b_router(T)
            b_rank(T)
            E["selsum"].wait(pe, PT)
            E["ohr"].wait(pe, PT)
            s_cnt.done(pe.matmul(B[6][:, 0:NE], ones[:, :], selsum[:, :], start=True, stop=True))

        @block.scalar
        def _(act):
            B = bank

            def f_ss(T):
                waitx(act, T)
                wv("lgp", act, T, back=3)
                wv("hTe", act, T, back=3)
                wv("ss1", act, T, back=1)
                E["ss1"].done(act.activation(hT[:, :, :].rearrange("p k n -> p (k n)")[0:T.n, :], x[T.par][0:T.n, :], ACT.Square,
                                             accum_out=ss1[0:T.n, :]))

            def f_xT(T):
                for half, e in enumerate(("trA", "trB")):
                    wv(e, act, T)
                    if half == 0:
                        wv("og", act, T, back=1)
                    E["xTe"].done(act.activation(
                        xT[:, 4 * half:4 * half + 4, 0:T.n],
                        B[half][:, 0:4 * T.n].rearrange("p (k n) -> p k n", k=4), ACT.Copy))

            def f_glr(T):
                wv("glr", act, T)
                E["glrs"].done(act.activation(glrs[:, 0:T.n], B[7][0:RANK, 0:T.n], ACT.Copy))

            def f_qk(T):
                wv("qk", act, T)
                wv("kd", act, T, back=1)
                E["qks"].done(act.activation(qks[:, :, 0:T.n], B[2][:, 0:4 * T.n].rearrange(
                    "p (k n) -> p k n", k=4), ACT.Copy))

            def f_gate(T):
                wv("az", act, T)
                E["e1"].done(act.activation(e1[:, 0:2 * T.n], az[:, 0:2 * T.n], ACT.Exp, scale=-1.0))
                wv("e1", act, T)
                E["l1"].done(act.activation(l1[:, 0:2 * T.n], e1[:, 0:2 * T.n], ACT.Ln, bias=1.0))

            def f_u(T):
                wv("u", act, T)
                src = B[3][:, 0:4 * T.n]
                if T.kind == "p":
                    wv("dT", act, T, back=2)
                    wv("hist", act, T, back=1)
                    E["uxe"].done(act.activation(ux[T.par][:, :, BUF:], src.rearrange("p (g n) -> p g n", g=NG),
                                                 ACT.Copy))
                else:
                    s_misc2.done(act.activation(uxs[:, :, :, BUF:], src.rearrange(
                        "p (g s l) -> p g s l", g=NG, l=LSEQ), ACT.Copy))
                    E["uxe"].done(act.activation(uc[:, :, :], src.rearrange("p (g n) -> p g n", g=NG), ACT.Copy))

            def f_v(T):
                wv("v", act, T)
                wv("Pc", act, T, back=2)
                E["vse"].done(act.activation(vs[T.par][0:T.n, :], B[0][0:T.n, :], ACT.Copy))

            def f_og(T):
                wv("og", act, T)
                E["eog"].done(act.activation(eog[0:T.n, :], B[1][0:T.n, :], ACT.Exp, scale=-1.0))

            def f_decay(T):
                wv("Dm", act, T)
                wv("qdz", act, T, back=1)
                E["eqk"].done(act.activation(eq[:, 0:2 * T.n], Dm[:, 0:2 * T.n], ACT.Exp, scale=1 / GATE_DIV))
                wv("kd", act, T, back=1)
                E["eqk"].done(act.activation(ek[:, 0:2 * T.n], Dm[:, 0:2 * T.n], ACT.Exp, scale=-1 / GATE_DIV))

            def f_small(T):
                wv("Pt", act, T, back=2)
                Gc = G[:, :].rearrange("p (q c) -> p q c", c=C)
                E["esm"].done(act.activation(esm[T.par][:, 0, :], Gc[:, :, C // 2 - 1], ACT.Exp, scale=1 / GATE_DIV))
                E["esm"].done(act.activation(esm[T.par][:, 1, :], Gc[:, :, C - 1], ACT.Exp, scale=1 / GATE_DIV))
                wv("lr", act, T)
                E["esm"].done(act.activation(esm[T.par][:, 2, :], lr[:, :], ACT.Exp, scale=1 / GATE_DIV))

            def m_os(T):
                wv("o", act, T)
                wv("on", act, T, back=1)
                E["os"].done(act.activation(os_[0:T.n, :], B[5][0:T.n, :], ACT.Copy))

            def m_pool(T):
                wv("zp", act, T)
                wv("mix", act, T, back=1)
                E["zpe"].done(act.activation(cat[:, NG:, 0:T.n], B[4][:, 0:4 * T.n].rearrange(
                    "p (g n) -> p g n", g=NG), ACT.Copy))

            def m_oT(T):
                wv("oT", act, T)
                E["oTe"].done(act.activation(cat[:, 0:H, 0:T.n], B[6][:, 0:4 * T.n].rearrange(
                    "p (g n) -> p g n", g=H), ACT.Copy, scale=glan[:, 0:1]))

            def b_ss(T):
                wv("x1", act, T)
                wv("hB", act, T, back=1)
                if not (T.static and T.t == 0):
                    act.wait_ge(h_st[0], T.t * 16)
                E["ss2"].done(act.activation(h[0:T.n, :], xr[0:T.n, :], ACT.Square, accum_out=ss2[0:T.n, :]))

            def b_hT(T):
                squares(T)
                for half, e in enumerate(("hA", "hB")):
                    wv(e, act, T)
                    b = (6, 4)[half]
                    E["hTe"].done(act.activation(hT[:, 4 * half:4 * half + 4, 0:T.n],
                                                 B[b][:, 0:4 * T.n].rearrange("p (k n) -> p k n", k=4), ACT.Copy))

            def b_gates(T):
                wv("ng", act, T)
                E["e4"].done(act.activation(e4[0:T.n, :], top[0:T.n, 0:TOPK], ACT.Exp, bias=ng[0:T.n, 0:1],
                                            accum_out=sum4[0:T.n, :]))

            def squares(T):
                M = T.later(2)
                wv("ss1", act, M if M else Tile(PT // 2, 0, "s"))

            def tile(T):
                N, M = T.later(1), T.later(2)
                f_xT(N)
                f_glr(N)
                f_qk(N)
                m_pool(T)
                f_gate(N)
                f_u(N)
                if N.kind == "p":
                    f_decay(N)
                    f_small(N)
                else:
                    s_decay(N)
                m_os(T)
                f_v(N)
                m_oT(T)
                if M:
                    f_ss(M)
                b_ss(T)
                f_og(N)
                b_hT(T)
                b_gates(T)

            def s_decay(T):
                wv("G", act, T)
                wv("qdz", act, T, back=1)
                wv("kd", act, T, back=1)
                E["eqk"].done(act.activation(eq[:, 0:2 * NS], G[:, 0:2 * NS], ACT.Exp, scale=1 / GATE_DIV))
                E["eqk"].done(act.activation(ek[:, 0:2 * NS], G[:, 0:2 * NS], ACT.Exp, scale=-1 / GATE_DIV))
                E["esm"].done(act.activation(els[:, :], G[:, 0:2 * NS].rearrange("p (q l) -> p q l", l=LSEQ)[:, :, LSEQ - 1],
                                             ACT.Exp, scale=1 / GATE_DIV))

            act.wait_ge(c_sem, 16 * N_CONST)
            s_old.wait(act, 0)
            s_olde.done(act.activation(uxs[:, :, :, 0:BUF], B[4][:, 0:480].rearrange(
                "p (g s r) -> p g s r", g=NG, s=NSEQ), ACT.Copy))
            T = Tile(0, 0)
            f_ss(T)
            f_xT(T)
            f_glr(T)
            f_qk(T)
            f_ss(Tile(0, 1))
            f_gate(T)
            f_u(T)
            f_decay(T)
            f_small(T)
            f_v(T)
            f_og(T)
            in_order(act, tile)
            s_pnt.wait(act, 0)
            E["on1"].wait(act, PT - 1)
            s_pne.done(act.activation(last_rows.rearrange("r (g c) -> r g c", g=NG), B[4][0:BUF, :].rearrange("r (g c) -> r g c", g=NG),
                                      ACT.Copy))
            T = Tile(PT // 2, 0, "s")
            s_newt.wait(act, 0)
            s_newe.done(act.activation(os_new, B[4][0:NS, :], ACT.Copy))
            m_os(T)
            m_pool(T)
            m_oT(T)
            b_ss(T)
            b_hT(T)
            b_gates(T)

        @block.vector
        def _(dve):
            B = bank

            def tt(e, out, a, b, op):
                E[e].done(dve.tensor_tensor(out, a, b, op))

            def f_ms(T):
                wv("ss1", dve, T)
                E["ms1"].done(dve.tensor_scalar(ms1[0:T.n, :], ss1[0:T.n, :], 1.0 / D, EPS, ALU.mult, ALU.add))

            def f_xn(T):
                wv("rs1", dve, T)
                wv("ss1", dve, T)
                E["xn"].done(dve.scalar_tensor_tensor(x[T.par][0:T.n, :], x[T.par][0:T.n, :], rs1[0:T.n, 0:1],
                                                      n1[0:T.n, :], ALU.mult, ALU.mult))

            def f_gate(T):
                n2_ = 2 * T.n
                wv("z", dve, T)
                for a in range(2):
                    E["zz"].done(dve.tensor_scalar(zz[:, a * T.n:(a + 1) * T.n], B[7][:, a * T.n:(a + 1) * T.n],
                                                   b_gk[:, a:a + 1], None, ALU.add))
                wv("zz", dve, T)
                E["az"].done(dve.scalar_tensor_tensor(az[:, 0:n2_], zz[:, 0:n2_], -1.0, zz[:, 0:n2_],
                                                      ALU.mult, ALU.max))
                wv("l1", dve, T)
                E["gk"].done(dve.scalar_tensor_tensor(gk[:, 0:n2_], zz[:, 0:n2_], 0.0, l1[:, 0:n2_],
                                                      ALU.min, ALU.subtract))
                wv("gk", dve, T)
                mask = scan_p if T.kind == "p" else scan_s
                wv("esm", dve, T, back=1)
                E["G"].done(dve.tensor_tensor_scan(G[:, 0:n2_], mask[:, 0:n2_], gk[:, 0:n2_], 0.0,
                                                   ALU.mult, ALU.add))
                wv("G", dve, T)
                if T.kind == "p":
                    Gc = G[:, :].rearrange("p (q c) -> p q c", c=C)
                    wv("eqk", dve, T, back=1)
                    tt("Dm", Dm[:, :].rearrange("p (q c) -> p q c", c=C), Gc,
                       Gc[:, :, C // 2 - 1:C // 2].to_broadcast([P, 4, C]), ALU.subtract)
                    tt("lr", lr[:, :], Gc[:, :, C - 1], Gc[:, :, C // 2 - 1], ALU.subtract)

            def f_og(T):
                wv("eog", dve, T)
                E["dog"].done(dve.tensor_scalar(dog[0:T.n, :], eog[0:T.n, :], 1.0, None, ALU.add))
                wv("dog", dve, T)
                E["rog"].done(dve.reciprocal(dog[0:T.n, :], dog[0:T.n, :]))
                wv("rog", dve, T)
                tt("sg", sg[T.par][0:T.n, :], B[1][0:T.n, :], dog[0:T.n, :], ALU.mult)

            def f_qd(T):
                n = T.n
                wv("qks", dve, T)
                wv("eqk", dve, T)
                wv("o", dve, T, back=2)
                eqv = eq[:, 0:2 * n].rearrange("p (a n) -> p a n", a=2)
                ekv = ek[:, 0:2 * n].rearrange("p (a n) -> p a n", a=2)
                for r in range(2):
                    s = slice(r * DK, (r + 1) * DK)
                    E["qdz"].done(dve.scalar_tensor_tensor(qdz[T.par][s, r::2, 0:n], qks[s, 0:2, 0:n], DK ** -0.5,
                                                           eqv[s], ALU.mult, ALU.mult))
                wv("kdT", dve, T, back=2)
                tt("kd", kd[T.par][:, :, 0:n], qks[:, 2:4, 0:n], ekv, ALU.mult)

            def m_AT(T):
                wv("kdT", dve, T)
                wv("o", dve, T, back=1)
                for c in range(NC):
                    s = slice(c * C, (c + 1) * C)
                    E["kdTz"].done(dve.tensor_copy(kdTz[s, c, :], B[4][s, 256:512]))
                for c in range(NC):
                    s = slice(c * C, (c + 1) * C)
                    E["ATs"].done(dve.copy_predicated(
                        ATs[s, :, s], causal_p[s, :].rearrange("p (a i) -> p a i", a=H),
                        B[4][s, 0:H * C].rearrange("p (a i) -> p a i", a=H)))

            def small(T, k, c, s=slice(0, P)):
                return esm[T.par][s, k, c::NC].unsqueeze(2).to_broadcast([s.stop - s.start, 2, DV])

            def m_Sp(T, c):
                if c == 0:
                    wv("esm", dve, T)
                    wv("S", dve, T, back=1)
                else:
                    wv("S", dve, T, 1)
                tt("Sp", Sp[c][:, :, :], S[:, :, :], small(T, 0, c), ALU.mult)

            def m_S(T, c):
                tt("Sm", Sm[:, :, :], S[:, :, :], small(T, 1, c), ALU.mult)
                wv("Pc", dve, T, c + 1)
                for r in range(2):
                    s = slice(r * DK, (r + 1) * DK)
                    src = B[6][s, :].rearrange("p (a b v) -> p a b v", a=2, b=2)[:, :, r, :]
                    tt("Pt", Pt[s, :, :], src, small(T, 2, c, s), ALU.mult)
                wv("Sm", dve, T, c + 1)
                wv("Pt", dve, T, 2 * c + 2)
                tt("S", S[:, :, :], Sm[:, :, :], Pt[:, :, :], ALU.add)

            def m_o(T):
                n = T.n
                wv("os", dve, T)
                wv("oT", dve, T, back=1)
                tt("osq", osq[0:n, :], os_[0:n, :], os_[0:n, :], ALU.mult)
                wv("osq", dve, T)
                E["so"].done(dve.tensor_reduce(so[0:n, :], osq[0:n, :].rearrange("p (a v) -> p a v", a=H), AX, ALU.add))
                wv("so", dve, T)
                E["mso"].done(dve.tensor_scalar(mso[0:n, :], so[0:n, :], 1.0 / DV, EPS, ALU.mult, ALU.add))
                wv("sg", dve, T)
                tt("on1", os_[0:n, :], os_[0:n, :], sg[T.par][0:n, :], ALU.mult)
                wv("rso", dve, T)
                wv("on1", dve, T)
                tt("on", osq[0:n, :].rearrange("p (a v) -> p a v", a=H),
                   os_[0:n, :].rearrange("p (a v) -> p a v", a=H),
                   rso[0:n, :].unsqueeze(2).to_broadcast([n, H, DV]), ALU.mult)

            def b_x1(T):
                dve.wait_ge(xr_in, T.t * 16 + 16)
                for half in range(2):
                    c = slice(half * 512, (half + 1) * 512)
                    wv("mix", dve, T, half + 1)
                    tt("x1", xr[0:T.n, c], B[4 + half][0:T.n, :], xr[0:T.n, c], ALU.add)

            def b_h(T):
                wv("ss2", dve, T)
                E["ms2"].done(dve.tensor_scalar(ms2[0:T.n, :], ss2[0:T.n, :], 1.0 / D, EPS, ALU.mult, ALU.add))
                wv("rs2", dve, T)
                wv("x1", dve, T)
                E["h"].done(dve.scalar_tensor_tensor(h[0:T.n, :], xr[0:T.n, :], rs2[0:T.n, 0:1], n2[0:T.n, :],
                                                     ALU.mult, ALU.mult))

            def b_top(T):
                n = T.n
                wv("lgp", dve, T)
                tt("lg", lg[0:n, :], B[5][0:n, 0:NE], b_r[0:n, :], ALU.add)
                pairs = T.pair * 64
                if not (isinstance(pairs, int) and pairs == 0):
                    dve.wait_ge(slot_st[T.par], pairs)
                wv("lg", dve, T)
                tok = token_no[:, PT:NT] if T.kind == "s" else token_no[:, bass.ds(T.t, 1)]
                E["tokid"].done(dve.tensor_copy(meta[T.par][0:n, :, 0], tok[0:n, :].to_broadcast([n, TOPK])))
                E["top"].done(dve.max(top[0:n, :], lg[0:n, :]))
                wv("top", dve, T)
                E["ng"].done(dve.tensor_scalar(ng[0:n, :], top[0:n, 0:1], -1.0, None, ALU.mult))
                E["idx"].done(dve.max_index(idx[0:n, :], top[0:n, :], lg[0:n, :]))
                wv("idx", dve, T)
                E["idf"].done(dve.tensor_copy(idf[0:n, :], idx[0:n, 0:TOPK]))
                wv("idf", dve, T)
                tt("oh", oh[0:n, :, :], expert_no[0:n, :].rearrange("p (k e) -> p k e", k=TOPK),
                   idf[0:n, :].unsqueeze(2).to_broadcast([n, TOPK, NE]), ALU.is_equal)
                wv("oh", dve, T)
                wv("rank", dve, T, back=1)
                E["sel"].done(dve.tensor_reduce(sel[0:n, :], oh[0:n, :, :].rearrange("p k e -> p e k"), AX, ALU.add))

            def b_gates(T):
                n = T.n
                wv("e4", dve, T)
                E["rs4"].done(dve.reciprocal(rs4[0:n, :], sum4[0:n, :]))
                wv("rs4", dve, T)
                E["gate"].done(dve.tensor_scalar(meta[T.par][0:n, :, 1].bitcast(F32), e4[0:n, :], rs4[0:n, 0:1],
                                                 None, ALU.mult))

            def b_slot(T):
                n = T.n
                wv("rank", dve, T)
                tt("ohr", ohr[0:n, :, :], B[6][0:n, 0:NE].unsqueeze(1).to_broadcast([n, TOPK, NE]), oh[0:n, :, :],
                   ALU.mult)
                wv("sel", dve, T)
                tt("selsum", selsum[0:n, :], selsum[0:n, :], sel[0:n, :], ALU.add)
                wv("ohr", dve, T)
                E["r4"].done(dve.tensor_reduce(r4[0:n, :], ohr[0:n, :, :], AX, ALU.add))
                wv("r4", dve, T)
                E["slotf"].done(dve.scalar_tensor_tensor(slotf[0:n, :], idf[0:n, :], float(REGION), r4[0:n, :],
                                                         ALU.mult, ALU.add))
                wv("slotf", dve, T)
                E["slot"].done(dve.tensor_copy(slot[T.par][0:n, :], slotf[0:n, :]))

            def tile(T):
                N, M, L = T.later(1), T.later(2), T.later(-1)
                m_Sp(T, 0)
                m_AT(T)
                if L:
                    b_slot(L)
                m_S(T, 0)
                m_Sp(T, 1)
                f_gate(N)
                m_S(T, 1)
                m_o(T)
                f_qd(N)
                if M:
                    f_ms(M)
                b_x1(T)
                if M:
                    f_xn(M)
                b_h(T)
                f_og(N)
                b_top(T)
                b_gates(T)

            dve.wait_ge(c_sem, 16 * N_CONST)
            for buf in (S, selsum, ATs, kdTz, qdz[0], qdz[1]):
                memo.done(dve.memset(buf[tuple([slice(None)] * len(buf.shape))], 0.0))
            dve.wait_ge(w_sem, 16 * 4)
            memo.done(dve.tensor_tensor(w_pool[:, :, :].rearrange("p g e -> p (g e)"),
                                        w_pool[:, :, :].rearrange("p g e -> p (g e)"), pscale[:, :], ALU.mult))
            memo.wait(dve, 0, 7)
            T = Tile(0, 0)
            f_ms(T)
            f_xn(T)
            f_ms(T.later(1))
            f_xn(T.later(1))
            f_gate(T)
            f_qd(T)
            f_og(T)
            in_order(dve, tile)
            b_slot(Tile(PT // 2 - 1, 1))
            T = Tile(PT // 2, 0, "s")
            wv("qdz", dve, T)
            wv("og", dve, T)
            memo.done(dve.memset(Q8, 0.0))
            memo.wait(dve, 0, 8)
            for b in range(NSEQ):
                s_misc.done(dve.tensor_copy(Q8[:, :, b, b * LSEQ:(b + 1) * LSEQ],
                                            qdz[0][:, :, b * LSEQ:(b + 1) * LSEQ]))
            wv("kdT", dve, T)
            wv("o", dve, T, back=1)
            s_misc.done(dve.memset(ATs[0:NS, :, 0:NS], 0.0))
            s_misc.wait(dve, 0, NSEQ + 1)
            for s in (slice(0, NS // 2), slice(NS // 2, NS)):
                E["ATs"].done(dve.copy_predicated(ATs[s, :, 0:NS],
                                                  causal_s[s, :].rearrange("p (a i) -> p a i", a=H),
                                                  B[4][s, 0:H * NS].rearrange("p (a i) -> p a i", a=H)))
            for b in range(NSEQ):
                s_T8.done(dve.tensor_scalar(kdT8[:, b, :], B[4][0:NS, 256:512], seq_of[:, b:b + 1], None, ALU.mult))
            wv("esm", dve, T, 1)
            wv("o", dve, T)
            for b in range(NSEQ):
                s_P8.wait(dve, 0, b + 1)
                for r in range(2):
                    s = slice(r * DK, (r + 1) * DK)
                    src = B[6][s, :].rearrange("p (a b v) -> p a b v", a=2, b=2)[:, :, r, :]
                    s_misc.done(dve.tensor_tensor(S0[s, b, :, :], src, S0[s, b, :, :], ALU.add))
                s_misc.wait(dve, 0, NSEQ + 3 + 2 * b)
                el = els[:, b::NSEQ].unsqueeze(2).to_broadcast([P, 2, DV])
                s_S8.done(dve.tensor_tensor(S0[:, b, :, :], S0[:, b, :, :], el, ALU.mult))
            m_o(T)
            b_x1(T)
            b_h(T)
            b_top(T)
            b_gates(T)
            b_slot(T)
            s_cnt.wait(dve, 0)
            step = [0]

            def chain(ins):
                step[0] += 1
                s_tab.done(ins)
                s_tab.wait(dve, 0, step[0])

            cnt, nch, end = ctab["cnt"], ctab["nch"], ctab["end"]
            dve.wait_ge(no_sem, 16)
            chain(dve.tensor_copy(cnt[0:1, :], B[6][0:1, 0:NE]))
            chain(dve.tensor_scalar(nch[0:1, :], cnt[0:1, :], 0.0, None, ALU.is_gt))
            for m in range(1, CPE):
                chain(dve.scalar_tensor_tensor(nch[0:1, :], cnt[0:1, :], float(m * CHUNK), nch[0:1, :],
                                               ALU.is_gt, ALU.add))
            chain(dve.tensor_tensor_scan(end[0:1, :], ones[0:1, 0:NE], nch[0:1, :], 0.0, ALU.mult, ALU.add))
            def bc(a):
                return a[0:1, :].unsqueeze(1).to_broadcast([1, NTAB, NE])
            cn = chunk_no.rearrange("o (i e) -> o i e", e=NE)
            chain(dve.tensor_tensor(ge, cn, bc(end), ALU.is_ge))
            chain(dve.tensor_tensor(geb, ge, bc(nch), ALU.mult))
            ex, bs, sz = ctab["ex"], ctab["bs"], ctab["sz"]
            chain(dve.tensor_reduce(ex[0:1, :], ge, AX, ALU.add))
            chain(dve.tensor_reduce(bs[0:1, :], geb, AX, ALU.add))
            chain(dve.tensor_scalar(ex[0:1, :], ex[0:1, :], float(NE - 1), None, ALU.min))
            chain(dve.tensor_tensor(bs[0:1, :], cn[:, :, 0], bs[0:1, :], ALU.subtract))
            chain(dve.tensor_scalar(bs[0:1, :], bs[0:1, :], float(CPE - 1), float(CHUNK), ALU.min, ALU.mult))
            exb = ex[0:1, :].unsqueeze(2).to_broadcast([1, NTAB, NE])
            eno = expert_no[0:1, 0:NE].unsqueeze(1).to_broadcast([1, NTAB, NE])
            chain(dve.tensor_tensor(ge, eno, exb, ALU.is_equal))
            chain(dve.tensor_tensor(ge, ge, bc(cnt), ALU.mult))
            chain(dve.tensor_reduce(sz[0:1, :], ge, AX, ALU.add))
            chain(dve.tensor_tensor(sz[0:1, :], sz[0:1, :], bs[0:1, :], ALU.subtract))
            chain(dve.tensor_scalar(sz[0:1, :], sz[0:1, :], 0.0, float(CHUNK), ALU.max, ALU.min))
            chain(dve.tensor_copy(tab[0:1, SIZES:SIZES + NTAB], sz[0:1, :]))
            chain(dve.scalar_tensor_tensor(bs[0:1, :], ex[0:1, :], float(REGION), bs[0:1, :], ALU.mult, ALU.add))
            chain(dve.tensor_copy(tab[0:1, 0:NTAB], ex[0:1, :]))
            chain(dve.tensor_copy(tab[0:1, NTAB:2 * NTAB], bs[0:1, :]))
            chain(dve.tensor_copy(tab[0:1, 2 * NTAB:2 * NTAB + 1], end[0:1, NE - 1:NE]))

        @block.gpsimd
        def _(pool):
            def root(T, src, dst, e_in, e, m):
                wv(e_in, pool, T)
                E[e].done(pool.tensor_tensor(dst[0:T.n, :], src[0:T.n, :], neghalf[0:T.n, 0:m], ALU.pow))

            one = ones[:, 0:NG * BUF].rearrange("p (g r) -> p g r", g=NG)

            def f_pool(T):
                n = T.n
                if T.kind == "p":
                    cur = ux[T.par]
                    if T.static and T.t == 0:
                        E["hist"].done(pool.memset(cur[:, :, 0:BUF], 0.0))
                    else:
                        wv("uxe", pool, T, back=1)
                        last = ux[1 - T.par][:, :, P:P + BUF]
                        E["hist"].done(pool.tensor_tensor(cur[:, :, 0:BUF], last, one, ALU.mult))
                    wv("uxe", pool, T)
                    wv("hist", pool, T)
                    L, s = P, 1
                    src = cur[:, :, :].unsqueeze(2)
                else:
                    s_olde.wait(pool, 0)
                    s_misc2.wait(pool, 0)
                    L, s = LSEQ, NSEQ
                    src = uxs[:, :, :, :]
                W = BUF + L
                A = pa[:, :, 0:s * W].rearrange("p g (s w) -> p g s w", s=s)
                B_ = pb[:, :, 0:s * W].rearrange("p g (s w) -> p g s w", s=s)

                def grow(dst, a, g0, lo, step, k):
                    E["pool"].done(pool.tensor_tensor(dst[:, g0:, :, lo:W], a[:, g0:, :, lo:W],
                                                      a[:, g0:, :, lo - step:W - step], ALU.add))
                    wv("pool", pool, T, k)

                grow(A, src, 0, 1, 1, 1)
                grow(B_, A, 1, 3, 2, 2)
                grow(A, B_, 2, 7, 4, 3)
                grow(B_, A, 3, 15, 8, 4)
                wv("zp", pool, T, back=2)
                d4 = dT[T.par][:, :, 0:n].rearrange("p g (s l) -> p g s l", s=s)
                i4 = inv[:, :, 0:n].rearrange("p g (s l) -> p g s l", s=s)
                for q, a in enumerate((A, B_)):
                    E["mean"].done(pool.tensor_tensor(d4[:, q::2], a[:, q::2, :, BUF:], i4[:, q::2], ALU.mult))
                wv("mean", pool, T)
                E["dT"].done(pool.tensor_tensor(d4, d4, src[:, :, :, BUF:], ALU.subtract))
                rest = inv_rest[:, :].rearrange("p (g r) -> p g r", g=NG)
                E["pool"].done(pool.tensor_tensor(inv[:, :, 0:BUF], rest, one, ALU.mult))
                wv("pool", pool, T)

            def b_routed(T, back=0):
                wv("slot", pool, T, back=back)
                wv("gate", pool, T, back=back)
                wv("tokid", pool, T, back=back)

            def b_scatter(par, n):
                for k in range(TOPK):
                    pool.indirect_dma_start(
                        X["slots"][:, :], bass.IndirectOffsetOnAxis(slot[par][0:n, k:k + 1], 0),
                        meta[par][0:n, k, :], None).then_inc(slot_st[par], 16)

            def tile(T):
                b_routed(T, back=1)
                root(T, mso, rso, "mso", "rso", 4)
                if T.later(-1):
                    b_scatter(1 - T.par, P)
                f_pool(T.later(1))
                if T.later(2):
                    root(T.later(2), ms1, rs1, "ms1", "rs1", 1)
                root(T, ms2, rs2, "ms2", "rs2", 1)

            neg = ev("neghalf_set")
            neg.done(pool.memset(neghalf[:, :], -0.5))
            neg.wait(pool, 0)
            pool.wait_ge(c_sem, 16 * N_CONST)
            pool.wait_ge(init_sem, 48)
            for T in (Tile(0, 0), Tile(0, 1)):
                root(T, ms1, rs1, "ms1", "rs1", 1)
            f_pool(Tile(0, 0))
            in_order(pool, tile)
            b_routed(Tile(PT // 2 - 1, 1))
            T = Tile(PT // 2, 0, "s")
            root(T, mso, rso, "mso", "rso", 4)
            b_scatter(1, P)
            root(T, ms2, rs2, "ms2", "rs2", 1)
            b_routed(T)
            b_scatter(0, NS)

N_CONST = 2 + 11 + 2 + 3 + 1

def experts(nc, I, X, tab):
    with ExitStack() as ctx:
        def sb(name, shape, dt=F32):
            return ctx.enter_context(nc.sbuf_tensor(name, shape, dt))

        def sem(name):
            return ctx.enter_context(nc.semaphore(name))

        def ev(name, per=1):
            return Event(ctx, nc, name, per)

        B = [ctx.enter_context(nc.psum_tensor(f"ebank{b}", [P, 512], F32)) for b in range(7)]
        raw = [sb(f"raw{b}", [P, PIECE]) for b in range(2)]
        wh = [sb(f"wh{b}", [P, PIECE // 2], F32R) for b in range(4)]
        wl = [sb(f"wl{b}", [P, PIECE // 2], F32R) for b in range(4)]
        xg = sb("xg", [P, 3, D])
        xh = sb("xh", [P, KD, CHUNK], F32R)
        xl = sb("xl", [P, KD, CHUNK], F32R)
        ah = sb("ah", [P, KD, CHUNK], F32R)
        al = sb("al", [P, KD, CHUNK], F32R)
        g_, u_, u2, gu_, sg_ = (sb(n, [P, CHUNK]) for n in ("gate", "up", "up1", "gateup", "sig"))
        a_ = [sb(f"act{b}", [P, CHUNK]) for b in range(2)]
        osb = sb("osb", [P, 3, D])
        bd = sb("b_down_rows", [P, D])
        ident = sb("eident", [P, P])
        bgu_rows = sb("bgu_rows", [NE, 2 * FF])
        bgu = sb("bgu", [P, 2 * KD, NE])
        bcur = sb("bcur", [P, 2 * KD])
        mnx = sb("slots_next", [P, 3, 2], I32)
        mcur = sb("slots_now", [P, 3, 2], I32)

        raw_in = [sem("raw_in0"), sem("raw_in1")]
        ld, meta_in, x_in, bd_in, sc = (sem(n) for n in ("loaded", "slots_in", "rows_in", "b_down_in", "rows_added"))
        bturn, bkept = ev("bias_turned"), ev("bias_kept")
        hi, lo = ev("w_hi", 12), ev("w_lo", 12)
        trx, xhe, xle = ev("x_turned", 8), ev("x_hi", 8), ev("x_lo", 8)
        gu, dn = ev("gate_up_done", 8), ev("down_done", 6)
        mc, bc = ev("slots_now_set", 2), ev("bias_now_set")
        g1, u1, u1b, gm, ac = (ev(n, 8) for n in ("gate_clamped", "up_clamped", "up_plus1", "gate_times_up", "act_done"))
        sgm, ahe, ale = ev("sigmoid_done", 8), ev("act_hi", 8), ev("act_lo", 8)
        ob, osc = ev("out_biased", 6), ev("out_scaled", 6)
        mc0, last = ev("first_slots_set"), ev("last_rows_scaled")
        carry = sb("carry", [1, 1])

        wgu = I["w_gate_up"][0].rearrange("e (k p) n -> e p k n", p=P)
        wdn = I["w_down"][0].rearrange("e (k p) n -> e p k n", p=P)

        def raw_part(q):
            r = raw[q // 2 % 2]
            if q % 12 < 8:
                return r[:, :].rearrange("p (gk c) -> p gk c", c=256)[:, :, q % 2 * P:q % 2 * P + P]
            return r[:, q % 2 * (PIECE // 2):(q % 2 + 1) * (PIECE // 2)].rearrange("p (gk c) -> p gk c", c=P)

        def part(w, q):
            return w[q % 4][:, :].rearrange("p (gk c) -> p gk c", c=P)

        def n_chunks(eng):
            return eng.value_load(tab[0:1, 2 * NTAB:2 * NTAB + 1], min_val=1, max_val=MAXC)

        def expert_of(eng, i):
            return eng.value_load(tab[0:1, bass.ds(i, 1)], min_val=0, max_val=NE - 1)

        block = ctx.enter_context(nc.Block())

        @block.sync
        def _(sp):
            def piece(e, i, p):
                sp.wait_ge(lo.sem, i * 12 + (2 * p + 2))
                s = p % 2
                if p < 4:
                    v = raw[s][:, :].rearrange("p (g k c) -> p g k c", g=2, k=KD)
                    for g in range(2):
                        sp.dma_start(v[:, g], wgu[e, :, :, g * FF + p * 256:g * FF + (p + 1) * 256]).then_inc(raw_in[s], 16)
                else:
                    v = raw[s][:, :].rearrange("p (k c) -> p k c", k=KD)
                    for q in range(2):
                        sp.dma_start(v[:, 4 * q:4 * q + 4], wdn[e, :, 4 * q:4 * q + 4, (p - 4) * 512:(p - 3) * 512]).then_inc(raw_in[s], 16)

            sp.dma_start(ident[:, :], I["ident"]).then_inc(ld, 16)
            sp.dma_start(bgu_rows[:, :], I["b_gate_up"][0]).then_inc(ld, 16)
            n = n_chunks(sp)
            with sp.Fori(0, n) as i:
                e = expert_of(sp, i)
                for p in range(6):
                    piece(e, i, p)
                    if p == 2:
                        ob.wait(sp, i, 3)
                        sp.dma_start(bd[:, :], I["b_down"][0, bass.ds(e, 1), :].to_broadcast([P, D])).then_inc(bd_in, 16)
            e = expert_of(sp, n)
            for p in range(2):
                piece(e, n, p)

        @block.tensor
        def _(pe):
            def turn_x(i, k):
                for s0, m in SUBS:
                    ins = pe.transpose(B[k % 4][:, s0:s0 + m], xg[0:m, s0 // P, k * P:(k + 1) * P], ident[0:m, 0:m])
                trx.done(ins)

            def gate_up(i, j, width):
                jj = j % 2
                pe.wait_ge(lo.sem, i * 12 + (j + 5))
                if j >= 2:
                    u1.wait(pe, i, j - 1)
                h_, l_ = (w[j % 4][:, :].rearrange("p (g k c) -> p g k c", g=2, k=KD) for w in (wh, wl))
                for g in range(2):
                    out = B[2 * jj + g][:, 0:width]
                    for k in range(KD):
                        if j == 0 and g == 0 and k >= 5:
                            xle.wait(pe, i, k + 1)
                        pe.matmul(out, h_[:, g, k, :], xh[:, k, 0:width], start=(k == 0), stop=False)
                        pe.matmul(out, h_[:, g, k, :], xl[:, k, 0:width], start=False, stop=False)
                        ins = pe.matmul(out, l_[:, g, k, :], xh[:, k, 0:width], start=False, stop=(k == KD - 1))
                gu.done(ins)

            def down(i, half, s, ks=range(KD)):
                s0, m = SUBS[s]
                if ks[0] == 0:
                    pe.wait_ge(ob.sem, i * 6 + (3 * half + s + 1))
                out = B[4 + s][0:m, :]
                for k in ks:
                    if s == 0 and k % 4 == 0:
                        pe.wait_ge(lo.sem, i * 12 + (8 + 2 * half + k // 4 + 5))
                    if half == 0 and s == 0:
                        ale.wait(pe, i, k + 1)
                    q = (2 * half + k // 4) % 4
                    h_, l_ = (w[q][:, :].rearrange("p (k c) -> p k c", k=4) for w in (wh, wl))
                    pe.matmul(out, ah[:, k, s0:s0 + m], h_[:, k % 4, :], start=(k == 0), stop=False)
                    pe.matmul(out, ah[:, k, s0:s0 + m], l_[:, k % 4, :], start=False, stop=False)
                    ins = pe.matmul(out, al[:, k, s0:s0 + m], h_[:, k % 4, :], start=False, stop=(k == KD - 1))
                if ks[-1] == KD - 1:
                    dn.done(ins)

            def no_down(i, half, s):
                pe.wait_ge(ob.sem, i * 6 + (3 * half + s + 1))
                dn.done(pe.transpose(B[4 + s][:, 0:P], ident[:, :], ident[:, :]))

            def chunk(i, width):
                xle.wait(pe, i, 6)
                for j in range(8):
                    if j == 1:
                        xle.wait(pe, i)
                    gate_up(i, j, width)
                last = down if width > SUBS[2][0] else no_down
                for ks in (range(5), range(5, KD)):
                    for s in range(2):
                        down(i, 0, s, ks)
                last(i, 0, 2)
                u1.wait(pe, i)
                pe.wait_ge(x_in, i * 48 + 96)
                for k in range(4):
                    turn_x(i + 1, k)
                down(i, 1, 0)
                for k in range(4, 8):
                    xle.wait(pe, i + 1, k - 3)
                    turn_x(i + 1, k)
                down(i, 1, 1)
                last(i, 1, 2)

            pe.wait_ge(ld, 32)
            for q in range(4):
                pe.transpose(B[6][:, q * P:(q + 1) * P], ident[:, :], ident[:, :])
            for q in range(2):
                for jj in range(8):
                    ins = pe.transpose(B[4 + q][:, jj * NE:(jj + 1) * NE],
                                       bgu_rows[:, (8 * q + jj) * P:(8 * q + jj + 1) * P], ident[0:NE, 0:NE])
                bturn.done(ins)
            pe.wait_ge(x_in, 48)
            for k in range(KD):
                if k >= 4:
                    xle.wait(pe, 0, k - 3)
                turn_x(0, k)
            bkept.wait(pe, 0, 2)
            n = n_chunks(pe)
            with pe.Fori(0, n) as i:
                size = pe.value_load(tab[0:1, bass.ds(i + SIZES, 1)], min_val=0, max_val=CHUNK)

                def narrowest(widths):
                    if len(widths) == 1:
                        chunk(i, widths[0])
                        return
                    with pe.If(size < widths[0] + 1):
                        chunk(i, widths[0])
                    with pe.Else():
                        narrowest(widths[1:])
                narrowest(WIDTHS)

        @block.scalar
        def _(act):
            def w_hi(i, q):
                if 4 <= q < 12:
                    gu.wait(act, i, q - 3)
                act.wait_ge(raw_in[q // 2 % 2], i * 96 + 32 * (q // 4 + 1))
                hi.done(act.activation(part(wh, q), raw_part(q), ACT.Copy))

            def x_hi(i, k):
                trx.wait(act, i, k + 1)
                xhe.done(act.activation(xh[:, k, :], B[k % 4][:, 0:CHUNK], ACT.Copy))

            def sigmoid(i, j):
                g1.wait(act, i, j + 1)
                if j == 0:
                    ob.wait(act, i, 3)
                else:
                    ac.wait(act, i, j)
                sgm.done(act.activation(sg_[:, :], g_[:, :], ACT.Sigmoid, scale=ALPHA))

            def a_hi(i, j):
                ac.wait(act, i, j + 1)
                ahe.done(act.activation(ah[:, j, :], a_[j % 2][:, :], ACT.Copy))

            def scale(i, half, s):
                s0, m = SUBS[s]
                ob.wait(act, i, 3 * half + s + 4)
                v = osb[0:m, s, half * 512:(half + 1) * 512]
                osc.done(act.activation(v, v, ACT.Copy, scale=mcur[0:m, s, 1:2].bitcast(F32)))

            for q in range(4):
                w_hi(0, q)
            for k in range(KD):
                x_hi(0, k)
            mc0.wait(act, 0, 4)
            osc.done(act.activation(carry[:, :], carry[:, :], ACT.Copy))
            osc.wait(act, 0, 1)
            n = n_chunks(act)
            with act.Fori(0, n) as i:
                for j in range(8):
                    sigmoid(i, j)
                    if j == 7:
                        a_hi(i, j)
                        w_hi(i, j + 4)
                    else:
                        w_hi(i, j + 4)
                        a_hi(i, j)
                for s in range(3):
                    scale(i, 0, s)
                for k in range(4):
                    x_hi(i + 1, k)
                dn.wait(act, i, 3)
                w_hi(i + 1, 0)
                w_hi(i + 1, 1)
                scale(i, 1, 0)
                for k in range(4, 8):
                    x_hi(i + 1, k)
                scale(i, 1, 1)
                scale(i, 1, 2)
                dn.wait(act, i, 6)
                w_hi(i + 1, 2)
                w_hi(i + 1, 3)

        @block.vector
        def _(dve):
            def w_lo(i, q):
                hi.wait(dve, i, q + 1)
                lo.done(dve.tensor_tensor(part(wl, q), raw_part(q), part(wh, q).bitcast(F32), ALU.subtract))

            def x_lo(i, k):
                xhe.wait(dve, i, k + 1)
                xle.done(dve.tensor_tensor(xl[:, k, :], B[k % 4][:, 0:CHUNK], xh[:, k, :].bitcast(F32), ALU.subtract))

            def clamp(i, j):
                G, U = B[2 * (j % 2)][:, 0:CHUNK], B[2 * (j % 2) + 1][:, 0:CHUNK]
                gu.wait(dve, i, j + 1)
                g1.done(dve.tensor_scalar(g_[:, :], G, bcur[:, j:j + 1], LIMIT, ALU.add, ALU.min))
                u1.done(dve.tensor_scalar(u_[:, :], U, bcur[:, KD + j:KD + j + 1], LIMIT, ALU.add, ALU.min))
                u1.wait(dve, i, j + 1)
                u1b.done(dve.tensor_scalar(u2[:, :], u_[:, :], -LIMIT, 1.0, ALU.max, ALU.add))
                g1.wait(dve, i, j + 1)
                u1b.wait(dve, i, j + 1)
                gm.done(dve.tensor_tensor(gu_[:, :], g_[:, :], u2[:, :], ALU.mult))

            def gated(i, j):
                gm.wait(dve, i, j + 1)
                sgm.wait(dve, i, j + 1)
                if j >= 2:
                    ale.wait(dve, i, j - 1)
                ac.done(dve.tensor_tensor(a_[j % 2][:, :], gu_[:, :], sg_[:, :], ALU.mult))

            def out_bias(i, half, s):
                s0, m = SUBS[s]
                c = slice(half * 512, (half + 1) * 512)
                dn.wait(dve, i, 3 * half + s + 1)
                if half == 0 and s == 0:
                    dve.wait_ge(bd_in, i * 16 + 16)
                    dve.wait_ge(sc, i * 48 + 48)
                ob.done(dve.tensor_tensor(osb[0:m, s, c], B[4 + s][0:m, :], bd[0:m, c], ALU.add))

            def take_slots(i):
                dve.wait_ge(meta_in, i * 48 + 48)
                dve.wait_ge(x_in, i * 48 + 48)
                dve.wait_ge(sc, i * 48 + 48)
                mc.done(dve.tensor_copy(mcur[:, 0:2, :], mnx[:, 0:2, :]))
                mc.done(dve.tensor_copy(mcur[0:64, 2, :], mnx[0:64, 2, :]))

            for q in range(4):
                lo.done(dve.memset(u2[:, q:q + 1], 0.0))
            for q in range(4, 7):
                ob.done(dve.memset(u2[:, q:q + 1], 0.0))
            lo.wait(dve, 0, 4)
            for q in range(2):
                bturn.wait(dve, 0, q + 1)
                bkept.done(dve.tensor_copy(bgu[:, 8 * q:8 * q + 8, :],
                                           B[4 + q][:, 0:8 * NE].rearrange("p (j e) -> p j e", j=8)))
            bkept.wait(dve, 0, 2)
            ob.wait(dve, 0, 3)
            for q in range(4):
                w_lo(0, q)
            for k in range(KD):
                x_lo(0, k)
            dve.wait_ge(meta_in, 48)
            mc0.done(dve.memset(osb[:, :, :], 0.0))
            mc0.done(dve.memset(carry[:, :], 0.0))
            mc0.done(dve.tensor_copy(mcur[:, 0:2, :], mnx[:, 0:2, :]))
            mc0.done(dve.tensor_copy(mcur[0:64, 2, :], mnx[0:64, 2, :]))
            mc0.wait(dve, 0, 4)
            n = n_chunks(dve)
            with dve.Fori(0, n) as i:
                e = expert_of(dve, i)
                bc.done(dve.tensor_copy(bcur[:, :], bgu[:, :, bass.ds(e, 1)].rearrange("p j o -> p (j o)")))
                bc.wait(dve, i)
                for j in range(8):
                    clamp(i, j)
                    if j == 7:
                        gated(i, j)
                        w_lo(i, j + 4)
                    else:
                        w_lo(i, j + 4)
                        gated(i, j)
                    if j == 3:
                        take_slots(i)
                for s in range(3):
                    out_bias(i, 0, s)
                for k in range(4):
                    x_lo(i + 1, k)
                w_lo(i + 1, 0)
                w_lo(i + 1, 1)
                out_bias(i, 1, 0)
                for k in range(4, 8):
                    x_lo(i + 1, k)
                out_bias(i, 1, 1)
                out_bias(i, 1, 2)
                w_lo(i + 1, 2)
                w_lo(i + 1, 3)

        @block.gpsimd
        def _(pool):
            def load_slots(i):
                r = pool.value_load(tab[0:1, bass.ds(i + NTAB, 1)], min_val=0, max_val=SLOTS - CHUNK)
                for s, (s0, m) in enumerate(SUBS):
                    pool.dma_start(mnx[0:m, s, :], X["slots"][bass.ds(r + s0, m), :]).then_inc(meta_in, 16)

            def gather():
                for s, (s0, m) in enumerate(SUBS):
                    pool.indirect_dma_start(
                        xg[0:m, s, :], None, X["h"][:, :],
                        bass.IndirectOffsetOnAxis(mnx[0:m, s, 0:1].bitcast(U32), 0)).then_inc(x_in, 16)

            def act_lo(i, j):
                ahe.wait(pool, i, j + 1)
                ale.done(pool.tensor_tensor(al[:, j, :], a_[j % 2][:, :], ah[:, j, :].bitcast(F32), ALU.subtract))

            def add_rows():
                for s, (s0, m) in enumerate(SUBS):
                    pool.indirect_dma_start(
                        X["y"][:, :], bass.IndirectOffsetOnAxis(mcur[0:m, s, 0:1].bitcast(U32), 0),
                        osb[0:m, s, :], None, compute_op=ALU.add).then_inc(sc, 16)

            load_slots(0)
            pool.wait_ge(meta_in, 48)
            gather()
            mc0.wait(pool, 0, 4)
            n = n_chunks(pool)
            with pool.Fori(0, n) as i:
                osc.wait(pool, i, 1)
                act_lo(i, 0)
                add_rows()
                act_lo(i, 1)
                act_lo(i, 2)
                act_lo(i, 3)
                mc.wait(pool, i)
                act_lo(i, 4)
                load_slots(i + 1)
                pool.wait_ge(meta_in, i * 48 + 96)
                trx.wait(pool, i)
                act_lo(i, 5)
                gather()
                act_lo(i, 6)
                act_lo(i, 7)
            osc.wait(pool, n, 1)
            mc.wait(pool, n - 1)
            last.done(pool.tensor_tensor(carry[:, :], carry[:, :], carry[:, :], ALU.add))
            add_rows()
            pool.wait_ge(sc, n * 48 + 48)
            pool.wait_ge(x_in, n * 48 + 48)

def final(nc, I, O, X):
    with ExitStack() as ctx:
        def sb(name, shape, dt=F32):
            return ctx.enter_context(nc.sbuf_tensor(name, shape, dt))

        def ev(name, per=1):
            return Event(ctx, nc, name, per)

        nf = sb("final_rows", [P, D])
        neghalf = sb("fneghalf", [P, 1])
        y = [sb(f"y{b}", [P, D]) for b in range(2)]
        yo = [sb(f"yo{b}", [P, D]) for b in range(2)]
        junk = sb("fjunk", [P, D])
        ss, ms, rs = ([sb(f"f{n}{b}", [P, 1]) for b in range(2)] for n in ("ss", "ms", "rs"))
        y_in = [ctx.enter_context(nc.semaphore(f"y_in{b}")) for b in range(2)]
        out_st = [ctx.enter_context(nc.semaphore(f"out_stored{b}")) for b in range(2)]
        nf_in = ctx.enter_context(nc.semaphore("final_norm_in"))
        ess, ems, ers, eo = (ev(n) for n in ("f_ss", "f_ms", "f_rs", "f_out"))
        neg = ev("f_neghalf_set")
        block = ctx.enter_context(nc.Block())
        ST = Tile(PT // 2, 0, "s")

        def every(eng, f):
            for t in range(2):
                f(Tile(0, t))
            with eng.Fori(1, PT // 2) as i:
                for t in range(2):
                    f(Tile(i, t))
            f(ST)

        @block.sync
        def _(sp):
            sp.dma_start(nf[:, :], I["final_norm"].partition_broadcast(P)).then_inc(nf_in, 16)

            def load(T):
                eo.wait(sp, T.t - 2)
                src = X["y"][SEQ:TOK, :] if T.kind == "s" else X["y"][bass.ds(T.t * P, P), :]
                sp.dma_start(y[T.par][0:T.n, :], src).then_inc(y_in[T.par], 16)
            every(sp, load)

        @block.scalar
        def _(act):
            def square(T):
                act.wait_ge(y_in[T.par], T.pair * 16 + 16)
                ems.wait(act, T.t - 2)
                ess.wait(act, T.t - 1)
                ess.done(act.activation(junk[0:T.n, :], y[T.par][0:T.n, :], ACT.Square, accum_out=ss[T.par][0:T.n, :]))
                eo.wait(act, T.t - 1)
                if not (T.static and T.t == 0):
                    store(T.t - 1, 1 - T.par, P)

            def store(t, par, n):
                if n == P:
                    dst = O["y_p"][0][bass.ds(t * P, P), :]
                else:
                    dst = O["y_s"].rearrange("b l d -> (b l) d")
                act.dma_start(dst, yo[par][0:n, :]).then_inc(out_st[par], 16)
            every(act, square)
            eo.wait(act, PT)
            store(PT, 0, NS)
            act.wait_ge(out_st[0], 16 * (PT // 2 + 1))
            act.wait_ge(out_st[1], 16 * (PT // 2))

        @block.gpsimd
        def _(pool):
            neg.done(pool.memset(neghalf[:, :], -0.5))
            neg.wait(pool, 0)

            def root(T):
                ems.wait(pool, T.t)
                eo.wait(pool, T.t - 2)
                ers.done(pool.tensor_tensor(rs[T.par][0:T.n, :], ms[T.par][0:T.n, :], neghalf[0:T.n, :], ALU.pow))
            every(pool, root)

        @block.vector
        def _(dve):
            dve.wait_ge(nf_in, 16)

            def norm(T):
                ess.wait(dve, T.t)
                ers.wait(dve, T.t - 2)
                ems.done(dve.tensor_scalar(ms[T.par][0:T.n, :], ss[T.par][0:T.n, :], 1.0 / D, EPS, ALU.mult, ALU.add))
                ers.wait(dve, T.t)
                dve.wait_ge(y_in[T.par], T.pair * 16 + 16)
                if not (T.static and T.pair == 0):
                    dve.wait_ge(out_st[T.par], T.pair * 16)
                eo.done(dve.scalar_tensor_tensor(yo[T.par][0:T.n, :], y[T.par][0:T.n, :], rs[T.par][0:T.n, 0:1],
                                                 nf[0:T.n, :], ALU.mult, ALU.mult))
            every(dve, norm)

def build(nc, I, O):
    X = {
        "slots": nc.dram_tensor("slot_rows", [SLOTS, 2], I32).ap(),
        "h": nc.dram_tensor("h_rows", [ROWS, D], F32).ap(),
        "y": nc.dram_tensor("y_rows", [ROWS, D], F32).ap(),
    }
    with nc.sbuf_tensor("chunk_table", [1, SIZES + NTAB], I32) as tab:
        with ExitStack() as ctx:
            ctab = {n: ctx.enter_context(nc.sbuf_tensor("t_" + n, [1, *s], F32)) for n, s in dict(
                cnt=[NE], nch=[NE], end=[NE], ex=[NTAB], bs=[NTAB], sz=[NTAB]).items()}
            mixer(nc, I, O, X, tab, ctab, None)
        experts(nc, I, X, tab)
    final(nc, I, O, X)

_INS = ["x_prompt", "x_sample", "state_gla", "state_pool", "norm1", "w_in", "w_gk2", "b_gk", "gla_norm", "w_pool",
        "pool_scale", "w_o", "norm2", "w_router", "b_router", "w_gate_up", "b_gate_up", "w_down", "b_down",
        "final_norm"]
_OUTS = {"y_p": (1, SEQ, D), "y_s": (NSEQ, LSEQ, D), "gla_p": (1, 1, H, DK, DV), "pool_p": (1, 1, BUF, PW),
         "gla_s": (1, NSEQ, H, DK, DV), "pool_s": (1, NSEQ, BUF, PW)}

def kernel(**inputs):
    import concourse.bacc as _bacc
    from concourse.bass_utils import run_bass_kernel_spmd as _run

    nc = _bacc.Bacc("TRN2", target_bir_lowering=False, num_devices=1)
    arrays = {f"in_{n}": np.ascontiguousarray(inputs[n]) for n in _INS}
    arrays.update({f"in_{n}": a for n, a in constants().items()})
    I = {n[3:]: nc.dram_tensor(n, a.shape, mybir.dt.from_np(a.dtype), kind="ExternalInput").ap()
         for n, a in arrays.items()}
    O = {n: nc.dram_tensor(f"out_{n}", s, F32, kind="ExternalOutput").ap() for n, s in _OUTS.items()}
    build(nc, I, O)
    r = _run(nc, [arrays], core_ids=[0])
    return tuple(r.results[0][f"out_{n}"] for n in _OUTS)
```

```python
from contextlib import ExitStack

import numpy as np

import concourse.bass as bass
from concourse import mybir

F32 = mybir.dt.float32
F32R = mybir.dt.float32r
I32 = mybir.dt.int32
U32 = mybir.dt.uint32
ALU = mybir.AluOpType
ACT = mybir.ActivationFunctionType
AX = mybir.AxisListType.X

P = 128
D = 1024
KD = D // P
SEQ = 2048
NSEQ, LSEQ = 8, 8
NS = NSEQ * LSEQ
PT = SEQ // P
NT = PT + 1
TOK = SEQ + NS
H, DK, DV = 4, 64, 128
QK = H * DK
VW = H * DV
RANK = 16
GATE_DIV = 16.0
C = 64
NC = P // C
PW = 512
NG = 4
BUF = 15
O_Q, O_K, O_V, O_OG, O_GLR, O_U = 0, QK, 2 * QK, 2 * QK + VW, 2 * QK + 2 * VW, 2 * QK + 2 * VW + RANK
IN_COLS = O_U + PW
NE = 32
TOPK = 4
FF = D
EPS = 1e-5
LIMIT = 7.0
ALPHA = 1.702
CHUNK = 320
SUBS = [(0, 128), (128, 128), (256, 64)]
TAIL, MT = SUBS[2]
assert 2 * MT == P
WIDTHS = [256, 272, 288, 304, CHUNK]
CPE = -(-TOK // CHUNK)
REGION = CPE * CHUNK
SLOTS = NE * REGION
MAXC = TOK * TOPK // CHUNK + NE
NTAB = 64
S_BANKS = (0, 1, 2, 3, 7)
SIZES, COUNT = 2 * NTAB, 3 * NTAB
ROWS = TOK + CHUNK
PIECE = 4096
assert MAXC + 1 <= NTAB
TAB_STEPS = CPE + 14

W_PARTS = {"glr_u": slice(O_GLR, IN_COLS), "qk": slice(O_Q, O_V), "v": slice(O_V, O_OG), "og": slice(O_OG, O_GLR)}
N_FIRST = 5
N_CONST = 9 + 2 + 3 + 1

def constants():
    p = np.arange(P)
    c = {}
    c["ident"] = np.eye(P, dtype=np.float32)
    c["before"] = (p[:, None] < p[None, :]).astype(np.float32)
    c["ones"] = np.ones((P, P), np.float32)
    c["scan_p"] = np.tile((np.arange(P) % C != 0).astype(np.float32), (P, 2))
    c["scan_s"] = np.tile((np.arange(NS) % LSEQ != 0).astype(np.float32), (P, 2))
    c["causal_p"] = np.tile((np.arange(C)[None, :] >= (p % C)[:, None]).astype(np.int32), (1, H))
    j, i = np.arange(NS)[:, None], np.arange(NS)[None, :]
    c["causal_s"] = np.tile(((i >= j) & (i // LSEQ == j // LSEQ)).astype(np.int32), (1, H))
    c["seq_of"] = (np.arange(NS)[:, None] // LSEQ == np.arange(NSEQ)[None, :]).astype(np.float32)
    c["expert_no"] = np.tile(np.arange(NE, dtype=np.float32), (P, TOPK))
    c["token_no"] = (p[:, None] + P * np.arange(NT)[None, :]).astype(np.int32)
    w = np.array([2, 4, 8, 16])
    first = 1.0 / np.minimum(w[:, None], np.arange(P)[None, :] + 1)
    c["inv_first"] = np.tile(first.astype(np.float32).reshape(1, -1), (P, 1))
    c["inv_rest"] = np.tile(np.repeat(1.0 / w, BUF).astype(np.float32)[None, :], (P, 1))
    slot = np.arange(SLOTS)
    c["empty_slots"] = np.stack([TOK + slot % CHUNK, 0 * slot], 1).astype(np.int32)
    c["chunk_no"] = np.arange(NTAB, dtype=np.float32)[:, None]
    c["zero_rows"] = np.zeros((CHUNK, D), np.float32)
    return c


class Event:

    def __init__(self, ctx, nc, name, per=1):
        self.sem = ctx.enter_context(nc.semaphore(name))
        self.per = per

    def done(self, ins):
        ins.then_inc(self.sem, 1)

    def wait(self, eng, t, k=None):
        if isinstance(t, int) and t < 0:
            return
        eng.wait_ge(self.sem, t * self.per + (self.per if k is None else k))

class Tile:

    def __init__(self, pair, par, kind="p"):
        self.t = pair * 2 + par
        self.pair, self.par, self.kind = pair, par, kind
        self.n = P if kind == "p" else NS
        self.static = isinstance(self.t, int)

    def later(self, k):
        par = (self.par + k) % 2
        pair = self.pair + (self.par + k - par) // 2
        if self.static and not 0 <= pair * 2 + par < NT:
            return None
        return Tile(pair, par, "s" if self.static and pair * 2 + par == PT else "p")


def in_order(eng, steps):
    for t in range(2):
        steps(Tile(0, t))
    with eng.Fori(1, PT // 2 - 1) as i:
        for t in range(2):
            steps(Tile(i, t))
    for t in range(2):
        steps(Tile(PT // 2 - 1, t))


def mixer(nc, I, O, X, tab):
    with ExitStack() as ctx:
        def sb(name, shape, dt=F32):
            return ctx.enter_context(nc.sbuf_tensor(name, shape, dt))

        def sem(name):
            return ctx.enter_context(nc.semaphore(name))

        def ev(name, per=1):
            return Event(ctx, nc, name, per)

        bank = [ctx.enter_context(nc.psum_tensor(f"bank{b}", [P, 512], F32)) for b in range(8)]
        w_in = sb("w_in_sb", [P, KD, IN_COLS])
        w_o = sb("w_o_sb", [P, KD, D])
        w_r = sb("w_r_sb", [P, KD, NE])
        w_gk = sb("w_gk_sb", [RANK, QK])
        w_pool = sb("w_pool_sb", [P, NG, P])
        b_gk = sb("b_gk_sb", [P, 2])
        glan = sb("glan_sb", [P, 1])
        n1 = sb("norm1_rows", [P, D])
        n2 = sb("norm2_rows", [P, D])
        b_r = sb("b_r_rows", [P, NE])
        ident = sb("ident", [P, P])
        before = sb("before", [P, P])
        ones = sb("ones", [P, P])
        scan_p = sb("scan_p", [P, 2 * P])
        scan_s = sb("scan_s", [P, 2 * NS])
        causal_p = sb("causal_p", [P, H * C], I32)
        causal_s = sb("causal_s", [NS, H * NS], I32)
        seq_of = sb("seq_of", [NS, NSEQ])
        expert_no = sb("expert_no", [P, TOPK * NE])
        token_no = sb("token_no", [P, NT], I32)
        inv = sb("inv_count", [P, NG, P])
        inv_rest = sb("inv_rest", [P, NG * BUF])
        ss1, ms1, rs1 = sb("ss1", [P, 1]), sb("ms1", [P, 1]), sb("rs1", [P, 1])
        ss2, ms2, rs2 = sb("ss2", [P, 1]), sb("ms2", [P, 1]), sb("rs2", [P, 1])
        neghalf = sb("neghalf", [P, 4])
        x = [sb(f"x{b}", [P, D]) for b in range(2)]
        xr = sb("x_residual", [P, D])
        xT = sb("xT", [P, KD, P])
        qks = sb("qks", [P, 4, P])
        ux = [sb(f"ux{b}", [P, NG, BUF + P]) for b in range(2)]
        uxs = sb("uxs", [P, NG, NSEQ, BUF + LSEQ])
        uc = sb("uc", [P, NG, NS])
        glrs = sb("glrs", [RANK, P])
        zz, az, G, Dm = (sb(n, [P, 2 * P]) for n in ("zz", "az", "G", "Dm"))
        e1 = l1 = az
        gk = zz
        eq, ek = sb("eq", [P, 2 * P]), sb("ek", [P, 2 * P])
        lr = sb("lr", [P, 4])
        esm = [sb(f"esm{b}", [P, 3, 4]) for b in range(2)]
        els = sb("els", [P, 2 * NSEQ])
        qdz = [sb(f"qdz{b}", [P, H, P]) for b in range(2)]
        kd = [sb(f"kd{b}", [P, 2, P]) for b in range(2)]
        vs = [sb(f"vs{b}", [P, VW]) for b in range(2)]
        eog = sb("eog", [P, VW])
        dog = eog
        sg = [sb(f"sg{b}", [P, VW]) for b in range(2)]
        pscale = sg[0]
        pa, pb = sb("pa", [P, NG, 8 * 23]), sb("pb", [P, NG, 8 * 23])
        dT = [sb(f"dT{b}", [P, NG, P]) for b in range(2)]
        ATs = sb("ATs", [P, H, P])
        kdTz = sb("kdTz", [P, NC, 2 * P])
        S, Sm, Pt = sb("S", [P, 2, DV]), sb("Sm", [P, 2, DV]), sb("Pt", [P, 2, DV])
        Sp = [sb(f"Sp{b}", [P, 2, DV]) for b in range(2)]
        os_, osq = sb("os", [P, VW]), sb("osq", [P, VW])
        so, mso, rso = sb("so", [P, H]), sb("mso", [P, H]), sb("rso", [P, H])
        cat = sb("cat", [P, KD, P])
        h = sb("h", [P, D])
        hT = sb("hT", [P, KD, P])
        lg = sb("lg", [P, NE])
        top = sb("top", [P, 8])
        idx = sb("idx", [P, 8], U32)
        idf = sb("idf", [P, TOPK])
        ng = sb("ng", [P, 1])
        e4, sum4, rs4 = sb("e4", [P, TOPK]), sb("sum4", [P, 1]), sb("rs4", [P, 1])
        oh, ohr = sb("oh", [P, TOPK, NE]), sb("ohr", [P, TOPK, NE])
        sel, selsum = sb("sel", [P, NE]), sb("selsum", [P, NE])
        r4, slotf = sb("r4", [P, TOPK]), sb("slotf", [P, TOPK])
        slot = [sb(f"slot{b}", [P, TOPK], U32) for b in range(2)]
        meta = [sb(f"meta{b}", [P, TOPK, 2], I32) for b in range(2)]
        Q8 = w_in[:, 0, 0:2048].rearrange("p (a b n) -> p a b n", a=H, b=NSEQ)
        kdT8 = w_in[0:NS, 1, 0:2048].rearrange("p (b n) -> p b n", b=NSEQ)
        cnt, nch, end, ge, gen = (w_in[0:NTAB, 2, i * NE:(i + 1) * NE] for i in range(5))
        ex, bs, sz, cn = (w_in[0:NTAB, 3, i:i + 1] for i in range(4))
        S0 = w_in[:, 5, 0:2048].rearrange("p (b a v) -> p b a v", b=NSEQ, a=2)
        pool_old = sb("pool_old", [NSEQ * BUF, PW])
        last_rows = sg[1][0:BUF, :]
        os_new = vs[1][0:NS, :]

        w_sem = {part: sem(f"w_{part}_loaded") for part in [*W_PARTS, "pool"]}
        wo_sem, c_sem, first_sem = sem("wo_loaded"), sem("consts_loaded"), sem("first_consts_loaded")
        init_sem = sem("dram_init")
        x_in = [sem("x_in0"), sem("x_in1")]
        xr_in = sem("x_residual_in")
        y_st, h_st = [sem("y_stored0")], [sem("h_stored0")]
        slot_st = [sem("slots_scattered0"), sem("slots_scattered1")]
        old_st = sem("states_stored")
        s0_in = sem("sampled_states_loaded")
        no_sem = sem("chunk_numbers_loaded")
        memo = ev("cleared")
        E = {n: ev(n, per) for n, per in dict(
            ss1=1, ms1=1, rs1=1, xn=1, trA=1, trB=1, xTe=2, glr=1, qk=1, u=1, z=1, v=1, og=1,
            qks=1, uxe=1, glrs=1, vse=1, eog=1, e1=1, l1=1, zz=2, az=1, gk=1, G=1, Dm=1, lr=1,
            eqk=2, esm=3, dog=1, rog=1, sg=1, qdz=2, kd=1, hist=1, pool=5, mean=2, dT=1,
            kdT=1, ATs=2, kdTz=2, Sp=2, Pc=2, Pt=4, Sm=2, S=2, zp=1, zpe=1, o=1, os=1, osq=1,
            so=1, mso=1, rso=1, on1=1, on=1, oT=1, oTe=1, mix=2, x1=2, ss2=1, ms2=1, rs2=1, h=1,
            hA=1, hB=1, hTe=2, lgp=1, lg=1, top=1, idx=1, idf=1, ng=1, e4=1, rs4=1, gate=1, oh=1,
            sel=1, rank=1, ohr=1, r4=1, slotf=1, slot=1, tokid=1, selsum=1).items()}
        s_misc = ev("sample_steps")
        s_misc2 = ev("sample_inputs_kept")
        s_S8, s_P8, s_T8 = ev("s_S8"), ev("s_P8"), ev("s_T8")
        s_tab = ev("table_steps")
        s_cnt = ev("counted")
        rows_turned, rows_kept = ev("rows_turned"), ev("rows_kept")
        OLD, LAST, NEW, TABLE = range(4)

        block = ctx.enter_context(nc.Block())
        xp, xs = I["x_prompt"][0], I["x_sample"].rearrange("b l d -> (b l) d")

        def rows_of(ap, T):
            return ap[SEQ:TOK, :] if T.kind == "s" else ap[bass.ds(T.t * P, P), :]

        def wv(E_, eng, T, k=None, back=0):
            E[E_].wait(eng, T.t - back, k)

        def waitx(eng, T):
            eng.wait_ge(x_in[T.par], T.pair * 16 + 16)

        @block.sync
        def _(sp):
            def c_load(dst, src):
                sp.dma_start(dst, src).then_inc(c_sem, 16)

            def load_x(T):
                wv("trB", sp, T, back=2)
                src = xs if T.kind == "s" else xp[bass.ds(T.t * P, P), :]
                sp.dma_start(x[T.par][0:T.n, :], src).then_inc(x_in[T.par], 16)

            def load_residual(T):
                src = xs if T.kind == "s" else xp[bass.ds(T.t * P, P), :]
                sp.dma_start(xr[0:T.n, :], src).then_inc(xr_in, 16)

            def store(T):
                wv("x1", sp, T)
                sp.dma_start(rows_of(X["y"], T), xr[0:T.n, :]).then_inc(y_st[0], 16)
                wv("h", sp, T)
                sp.dma_start(rows_of(X["h"], T), h[0:T.n, :]).then_inc(h_st[0], 16)

            def tile(T):
                if T.later(2):
                    load_x(T.later(2))
                store(T)
                sp.wait_ge(y_st[0], T.t * 16 + 16)
                load_residual(T.later(1))

            load_x(Tile(0, 0))
            for dst, src in ((n1, I["norm1"].partition_broadcast(P)), (ident, I["ident"]), (w_gk, I["w_gk2"][0]),
                             (b_gk, I["b_gk"][0].rearrange("(a p) -> p a", p=P)), (scan_p, I["scan_p"])):
                with nc.allow_non_contiguous_dma(reason="a few hundred bias elements"):
                    sp.dma_start(dst[:, :], src).then_inc(first_sem, 16)
            win = I["w_in"][0].rearrange("(k p) n -> p k n", p=P)
            for part, c in W_PARTS.items():
                sp.dma_start(w_in[:, :, c], win[:, :, c]).then_inc(w_sem[part], 16)
                if part == "glr_u":
                    load_x(Tile(0, 1))
            load_residual(Tile(0, 0))
            for dst, src in ((glan, I["gla_norm"].rearrange("a p -> p a")),
                             (n2, I["norm2"].partition_broadcast(P)),
                             (b_r, I["b_router"].partition_broadcast(P)),
                             (before, I["before"]), (ones, I["ones"]),
                             (causal_p, I["causal_p"]), (expert_no, I["expert_no"]),
                             (token_no, I["token_no"]), (inv_rest, I["inv_rest"])):
                with nc.allow_non_contiguous_dma(reason="a few hundred bias elements"):
                    c_load(dst[:, :], src)
            c_load(inv[:, :, :].rearrange("p g t -> p (g t)"), I["inv_first"])
            c_load(pscale[:, :], I["pool_scale"].partition_broadcast(P))
            for dst, src in ((scan_s, I["scan_s"]), (causal_s, I["causal_s"]), (seq_of, I["seq_of"])):
                c_load(dst[:, :], src)
            c_load(pool_old[:, :], I["state_pool"][0].rearrange("b r c -> (b r) c"))
            sp.dma_start(w_pool[:, :, :], I["w_pool"][0].rearrange("g c e -> c g e")).then_inc(w_sem["pool"], 16)
            wo = I["w_o"][0].rearrange("(k p) n -> p k n", p=P)
            for k0 in range(0, KD, 4):
                sp.dma_start(w_o[:, k0:k0 + 4, :], wo[:, k0:k0 + 4, :]).then_inc(wo_sem, 16)
            sp.dma_start(w_r[:, :, :], I["w_router"][0].rearrange("(k p) n -> p k n", p=P)).then_inc(wo_sem, 16)
            sp.dma_start(X["slots"][:, :], I["empty_slots"]).then_inc(init_sem, 16)
            sp.dma_start(X["h"][TOK:ROWS, :], I["zero_rows"]).then_inc(init_sem, 16)
            sp.dma_start(X["y"][TOK:ROWS, :], I["zero_rows"]).then_inc(init_sem, 16)
            sp.dma_start(O["pool_s"][0, :, 0:BUF - LSEQ, :],
                         I["state_pool"][0, :, LSEQ:BUF, :]).then_inc(old_st, 16)
            in_order(sp, tile)
            E["S"].wait(sp, PT - 1)
            for c in range(2):
                sp.dma_start(O["gla_p"][0, 0].rearrange("(a c) k v -> c k a v", c=2)[c],
                             S[c * DK:(c + 1) * DK, :, :]).then_inc(old_st, 16)
            rows_kept.wait(sp, LAST)
            sp.dma_start(O["pool_p"][0, 0], last_rows).then_inc(old_st, 16)
            E["og"].wait(sp, PT)
            sg_in = I["state_gla"][0].rearrange("b (a c) k v -> c k b a v", c=2)
            for c in range(2):
                for a in range(2):
                    sp.dma_start(S0[c * DK:(c + 1) * DK, :, a, :], sg_in[c, :, :, a, :]).then_inc(s0_in, 16)
            with nc.allow_non_contiguous_dma(reason="64 numbers"):
                sp.dma_start(cn, I["chunk_no"]).then_inc(no_sem, 16)
            store(Tile(PT // 2, 0, "s"))
            rows_kept.wait(sp, NEW)
            for b in range(NSEQ):
                sp.dma_start(O["pool_s"][0, b, BUF - LSEQ:BUF, :],
                             os_new[b * LSEQ:(b + 1) * LSEQ, :]).then_inc(old_st, 16)
            s_S8.wait(sp, 0, NSEQ)
            sg_out = O["gla_s"][0].rearrange("b (a c) k v -> c k b a v", c=2)
            for c in range(2):
                for a in range(2):
                    sp.dma_start(sg_out[c, :, :, a, :], S0[c * DK:(c + 1) * DK, :, a, :]).then_inc(old_st, 16)
            sp.wait_ge(old_st, 16 * (1 + 2 + 1 + NSEQ + 4))
            sp.wait_ge(y_st[0], 16 * NT)
            sp.wait_ge(h_st[0], 16 * NT)
            sp.wait_ge(init_sem, 48)
            sp.wait_ge(slot_st[0], 64 * ((NT + 1) // 2))
            sp.wait_ge(slot_st[1], 64 * (NT // 2))

        @block.tensor
        def _(pe):
            B = bank

            def turn(src, b, ks, n, e):
                for q, k in enumerate(ks):
                    ins = pe.transpose(B[b][:, q * n:(q + 1) * n], src[0:n, k * P:(k + 1) * P], ident[0:n, 0:n])
                E[e].done(ins)

            def proj_T(b, cols, n, e, m=P):
                for q, c0 in enumerate(cols):
                    for k in range(KD):
                        ins = pe.matmul(B[b][0:m, q * n:(q + 1) * n], w_in[:, k, c0:c0 + m], xT[:, k, 0:n],
                                        start=(k == 0), stop=(k == KD - 1))
                E[e].done(ins)

            def proj(b, c0, n, e, ks=range(KD)):
                for k in ks:
                    ins = pe.matmul(B[b][0:n, :], xT[:, k, 0:n], w_in[:, k, c0:c0 + 512],
                                    start=(k == 0), stop=(k == KD - 1))
                if k == KD - 1:
                    E[e].done(ins)

            def f_turnA(T):
                wv("xn", pe, T)
                wv("vse", pe, T, back=1)
                turn(x[T.par], 0, range(4), T.n, "trA")

            def f_turnB(T):
                wv("zz", pe, T, back=1)
                turn(x[T.par], 7, range(4, 8), T.n, "trB")

            def f_glr(T):
                wv("xTe", pe, T)
                proj_T(7, [O_GLR], T.n, "glr", RANK)

            def f_qk(T):
                wv("qks", pe, T, back=1)
                proj_T(2, [O_Q, O_Q + P, O_K, O_K + P], T.n, "qk")

            def f_z(T):
                wv("glrs", pe, T)
                for a in range(2):
                    ins = pe.matmul(B[7][:, a * T.n:(a + 1) * T.n], w_gk[:, a * P:(a + 1) * P],
                                    glrs[:, 0:T.n], start=True, stop=True)
                E["z"].done(ins)

            def f_u(T):
                wv("uxe", pe, T, back=1)
                proj_T(3, [O_U + g * P for g in range(NG)], T.n, "u")

            def f_v(T, ks=range(KD)):
                proj(0, O_V, T.n, "v", ks)

            def f_og(T, ks):
                if ks[0] == 0:
                    wv("sg", pe, T, back=1)
                proj(1, O_OG, T.n, "og", ks)

            def m_AT(T):
                wv("qdz", pe, T)
                wv("kd", pe, T)
                wv("hTe", pe, T, back=1)
                for a in range(H):
                    for c in range(NC):
                        ins = pe.matmul(B[4][c * C:(c + 1) * C, a * C:(a + 1) * C],
                                        kd[T.par][:, a // 2, c * C:(c + 1) * C],
                                        qdz[T.par][:, a, c * C:(c + 1) * C], start=True, stop=True,
                                        skip_group_check=True)
                for a in range(2):
                    ins = pe.transpose(B[4][:, 256 + a * P:256 + (a + 1) * P], kd[T.par][:, a, :], ident[:, :])
                E["kdT"].done(ins)

            def m_o0(T):
                wv("ATs", pe, T)
                wv("vse", pe, T)
                wv("lg", pe, T, back=1)
                for a in range(H):
                    pe.matmul(B[5][:, a * DV:(a + 1) * DV], ATs[:, a, :], vs[T.par][:, a * DV:(a + 1) * DV],
                              start=(a == 0), stop=False, skip_group_check=True)
                wv("Sp", pe, T, 1)
                m_inter(T, 0)

            def m_inter(T, c):
                for a in range(H):
                    ins = pe.matmul(B[5][c * C:(c + 1) * C, a * DV:(a + 1) * DV],
                                    qdz[T.par][:, a, c * C:(c + 1) * C], Sp[c][:, a // 2, :],
                                    start=False, stop=(a == H - 1), skip_group_check=True)
                if c == NC - 1:
                    E["o"].done(ins)

            def m_P(T, c):
                wv("kdTz", pe, T)
                if c == 0:
                    wv("ohr", pe, T, back=1)
                else:
                    wv("Pt", pe, T, 2)
                for a in range(2):
                    ins = pe.matmul(B[6][:, a * 256:(a + 1) * 256], kdTz[:, c, a * P:(a + 1) * P],
                                    vs[T.par][:, a * 256:(a + 1) * 256], start=True, stop=True)
                E["Pc"].done(ins)

            def m_pool(T):
                wv("dT", pe, T)
                wv("kdTz", pe, T)
                for g in range(NG):
                    ins = pe.matmul(B[4][:, g * T.n:(g + 1) * T.n], w_pool[:, g, :], dT[T.par][:, g, 0:T.n],
                                    start=True, stop=True)
                E["zp"].done(ins)

            def m_oT(T):
                wv("on", pe, T)
                if T.kind == "p":
                    wv("Pt", pe, T)
                for a in range(H):
                    ins = pe.transpose(B[6][:, a * T.n:(a + 1) * T.n], osq[0:T.n, a * P:(a + 1) * P],
                                       ident[0:T.n, 0:T.n])
                E["oT"].done(ins)

            def b_mix(T):
                wv("zpe", pe, T)
                wv("os", pe, T)
                for half in range(2):
                    for q, k in enumerate([4, 5, 6, 7, 0, 1, 2, 3]):
                        if half == 0 and k == 0:
                            wv("oTe", pe, T)
                        ins = pe.matmul(B[4 + half][0:T.n, :], cat[:, k, 0:T.n],
                                        w_o[:, k, half * 512:(half + 1) * 512],
                                        start=(q == 0), stop=(q == KD - 1))
                    E["mix"].done(ins)

            def b_hT(T):
                wv("h", pe, T)
                turn(h, 6, range(4), T.n, "hA")
                turn(h, 4, range(4, 8), T.n, "hB")

            def b_router(T):
                wv("hTe", pe, T)
                for k in range(KD):
                    ins = pe.matmul(B[5][0:T.n, 0:NE], hT[:, k, 0:T.n], w_r[:, k, :],
                                    start=(k == 0), stop=(k == KD - 1))
                E["lgp"].done(ins)

            def b_rank(T):
                wv("sel", pe, T)
                pe.matmul(B[6][0:T.n, 0:NE], before[0:T.n, 0:T.n], sel[0:T.n, :], start=True, stop=False)
                wv("selsum", pe, T, back=1)
                ins = pe.matmul(B[6][0:T.n, 0:NE], ones[:, 0:T.n], selsum[:, :], start=False, stop=True)
                E["rank"].done(ins)

            def tile(T):
                N, L = T.later(1), T.later(-1)
                f_turnA(N)
                m_AT(T)
                f_turnB(N)
                f_glr(N)
                f_qk(N)
                if L:
                    b_rank(L)
                m_o0(T)
                m_P(T, 0)
                m_pool(T)
                f_z(N)
                f_u(N)
                wv("Sp", pe, T, 2)
                m_inter(T, 1)
                m_P(T, 1)
                f_v(N, range(7))
                m_oT(T)
                b_mix(T)
                f_v(N, range(7, KD))
                f_og(N, range(4))
                b_hT(T)
                f_og(N, range(4, KD))
                b_router(T)

            pe.wait_ge(first_sem, 16 * N_FIRST)
            T = Tile(0, 0)
            f_turnA(T)
            f_turnB(T)
            pe.wait_ge(w_sem["glr_u"], 16)
            f_glr(T)
            f_u(T)
            f_z(T)
            pe.wait_ge(w_sem["qk"], 16)
            f_qk(T)
            pe.wait_ge(w_sem["v"], 16)
            f_v(T)
            pe.wait_ge(w_sem["og"], 16)
            f_og(T, range(KD))
            pe.wait_ge(c_sem, 16 * N_CONST)
            for g in range(NG):
                ins = pe.transpose(B[4][:, g * 120:(g + 1) * 120], pool_old[:, g * P:(g + 1) * P],
                                   ident[0:120, 0:120])
            rows_turned.done(ins)
            memo.wait(pe, 0, 8)
            rows_kept.wait(pe, OLD)
            pe.wait_ge(wo_sem, 16 * 3)
            in_order(pe, tile)
            b_rank(Tile(PT // 2 - 1, 1))
            E["hTe"].wait(pe, PT - 1)
            for g in range(NG):
                ins = pe.transpose(B[4][0:BUF, g * P:(g + 1) * P], ux[1][:, g, P:P + BUF], ident[:, :])
            rows_turned.done(ins)
            T = Tile(PT // 2, 0, "s")
            rows_kept.wait(pe, LAST)
            E["uxe"].wait(pe, PT)
            rows_kept.wait(pe, OLD)
            for g in range(NG):
                ins = pe.transpose(B[4][0:NS, g * P:(g + 1) * P], uc[:, g, :], ident[:, :])
            rows_turned.done(ins)
            wv("qdz", pe, T)
            wv("kd", pe, T)
            rows_kept.wait(pe, NEW)
            for a in range(H):
                ins = pe.matmul(B[4][0:NS, a * NS:(a + 1) * NS], kd[0][:, a // 2, 0:NS], qdz[0][:, a, 0:NS],
                                start=True, stop=True, skip_group_check=True)
            for a in range(2):
                ins = pe.transpose(B[4][0:NS, 256 + a * P:256 + (a + 1) * P], kd[0][:, a, 0:NS], ident[:, :])
            E["kdT"].done(ins)
            wv("ATs", pe, T)
            wv("vse", pe, T)
            wv("lg", pe, T, back=1)
            for a in range(H):
                pe.matmul(B[5][0:NS, a * DV:(a + 1) * DV], ATs[0:NS, a, 0:NS], vs[0][0:NS, a * DV:(a + 1) * DV],
                          start=(a == 0), stop=False, skip_group_check=True)
            pe.wait_ge(s0_in, 64)
            s_misc.wait(pe, 0, NSEQ)
            for b in range(NSEQ):
                for a in range(H):
                    ins = pe.matmul(B[5][0:NS, a * DV:(a + 1) * DV], Q8[:, a, b, :], S0[:, b, a // 2, :],
                                    start=False, stop=(b == NSEQ - 1), skip_group_check=True)
            E["o"].done(ins)
            wv("sg", pe, T)

            def update(bs):
                for b in bs:
                    s_T8.wait(pe, 0, b + 1)
                    if b >= len(S_BANKS):
                        s_S8.wait(pe, 0, b - len(S_BANKS) + 1)
                    for a in range(2):
                        ins = pe.matmul(B[S_BANKS[b % len(S_BANKS)]][:, a * 256:(a + 1) * 256],
                                        kdT8[:, b, a * P:(a + 1) * P], vs[0][0:NS, a * 256:(a + 1) * 256],
                                        start=True, stop=True)
                    s_P8.done(ins)

            update(range(len(S_BANKS)))
            s_T8.wait(pe, 0, NSEQ)
            wv("dT", pe, T)
            for g in range(NG):
                ins = pe.matmul(B[4][:, g * NS:(g + 1) * NS], w_pool[:, g, :], dT[0][:, g, 0:NS],
                                start=True, stop=True)
            E["zp"].done(ins)
            wv("ohr", pe, T, back=1)
            m_oT(T)
            b_mix(T)
            update(range(len(S_BANKS), NSEQ))
            b_hT(T)
            b_router(T)
            b_rank(T)
            E["selsum"].wait(pe, PT)
            E["ohr"].wait(pe, PT)
            s_cnt.done(pe.matmul(B[6][:, 0:NE], ones[:, :], selsum[:, :], start=True, stop=True))
            s_tab.wait(pe, 0, TAB_STEPS)
            for q, col in enumerate((ex, bs, sz)):
                ins = pe.matmul(B[6][0:1, q * NTAB:(q + 1) * NTAB], col, ident[0:NTAB, 0:NTAB], start=True, stop=True,
                                skip_group_check=True)
            rows_turned.done(ins)

        @block.scalar
        def _(act):
            B = bank

            def f_ss(T):
                waitx(act, T)
                wv("lgp", act, T, back=3)
                wv("hTe", act, T, back=3)
                wv("ss1", act, T, back=1)
                E["ss1"].done(act.activation(hT[:, :, :].rearrange("p k n -> p (k n)")[0:T.n, :], x[T.par][0:T.n, :], ACT.Square,
                                             accum_out=ss1[0:T.n, :]))

            def f_xT(T):
                for half, e in enumerate(("trA", "trB")):
                    wv(e, act, T)
                    if half == 0:
                        wv("og", act, T, back=1)
                    E["xTe"].done(act.activation(
                        xT[:, 4 * half:4 * half + 4, 0:T.n],
                        B[(0, 7)[half]][:, 0:4 * T.n].rearrange("p (k n) -> p k n", k=4), ACT.Copy))

            def f_glr(T):
                wv("glr", act, T)
                E["glrs"].done(act.activation(glrs[:, 0:T.n], B[7][0:RANK, 0:T.n], ACT.Copy))

            def f_qk(T):
                wv("qk", act, T)
                wv("kd", act, T, back=1)
                E["qks"].done(act.activation(qks[:, :, 0:T.n], B[2][:, 0:4 * T.n].rearrange(
                    "p (k n) -> p k n", k=4), ACT.Copy))

            def f_gate(T):
                wv("az", act, T)
                E["e1"].done(act.activation(e1[:, 0:2 * T.n], az[:, 0:2 * T.n], ACT.Exp, scale=-1.0))
                wv("e1", act, T)
                E["l1"].done(act.activation(l1[:, 0:2 * T.n], e1[:, 0:2 * T.n], ACT.Ln, bias=1.0))

            def f_u(T):
                wv("u", act, T)
                src = B[3][:, 0:4 * T.n]
                if T.kind == "p":
                    wv("dT", act, T, back=2)
                    wv("hist", act, T, back=1)
                    E["uxe"].done(act.activation(ux[T.par][:, :, BUF:], src.rearrange("p (g n) -> p g n", g=NG),
                                                 ACT.Copy))
                else:
                    s_misc2.done(act.activation(uxs[:, :, :, BUF:], src.rearrange(
                        "p (g s l) -> p g s l", g=NG, l=LSEQ), ACT.Copy))
                    E["uxe"].done(act.activation(uc[:, :, :], src.rearrange("p (g n) -> p g n", g=NG), ACT.Copy))

            def f_v(T):
                wv("v", act, T)
                wv("Pc", act, T, back=2)
                E["vse"].done(act.activation(vs[T.par][0:T.n, :], B[0][0:T.n, :], ACT.Copy))

            def f_og(T):
                wv("og", act, T)
                E["eog"].done(act.activation(eog[0:T.n, :], B[1][0:T.n, :], ACT.Exp, scale=-1.0))

            def f_decay(T):
                wv("Dm", act, T)
                wv("qdz", act, T, back=1)
                E["eqk"].done(act.activation(eq[:, 0:2 * T.n], Dm[:, 0:2 * T.n], ACT.Exp, scale=1 / GATE_DIV))
                wv("kd", act, T, back=1)
                E["eqk"].done(act.activation(ek[:, 0:2 * T.n], Dm[:, 0:2 * T.n], ACT.Exp, scale=-1 / GATE_DIV))

            def f_small(T):
                wv("Pt", act, T, back=2)
                Gc = G[:, :].rearrange("p (q c) -> p q c", c=C)
                E["esm"].done(act.activation(esm[T.par][:, 0, :], Gc[:, :, C // 2 - 1], ACT.Exp, scale=1 / GATE_DIV))
                E["esm"].done(act.activation(esm[T.par][:, 1, :], Gc[:, :, C - 1], ACT.Exp, scale=1 / GATE_DIV))
                wv("lr", act, T)
                E["esm"].done(act.activation(esm[T.par][:, 2, :], lr[:, :], ACT.Exp, scale=1 / GATE_DIV))

            def m_os(T):
                wv("o", act, T)
                wv("on", act, T, back=1)
                E["os"].done(act.activation(os_[0:T.n, :], B[5][0:T.n, :], ACT.Copy))

            def m_pool(T):
                wv("zp", act, T)
                wv("mix", act, T, back=1)
                E["zpe"].done(act.activation(cat[:, NG:, 0:T.n], B[4][:, 0:4 * T.n].rearrange(
                    "p (g n) -> p g n", g=NG), ACT.Copy))

            def m_oT(T):
                wv("oT", act, T)
                E["oTe"].done(act.activation(cat[:, 0:H, 0:T.n], B[6][:, 0:4 * T.n].rearrange(
                    "p (g n) -> p g n", g=H), ACT.Copy, scale=glan[:, 0:1]))

            def b_ss(T):
                wv("x1", act, T)
                wv("hB", act, T, back=1)
                if not (T.static and T.t == 0):
                    act.wait_ge(h_st[0], T.t * 16)
                E["ss2"].done(act.activation(h[0:T.n, :], xr[0:T.n, :], ACT.Square, accum_out=ss2[0:T.n, :]))

            def b_hT(T):
                squares(T)
                for half, e in enumerate(("hA", "hB")):
                    wv(e, act, T)
                    b = (6, 4)[half]
                    E["hTe"].done(act.activation(hT[:, 4 * half:4 * half + 4, 0:T.n],
                                                 B[b][:, 0:4 * T.n].rearrange("p (k n) -> p k n", k=4), ACT.Copy))

            def b_gates(T):
                wv("ng", act, T)
                E["e4"].done(act.activation(e4[0:T.n, :], top[0:T.n, 0:TOPK], ACT.Exp, bias=ng[0:T.n, 0:1],
                                            accum_out=sum4[0:T.n, :]))

            def squares(T):
                M = T.later(2)
                wv("ss1", act, M if M else Tile(PT // 2, 0, "s"))

            def tile(T):
                N, M = T.later(1), T.later(2)
                f_xT(N)
                if T.later(-1):
                    b_gates(T.later(-1))
                f_glr(N)
                f_qk(N)
                m_pool(T)
                f_gate(N)
                f_u(N)
                if N.kind == "p":
                    f_decay(N)
                    f_small(N)
                else:
                    s_decay(N)
                m_os(T)
                m_oT(T)
                if M:
                    f_ss(M)
                f_v(N)
                b_ss(T)
                b_hT(T)
                f_og(N)

            def s_decay(T):
                wv("G", act, T)
                wv("qdz", act, T, back=1)
                wv("kd", act, T, back=1)
                E["eqk"].done(act.activation(eq[:, 0:2 * NS], G[:, 0:2 * NS], ACT.Exp, scale=1 / GATE_DIV))
                E["eqk"].done(act.activation(ek[:, 0:2 * NS], G[:, 0:2 * NS], ACT.Exp, scale=-1 / GATE_DIV))
                E["esm"].done(act.activation(els[:, :], G[:, 0:2 * NS].rearrange("p (q l) -> p q l", l=LSEQ)[:, :, LSEQ - 1],
                                             ACT.Exp, scale=1 / GATE_DIV))

            T = Tile(0, 0)
            f_ss(T)
            f_xT(T)
            f_ss(Tile(0, 1))
            f_glr(T)
            f_u(T)
            f_gate(T)
            f_qk(T)
            f_decay(T)
            f_small(T)
            f_v(T)
            f_og(T)
            act.wait_ge(c_sem, 16 * N_CONST)
            rows_turned.wait(act, OLD)
            rows_kept.done(act.activation(uxs[:, :, :, 0:BUF], B[4][:, 0:480].rearrange(
                "p (g s r) -> p g s r", g=NG, s=NSEQ), ACT.Copy))
            in_order(act, tile)
            b_gates(Tile(PT // 2 - 1, 1))
            rows_turned.wait(act, LAST)
            E["on1"].wait(act, PT - 1)
            rows_kept.done(act.activation(last_rows.rearrange("r (g c) -> r g c", g=NG), B[4][0:BUF, :].rearrange("r (g c) -> r g c", g=NG),
                                      ACT.Copy))
            T = Tile(PT // 2, 0, "s")
            rows_turned.wait(act, NEW)
            rows_kept.done(act.activation(os_new, B[4][0:NS, :], ACT.Copy))
            m_os(T)
            m_pool(T)
            m_oT(T)
            b_ss(T)
            b_hT(T)
            b_gates(T)

        @block.vector
        def _(dve):
            B = bank

            def tt(e, out, a, b, op):
                E[e].done(dve.tensor_tensor(out, a, b, op))

            def f_ms(T):
                wv("ss1", dve, T)
                E["ms1"].done(dve.tensor_scalar(ms1[0:T.n, :], ss1[0:T.n, :], 1.0 / D, EPS, ALU.mult, ALU.add))

            def f_xn(T):
                wv("rs1", dve, T)
                wv("ss1", dve, T)
                E["xn"].done(dve.scalar_tensor_tensor(x[T.par][0:T.n, :], x[T.par][0:T.n, :], rs1[0:T.n, 0:1],
                                                      n1[0:T.n, :], ALU.mult, ALU.mult))

            def f_gate(T):
                n2_ = 2 * T.n
                wv("z", dve, T)
                for a in range(2):
                    E["zz"].done(dve.tensor_scalar(zz[:, a * T.n:(a + 1) * T.n], B[7][:, a * T.n:(a + 1) * T.n],
                                                   b_gk[:, a:a + 1], None, ALU.add))
                wv("zz", dve, T)
                E["az"].done(dve.scalar_tensor_tensor(az[:, 0:n2_], zz[:, 0:n2_], -1.0, zz[:, 0:n2_],
                                                      ALU.mult, ALU.max))
                wv("l1", dve, T)
                E["gk"].done(dve.scalar_tensor_tensor(gk[:, 0:n2_], zz[:, 0:n2_], 0.0, l1[:, 0:n2_],
                                                      ALU.min, ALU.subtract))
                wv("gk", dve, T)
                mask = scan_p if T.kind == "p" else scan_s
                wv("esm", dve, T, back=1)
                E["G"].done(dve.tensor_tensor_scan(G[:, 0:n2_], mask[:, 0:n2_], gk[:, 0:n2_], 0.0,
                                                   ALU.mult, ALU.add))
                wv("G", dve, T)
                if T.kind == "p":
                    Gc = G[:, :].rearrange("p (q c) -> p q c", c=C)
                    wv("eqk", dve, T, back=1)
                    tt("Dm", Dm[:, :].rearrange("p (q c) -> p q c", c=C), Gc,
                       Gc[:, :, C // 2 - 1:C // 2].to_broadcast([P, 4, C]), ALU.subtract)
                    tt("lr", lr[:, :], Gc[:, :, C - 1], Gc[:, :, C // 2 - 1], ALU.subtract)

            def f_og(T):
                wv("eog", dve, T)
                E["dog"].done(dve.tensor_scalar(dog[0:T.n, :], eog[0:T.n, :], 1.0, None, ALU.add))
                wv("dog", dve, T)
                E["rog"].done(dve.reciprocal(dog[0:T.n, :], dog[0:T.n, :]))
                wv("rog", dve, T)
                tt("sg", sg[T.par][0:T.n, :], B[1][0:T.n, :], dog[0:T.n, :], ALU.mult)

            def f_qd(T):
                n = T.n
                wv("qks", dve, T)
                wv("eqk", dve, T)
                wv("o", dve, T, back=2)
                eqv = eq[:, 0:2 * n].rearrange("p (a n) -> p a n", a=2)
                ekv = ek[:, 0:2 * n].rearrange("p (a n) -> p a n", a=2)
                for r in range(2):
                    s = slice(r * DK, (r + 1) * DK)
                    E["qdz"].done(dve.scalar_tensor_tensor(qdz[T.par][s, r::2, 0:n], qks[s, 0:2, 0:n], DK ** -0.5,
                                                           eqv[s], ALU.mult, ALU.mult))
                wv("kdT", dve, T, back=2)
                tt("kd", kd[T.par][:, :, 0:n], qks[:, 2:4, 0:n], ekv, ALU.mult)

            def m_AT(T):
                wv("kdT", dve, T)
                wv("o", dve, T, back=1)
                for c in range(NC):
                    s = slice(c * C, (c + 1) * C)
                    E["kdTz"].done(dve.tensor_copy(kdTz[s, c, :], B[4][s, 256:512]))
                for c in range(NC):
                    s = slice(c * C, (c + 1) * C)
                    E["ATs"].done(dve.copy_predicated(
                        ATs[s, :, s], causal_p[s, :].rearrange("p (a i) -> p a i", a=H),
                        B[4][s, 0:H * C].rearrange("p (a i) -> p a i", a=H)))

            def small(T, k, c, s=slice(0, P)):
                return esm[T.par][s, k, c::NC].unsqueeze(2).to_broadcast([s.stop - s.start, 2, DV])

            def m_Sp(T, c):
                if c == 0:
                    wv("esm", dve, T)
                    wv("S", dve, T, back=1)
                else:
                    wv("S", dve, T, 1)
                tt("Sp", Sp[c][:, :, :], S[:, :, :], small(T, 0, c), ALU.mult)

            def m_S(T, c):
                tt("Sm", Sm[:, :, :], S[:, :, :], small(T, 1, c), ALU.mult)
                wv("Pc", dve, T, c + 1)
                for r in range(2):
                    s = slice(r * DK, (r + 1) * DK)
                    src = B[6][s, :].rearrange("p (a b v) -> p a b v", a=2, b=2)[:, :, r, :]
                    tt("Pt", Pt[s, :, :], src, small(T, 2, c, s), ALU.mult)
                wv("Sm", dve, T, c + 1)
                wv("Pt", dve, T, 2 * c + 2)
                tt("S", S[:, :, :], Sm[:, :, :], Pt[:, :, :], ALU.add)

            def m_o(T):
                n = T.n
                wv("os", dve, T)
                wv("oT", dve, T, back=1)
                tt("osq", osq[0:n, :], os_[0:n, :], os_[0:n, :], ALU.mult)
                wv("osq", dve, T)
                E["so"].done(dve.tensor_reduce(so[0:n, :], osq[0:n, :].rearrange("p (a v) -> p a v", a=H), AX, ALU.add))
                wv("so", dve, T)
                E["mso"].done(dve.tensor_scalar(mso[0:n, :], so[0:n, :], 1.0 / DV, EPS, ALU.mult, ALU.add))
                wv("sg", dve, T)
                tt("on1", os_[0:n, :], os_[0:n, :], sg[T.par][0:n, :], ALU.mult)
                wv("rso", dve, T)
                wv("on1", dve, T)
                tt("on", osq[0:n, :].rearrange("p (a v) -> p a v", a=H),
                   os_[0:n, :].rearrange("p (a v) -> p a v", a=H),
                   rso[0:n, :].unsqueeze(2).to_broadcast([n, H, DV]), ALU.mult)

            def b_x1(T):
                dve.wait_ge(xr_in, T.t * 16 + 16)
                for half in range(2):
                    c = slice(half * 512, (half + 1) * 512)
                    wv("mix", dve, T, half + 1)
                    tt("x1", xr[0:T.n, c], B[4 + half][0:T.n, :], xr[0:T.n, c], ALU.add)

            def b_h(T):
                wv("ss2", dve, T)
                E["ms2"].done(dve.tensor_scalar(ms2[0:T.n, :], ss2[0:T.n, :], 1.0 / D, EPS, ALU.mult, ALU.add))
                wv("rs2", dve, T)
                wv("x1", dve, T)
                E["h"].done(dve.scalar_tensor_tensor(h[0:T.n, :], xr[0:T.n, :], rs2[0:T.n, 0:1], n2[0:T.n, :],
                                                     ALU.mult, ALU.mult))

            def b_top(T):
                n = T.n
                wv("lgp", dve, T)
                tt("lg", lg[0:n, :], B[5][0:n, 0:NE], b_r[0:n, :], ALU.add)
                pairs = T.pair * 64
                if not (isinstance(pairs, int) and pairs == 0):
                    dve.wait_ge(slot_st[T.par], pairs)
                wv("lg", dve, T)
                tok = token_no[:, PT:NT] if T.kind == "s" else token_no[:, bass.ds(T.t, 1)]
                E["tokid"].done(dve.tensor_copy(meta[T.par][0:n, :, 0], tok[0:n, :].to_broadcast([n, TOPK])))
                E["top"].done(dve.max(top[0:n, :], lg[0:n, :]))
                wv("top", dve, T)
                E["ng"].done(dve.tensor_scalar(ng[0:n, :], top[0:n, 0:1], -1.0, None, ALU.mult))
                E["idx"].done(dve.max_index(idx[0:n, :], top[0:n, :], lg[0:n, :]))
                wv("idx", dve, T)
                E["idf"].done(dve.tensor_copy(idf[0:n, :], idx[0:n, 0:TOPK]))
                wv("idf", dve, T)
                tt("oh", oh[0:n, :, :], expert_no[0:n, :].rearrange("p (k e) -> p k e", k=TOPK),
                   idf[0:n, :].unsqueeze(2).to_broadcast([n, TOPK, NE]), ALU.is_equal)
                wv("oh", dve, T)
                wv("rank", dve, T, back=1)
                E["sel"].done(dve.tensor_reduce(sel[0:n, :], oh[0:n, :, :].rearrange("p k e -> p e k"), AX, ALU.add))

            def b_gates(T):
                n = T.n
                wv("e4", dve, T)
                E["rs4"].done(dve.reciprocal(rs4[0:n, :], sum4[0:n, :]))
                wv("rs4", dve, T)
                E["gate"].done(dve.tensor_scalar(meta[T.par][0:n, :, 1].bitcast(F32), e4[0:n, :], rs4[0:n, 0:1],
                                                 None, ALU.mult))

            def b_slot(T):
                n = T.n
                wv("rank", dve, T)
                tt("ohr", ohr[0:n, :, :], B[6][0:n, 0:NE].unsqueeze(1).to_broadcast([n, TOPK, NE]), oh[0:n, :, :],
                   ALU.mult)
                wv("sel", dve, T)
                tt("selsum", selsum[0:n, :], selsum[0:n, :], sel[0:n, :], ALU.add)
                wv("ohr", dve, T)
                E["r4"].done(dve.tensor_reduce(r4[0:n, :], ohr[0:n, :, :], AX, ALU.add))
                wv("r4", dve, T)
                E["slotf"].done(dve.scalar_tensor_tensor(slotf[0:n, :], idf[0:n, :], float(REGION), r4[0:n, :],
                                                         ALU.mult, ALU.add))
                wv("slotf", dve, T)
                E["slot"].done(dve.tensor_copy(slot[T.par][0:n, :], slotf[0:n, :]))

            def tile(T):
                N, M, L = T.later(1), T.later(2), T.later(-1)
                m_Sp(T, 0)
                m_AT(T)
                if L:
                    b_gates(L)
                    b_slot(L)
                m_S(T, 0)
                m_Sp(T, 1)
                f_gate(N)
                m_S(T, 1)
                m_o(T)
                f_qd(N)
                if M:
                    f_ms(M)
                b_x1(T)
                if M:
                    f_xn(M)
                b_h(T)
                f_og(N)
                b_top(T)

            memo.done(dve.memset(neghalf[:, :], -0.5))
            for buf in (S, selsum, ATs, kdTz, qdz[0], qdz[1]):
                memo.done(dve.memset(buf[tuple([slice(None)] * len(buf.shape))], 0.0))
            dve.wait_ge(first_sem, 16 * N_FIRST)
            memo.wait(dve, 0, 7)
            T = Tile(0, 0)
            f_ms(T)
            f_xn(T)
            f_ms(T.later(1))
            f_xn(T.later(1))
            f_gate(T)
            f_qd(T)
            dve.wait_ge(c_sem, 16 * N_CONST)
            dve.wait_ge(w_sem["pool"], 16)
            memo.done(dve.tensor_tensor(w_pool[:, :, :].rearrange("p g e -> p (g e)"),
                                        w_pool[:, :, :].rearrange("p g e -> p (g e)"), pscale[:, :], ALU.mult))
            memo.wait(dve, 0, 8)
            f_og(T)
            in_order(dve, tile)
            b_gates(Tile(PT // 2 - 1, 1))
            b_slot(Tile(PT // 2 - 1, 1))
            T = Tile(PT // 2, 0, "s")
            wv("qdz", dve, T)
            wv("og", dve, T)
            memo.done(dve.memset(Q8, 0.0))
            memo.wait(dve, 0, 9)
            for b in range(NSEQ):
                s_misc.done(dve.tensor_copy(Q8[:, :, b, b * LSEQ:(b + 1) * LSEQ],
                                            qdz[0][:, :, b * LSEQ:(b + 1) * LSEQ]))
            wv("kdT", dve, T)
            wv("o", dve, T, back=1)
            s_misc.done(dve.memset(ATs[0:NS, :, 0:NS], 0.0))
            s_misc.wait(dve, 0, NSEQ + 1)
            for s in (slice(0, NS // 2), slice(NS // 2, NS)):
                E["ATs"].done(dve.copy_predicated(ATs[s, :, 0:NS],
                                                  causal_s[s, :].rearrange("p (a i) -> p a i", a=H),
                                                  B[4][s, 0:H * NS].rearrange("p (a i) -> p a i", a=H)))
            for b in range(NSEQ):
                s_T8.done(dve.tensor_scalar(kdT8[:, b, :], B[4][0:NS, 256:512], seq_of[:, b:b + 1], None, ALU.mult))
            wv("esm", dve, T, 1)
            wv("o", dve, T)
            def update(bs):
                for b in bs:
                    s_P8.wait(dve, 0, b + 1)
                    for r in range(2):
                        s = slice(r * DK, (r + 1) * DK)
                        src = B[S_BANKS[b % len(S_BANKS)]][s, :].rearrange(
                            "p (a b v) -> p a b v", a=2, b=2)[:, :, r, :]
                        s_misc.done(dve.tensor_tensor(S0[s, b, :, :], src, S0[s, b, :, :], ALU.add))
                    s_misc.wait(dve, 0, NSEQ + 3 + 2 * b)
                    el = els[:, b::NSEQ].unsqueeze(2).to_broadcast([P, 2, DV])
                    s_S8.done(dve.tensor_tensor(S0[:, b, :, :], S0[:, b, :, :], el, ALU.mult))

            m_o(T)
            update(range(len(S_BANKS)))
            b_x1(T)
            b_h(T)
            update(range(len(S_BANKS), NSEQ))
            b_top(T)
            b_gates(T)
            b_slot(T)
            s_cnt.wait(dve, 0)
            step = [0]

            def chain(ins):
                step[0] += 1
                s_tab.done(ins)
                s_tab.wait(dve, 0, step[0])

            dve.wait_ge(no_sem, 16)
            chain(dve.tensor_copy(cnt, B[6][0:NTAB, 0:NE]))
            chain(dve.tensor_scalar(nch, cnt, 0.0, None, ALU.is_gt))
            for m in range(1, CPE):
                chain(dve.scalar_tensor_tensor(nch, cnt, float(m * CHUNK), nch, ALU.is_gt, ALU.add))
            chain(dve.tensor_tensor_scan(end, ones[0:NTAB, 0:NE], nch, 0.0, ALU.mult, ALU.add))
            chain(dve.tensor_scalar(ge, end, cn, None, ALU.is_le))
            chain(dve.tensor_tensor(gen, ge, nch, ALU.mult))
            chain(dve.tensor_reduce(ex, ge, AX, ALU.add))
            chain(dve.tensor_reduce(bs, gen, AX, ALU.add))
            chain(dve.tensor_scalar(ex, ex, float(NE - 1), None, ALU.min))
            chain(dve.tensor_tensor(bs, cn, bs, ALU.subtract))
            chain(dve.tensor_scalar(bs, bs, float(CPE - 1), float(CHUNK), ALU.min, ALU.mult))
            chain(dve.scalar_tensor_tensor(ge, expert_no[0:NTAB, 0:NE], ex, cnt, ALU.is_equal, ALU.mult))
            chain(dve.tensor_reduce(sz, ge, AX, ALU.add))
            chain(dve.tensor_tensor(sz, sz, bs, ALU.subtract))
            chain(dve.tensor_scalar(sz, sz, 0.0, float(CHUNK), ALU.max, ALU.min))
            chain(dve.scalar_tensor_tensor(bs, ex, float(REGION), bs, ALU.mult, ALU.add))
            assert step[0] == TAB_STEPS
            chain(dve.tensor_copy(tab[0:1, COUNT:COUNT + 1], end[0:1, NE - 1:NE]))
            rows_turned.wait(dve, TABLE)
            chain(dve.tensor_copy(tab[0:1, 0:COUNT], B[6][0:1, 0:COUNT]))

        @block.gpsimd
        def _(pool):
            def root(T, src, dst, e_in, e, m):
                wv(e_in, pool, T)
                E[e].done(pool.tensor_tensor(dst[0:T.n, :], src[0:T.n, :], neghalf[0:T.n, 0:m], ALU.pow))

            one = ones[:, 0:NG * BUF].rearrange("p (g r) -> p g r", g=NG)

            def f_pool(T):
                n = T.n
                if T.kind == "p":
                    cur = ux[T.par]
                    if T.static and T.t == 0:
                        E["hist"].done(pool.memset(cur[:, :, 0:BUF], 0.0))
                    else:
                        wv("uxe", pool, T, back=1)
                        last = ux[1 - T.par][:, :, P:P + BUF]
                        E["hist"].done(pool.tensor_tensor(cur[:, :, 0:BUF], last, one, ALU.mult))
                    wv("uxe", pool, T)
                    wv("hist", pool, T)
                    L, s = P, 1
                    src = cur[:, :, :].unsqueeze(2)
                else:
                    rows_kept.wait(pool, OLD)
                    s_misc2.wait(pool, 0)
                    L, s = LSEQ, NSEQ
                    src = uxs[:, :, :, :]
                W = BUF + L
                A = pa[:, :, 0:s * W].rearrange("p g (s w) -> p g s w", s=s)
                B_ = pb[:, :, 0:s * W].rearrange("p g (s w) -> p g s w", s=s)

                def grow(dst, a, g0, lo, step, k):
                    E["pool"].done(pool.tensor_tensor(dst[:, g0:, :, lo:W], a[:, g0:, :, lo:W],
                                                      a[:, g0:, :, lo - step:W - step], ALU.add))
                    wv("pool", pool, T, k)

                grow(A, src, 0, 1, 1, 1)
                grow(B_, A, 1, 3, 2, 2)
                grow(A, B_, 2, 7, 4, 3)
                grow(B_, A, 3, 15, 8, 4)
                wv("zp", pool, T, back=2)
                d4 = dT[T.par][:, :, 0:n].rearrange("p g (s l) -> p g s l", s=s)
                i4 = inv[:, :, 0:n].rearrange("p g (s l) -> p g s l", s=s)
                for q, a in enumerate((A, B_)):
                    E["mean"].done(pool.tensor_tensor(d4[:, q::2], a[:, q::2, :, BUF:], i4[:, q::2], ALU.mult))
                wv("mean", pool, T)
                E["dT"].done(pool.tensor_tensor(d4, d4, src[:, :, :, BUF:], ALU.subtract))
                rest = inv_rest[:, :].rearrange("p (g r) -> p g r", g=NG)
                E["pool"].done(pool.tensor_tensor(inv[:, :, 0:BUF], rest, one, ALU.mult))
                wv("pool", pool, T)

            def b_routed(T, back=0):
                wv("slot", pool, T, back=back)
                wv("gate", pool, T, back=back)
                wv("tokid", pool, T, back=back)

            def b_scatter(par, n):
                for k in range(TOPK):
                    pool.indirect_dma_start(
                        X["slots"][:, :], bass.IndirectOffsetOnAxis(slot[par][0:n, k:k + 1], 0),
                        meta[par][0:n, k, :], None).then_inc(slot_st[par], 16)

            def tile(T):
                b_routed(T, back=1)
                root(T, mso, rso, "mso", "rso", 4)
                if T.later(-1):
                    b_scatter(1 - T.par, P)
                f_pool(T.later(1))
                if T.later(2):
                    root(T.later(2), ms1, rs1, "ms1", "rs1", 1)
                root(T, ms2, rs2, "ms2", "rs2", 1)

            memo.wait(pool, 0, 1)
            for T in (Tile(0, 0), Tile(0, 1)):
                root(T, ms1, rs1, "ms1", "rs1", 1)
            pool.wait_ge(c_sem, 16 * N_CONST)
            f_pool(Tile(0, 0))
            pool.wait_ge(init_sem, 48)
            in_order(pool, tile)
            b_routed(Tile(PT // 2 - 1, 1))
            T = Tile(PT // 2, 0, "s")
            root(T, mso, rso, "mso", "rso", 4)
            b_scatter(1, P)
            root(T, ms2, rs2, "ms2", "rs2", 1)
            b_routed(T)
            b_scatter(0, NS)


def experts(nc, I, X, tab):
    with ExitStack() as ctx:
        def sb(name, shape, dt=F32):
            return ctx.enter_context(nc.sbuf_tensor(name, shape, dt))

        def sem(name):
            return ctx.enter_context(nc.semaphore(name))

        def ev(name, per=1):
            return Event(ctx, nc, name, per)

        B = [ctx.enter_context(nc.psum_tensor(f"ebank{b}", [P, 512], F32)) for b in range(7)]
        raw = [sb(f"raw{b}", [P, PIECE]) for b in range(2)]
        wh = [sb(f"wh{b}", [P, PIECE // 2], F32R) for b in range(4)]
        wl = [sb(f"wl{b}", [P, PIECE // 2], F32R) for b in range(4)]
        xg = sb("xg", [P, 3, D])
        xh = sb("xh", [P, KD, CHUNK], F32R)
        xl = sb("xl", [P, KD, CHUNK], F32R)
        ahl = sb("ahl", [P, KD, 2 * CHUNK], F32R)
        g_, u_, u2, gu_, sg_ = (sb(n, [P, CHUNK]) for n in ("gate", "up", "up1", "gateup", "sig"))
        a_ = [sb(f"act{b}", [P, CHUNK]) for b in range(2)]
        osb = sb("osb", [P, 3, D])
        bd = sb("b_down_rows", [P, D])
        ident = sb("eident", [P, P])
        bgu_rows = sb("bgu_rows", [NE, 2 * FF])
        bgu = sb("bgu", [P, 2 * KD, NE])
        bcur = sb("bcur", [P, 2 * KD])
        mnx = sb("slots_next", [P, 3, 2], I32)
        mcur = sb("slots_now", [P, 3, 2], I32)

        raw_in = [sem("raw_in0"), sem("raw_in1")]
        ld, meta_in, x_in, bd_in, sc = (sem(n) for n in ("loaded", "slots_in", "rows_in", "b_down_in", "rows_added"))
        bturn, bkept = ev("bias_turned"), ev("bias_kept")
        hi, lo = ev("w_hi", 12), ev("w_lo", 12)
        trx, xhe, xle = ev("x_turned", 8), ev("x_hi", 8), ev("x_lo", 8)
        gu, dn = ev("gate_up_done", 8), ev("down_done", 6)
        mc, bc = ev("slots_now_set", 2), ev("bias_now_set")
        g1, u1, u1b, gm, ac = (ev(n, 8) for n in ("gate_clamped", "up_clamped", "up_plus1", "gate_times_up", "act_done"))
        sgm, ahe, ale = ev("sigmoid_done", 8), ev("act_hi", 8), ev("act_lo", 8)
        ob, osc = ev("out_biased", 6), ev("out_scaled", 6)
        ob2 = ev("out_high_biased", 2)
        mc0, last = ev("first_slots_set"), ev("last_rows_scaled")
        carry = sb("carry", [1, 1])

        wgu = I["w_gate_up"][0].rearrange("e (k p) n -> e p k n", p=P)
        wdn = I["w_down"][0].rearrange("e (k p) n -> e p k n", p=P)

        def raw_part(q):
            r = raw[q // 2 % 2]
            if q % 12 < 8:
                return r[:, :].rearrange("p (gk c) -> p gk c", c=256)[:, :, q % 2 * P:q % 2 * P + P]
            return r[:, q % 2 * (PIECE // 2):(q % 2 + 1) * (PIECE // 2)].rearrange("p (gk c) -> p gk c", c=P)

        def part(w, q):
            return w[q % 4][:, :].rearrange("p (gk c) -> p gk c", c=P)

        def n_chunks(eng):
            return eng.value_load(tab[0:1, COUNT:COUNT + 1], min_val=1, max_val=MAXC)

        def expert_of(eng, i):
            return eng.value_load(tab[0:1, bass.ds(i, 1)], min_val=0, max_val=NE - 1)

        block = ctx.enter_context(nc.Block())

        @block.sync
        def _(sp):
            def piece(e, i, p):
                sp.wait_ge(lo.sem, i * 12 + (2 * p + 2))
                s = p % 2
                if p < 4:
                    v = raw[s][:, :].rearrange("p (g k c) -> p g k c", g=2, k=KD)
                    for g in range(2):
                        sp.dma_start(v[:, g], wgu[e, :, :, g * FF + p * 256:g * FF + (p + 1) * 256]).then_inc(raw_in[s], 16)
                else:
                    v = raw[s][:, :].rearrange("p (k c) -> p k c", k=KD)
                    for q in range(2):
                        sp.dma_start(v[:, 4 * q:4 * q + 4], wdn[e, :, 4 * q:4 * q + 4, (p - 4) * 512:(p - 3) * 512]).then_inc(raw_in[s], 16)

            sp.dma_start(ident[:, :], I["ident"]).then_inc(ld, 16)
            sp.dma_start(bgu_rows[:, :], I["b_gate_up"][0]).then_inc(ld, 16)
            n = n_chunks(sp)
            with sp.Fori(0, n) as i:
                e = expert_of(sp, i)
                for p in range(6):
                    piece(e, i, p)
                    if p == 2:
                        ob.wait(sp, i, 3)
                        sp.dma_start(bd[:, :], I["b_down"][0, bass.ds(e, 1), :].to_broadcast([P, D])).then_inc(bd_in, 16)
            e = expert_of(sp, n)
            for p in range(2):
                piece(e, n, p)

        @block.tensor
        def _(pe):
            def turn_x(i, k):
                for s0, m in SUBS:
                    ins = pe.transpose(B[k % 4][:, s0:s0 + m], xg[0:m, s0 // P, k * P:(k + 1) * P], ident[0:m, 0:m])
                trx.done(ins)

            def gate_up(i, j, width):
                jj = j % 2
                pe.wait_ge(lo.sem, i * 12 + (j + 5))
                if j >= 2:
                    u1.wait(pe, i, j - 1)
                h_, l_ = (w[j % 4][:, :].rearrange("p (g k c) -> p g k c", g=2, k=KD) for w in (wh, wl))
                for g in range(2):
                    out = B[2 * jj + g][:, 0:width]
                    for k in range(KD):
                        if j == 0 and g == 0 and k >= 5:
                            xle.wait(pe, i, k + 1)
                        pe.matmul(out, h_[:, g, k, :], xh[:, k, 0:width], start=(k == 0), stop=False)
                        pe.matmul(out, h_[:, g, k, :], xl[:, k, 0:width], start=False, stop=False)
                        ins = pe.matmul(out, l_[:, g, k, :], xh[:, k, 0:width], start=False, stop=(k == KD - 1))
                gu.done(ins)

            def down(i, half, s, ks=range(KD)):
                s0, m = SUBS[s]
                if ks[0] == 0:
                    pe.wait_ge(ob.sem, i * 6 + (3 * half + s + 1))
                out = B[4 + s][:, :]
                for k in ks:
                    if s == 0 and k % 4 == 0:
                        pe.wait_ge(lo.sem, i * 12 + (8 + 2 * half + k // 4 + 5))
                    if half == 0 and s == 0:
                        ale.wait(pe, i, k + 1)
                    q = (2 * half + k // 4) % 4
                    h_, l_ = (w[q][:, :].rearrange("p (k c) -> p k c", k=4) for w in (wh, wl))
                    first, last = k == 0, k == KD - 1
                    if s == 2:
                        both = ahl[:, k, TAIL:CHUNK + MT]
                        pe.matmul(out, both, h_[:, k % 4, :], start=first, stop=False)
                        ins = pe.matmul(out, both, l_[:, k % 4, :], start=False, stop=last)
                        continue
                    low = CHUNK + MT + s0
                    pe.matmul(out, ahl[:, k, s0:s0 + m], h_[:, k % 4, :], start=first, stop=False)
                    pe.matmul(out, ahl[:, k, s0:s0 + m], l_[:, k % 4, :], start=False, stop=False)
                    ins = pe.matmul(out, ahl[:, k, low:low + m], h_[:, k % 4, :], start=False, stop=last)
                if ks[-1] == KD - 1:
                    dn.done(ins)

            def no_down(i, half, s):
                pe.wait_ge(ob.sem, i * 6 + (3 * half + s + 1))
                dn.done(pe.transpose(B[4 + s][:, 0:P], ident[:, :], ident[:, :]))

            def chunk(i, width):
                xle.wait(pe, i, 6)
                for j in range(8):
                    if j == 1:
                        xle.wait(pe, i)
                    gate_up(i, j, width)
                last = down if width > TAIL else no_down
                for ks in (range(KD - 1), range(KD - 1, KD)):
                    for s in range(2):
                        down(i, 0, s, ks)
                last(i, 0, 2)
                u1.wait(pe, i)
                pe.wait_ge(x_in, i * 48 + 96)
                for k in range(4):
                    turn_x(i + 1, k)
                down(i, 1, 0)
                for k in range(4, 8):
                    xle.wait(pe, i + 1, k - 3)
                    turn_x(i + 1, k)
                down(i, 1, 1)
                last(i, 1, 2)

            pe.wait_ge(ld, 32)
            for q in range(4):
                pe.transpose(B[6][:, q * P:(q + 1) * P], ident[:, :], ident[:, :])
            for q in range(2):
                for jj in range(8):
                    ins = pe.transpose(B[4 + q][:, jj * NE:(jj + 1) * NE],
                                       bgu_rows[:, (8 * q + jj) * P:(8 * q + jj + 1) * P], ident[0:NE, 0:NE])
                bturn.done(ins)
            pe.wait_ge(x_in, 48)
            for k in range(KD):
                if k >= 4:
                    xle.wait(pe, 0, k - 3)
                turn_x(0, k)
            bkept.wait(pe, 0, 2)
            n = n_chunks(pe)
            with pe.Fori(0, n) as i:
                size = pe.value_load(tab[0:1, bass.ds(i + SIZES, 1)], min_val=0, max_val=CHUNK)

                def narrowest(widths):
                    if len(widths) == 1:
                        chunk(i, widths[0])
                        return
                    with pe.If(size < widths[0] + 1):
                        chunk(i, widths[0])
                    with pe.Else():
                        narrowest(widths[1:])
                narrowest(WIDTHS)

        @block.scalar
        def _(act):
            def w_hi(i, q):
                if 4 <= q < 12:
                    gu.wait(act, i, q - 3)
                act.wait_ge(raw_in[q // 2 % 2], i * 96 + 32 * (q // 4 + 1))
                hi.done(act.activation(part(wh, q), raw_part(q), ACT.Copy))

            def x_hi(i, k):
                trx.wait(act, i, k + 1)
                xhe.done(act.activation(xh[:, k, :], B[k % 4][:, 0:CHUNK], ACT.Copy))

            def sigmoid(i, j):
                g1.wait(act, i, j + 1)
                if j == 0:
                    ob.wait(act, i, 3)
                else:
                    ac.wait(act, i, j)
                sgm.done(act.activation(sg_[:, :], g_[:, :], ACT.Sigmoid, scale=ALPHA))

            def a_hi(i, j):
                ac.wait(act, i, j + 1)
                ahe.done(act.activation(ahl[:, j, 0:CHUNK], a_[j % 2][:, :], ACT.Copy))

            def scale(i, half, s):
                s0, m = SUBS[s]
                ob.wait(act, i, 3 * half + s + 4)
                v = osb[0:m, s, half * 512:(half + 1) * 512]
                osc.done(act.activation(v, v, ACT.Copy, scale=mcur[0:m, s, 1:2].bitcast(F32)))

            w_hi(0, 0)
            w_hi(0, 1)
            for k in range(KD):
                x_hi(0, k)
            w_hi(0, 2)
            w_hi(0, 3)
            mc0.wait(act, 0, 4)
            osc.done(act.activation(carry[:, :], carry[:, :], ACT.Copy))
            osc.wait(act, 0, 1)
            n = n_chunks(act)
            with act.Fori(0, n) as i:
                for j in range(8):
                    w_hi(i, j + 4)
                    sigmoid(i, j)
                    a_hi(i, j)
                for s in range(3):
                    scale(i, 0, s)
                for k in range(4):
                    x_hi(i + 1, k)
                dn.wait(act, i, 3)
                w_hi(i + 1, 0)
                w_hi(i + 1, 1)
                scale(i, 1, 0)
                for k in range(4, 8):
                    x_hi(i + 1, k)
                scale(i, 1, 1)
                scale(i, 1, 2)
                dn.wait(act, i, 6)
                w_hi(i + 1, 2)
                w_hi(i + 1, 3)

        @block.vector
        def _(dve):
            def w_lo(i, q):
                hi.wait(dve, i, q + 1)
                lo.done(dve.tensor_tensor(part(wl, q), raw_part(q), part(wh, q).bitcast(F32), ALU.subtract))

            def x_lo(i, k):
                xhe.wait(dve, i, k + 1)
                xle.done(dve.tensor_tensor(xl[:, k, :], B[k % 4][:, 0:CHUNK], xh[:, k, :].bitcast(F32), ALU.subtract))

            def clamp(i, j):
                G, U = B[2 * (j % 2)][:, 0:CHUNK], B[2 * (j % 2) + 1][:, 0:CHUNK]
                gu.wait(dve, i, j + 1)
                g1.done(dve.tensor_scalar(g_[:, :], G, bcur[:, j:j + 1], LIMIT, ALU.add, ALU.min))
                u1.done(dve.tensor_scalar(u_[:, :], U, bcur[:, KD + j:KD + j + 1], LIMIT, ALU.add, ALU.min))
                u1.wait(dve, i, j + 1)
                u1b.done(dve.tensor_scalar(u2[:, :], u_[:, :], -LIMIT, 1.0, ALU.max, ALU.add))
                g1.wait(dve, i, j + 1)
                u1b.wait(dve, i, j + 1)
                gm.done(dve.tensor_tensor(gu_[:, :], g_[:, :], u2[:, :], ALU.mult))

            def gated(i, j):
                gm.wait(dve, i, j + 1)
                sgm.wait(dve, i, j + 1)
                if j >= 2:
                    ale.wait(dve, i, j - 1)
                ac.done(dve.tensor_tensor(a_[j % 2][:, :], gu_[:, :], sg_[:, :], ALU.mult))

            def out_bias(i, half, s):
                s0, m = SUBS[s]
                c = slice(half * 512, (half + 1) * 512)
                dn.wait(dve, i, 3 * half + s + 1)
                if half == 0 and s == 0:
                    dve.wait_ge(bd_in, i * 16 + 16)
                    dve.wait_ge(sc, i * 48 + 48)
                high = dve.tensor_tensor(osb[0:m, s, c], B[4 + s][0:m, :], bd[0:m, c], ALU.add)
                if s < 2:
                    ob.done(high)
                    return
                ob2.done(high)
                ob2.wait(dve, i, half + 1)
                ob.done(dve.tensor_tensor(osb[0:m, s, c], B[4 + s][m:2 * m, :], osb[0:m, s, c], ALU.add))

            def take_slots(i):
                dve.wait_ge(meta_in, i * 48 + 48)
                dve.wait_ge(x_in, i * 48 + 48)
                dve.wait_ge(sc, i * 48 + 48)
                mc.done(dve.tensor_copy(mcur[:, 0:2, :], mnx[:, 0:2, :]))
                mc.done(dve.tensor_copy(mcur[0:64, 2, :], mnx[0:64, 2, :]))

            for q in range(2):
                lo.done(dve.memset(u2[:, q:q + 1], 0.0))
            for q in range(4, 7):
                ob.done(dve.memset(u2[:, q:q + 1], 0.0))
            for q in range(2):
                bturn.wait(dve, 0, q + 1)
                bkept.done(dve.tensor_copy(bgu[:, 8 * q:8 * q + 8, :],
                                           B[4 + q][:, 0:8 * NE].rearrange("p (j e) -> p j e", j=8)))
            bkept.wait(dve, 0, 2)
            ob.wait(dve, 0, 3)
            dve.wait_ge(x_in, 48)
            for q in range(2, 4):
                lo.done(dve.memset(u2[:, q:q + 1], 0.0))
            lo.wait(dve, 0, 4)
            w_lo(0, 0)
            w_lo(0, 1)
            for k in range(KD):
                x_lo(0, k)
            w_lo(0, 2)
            w_lo(0, 3)
            dve.wait_ge(meta_in, 48)
            mc0.done(dve.memset(osb[:, :, :], 0.0))
            mc0.done(dve.memset(carry[:, :], 0.0))
            mc0.done(dve.tensor_copy(mcur[:, 0:2, :], mnx[:, 0:2, :]))
            mc0.done(dve.tensor_copy(mcur[0:64, 2, :], mnx[0:64, 2, :]))
            mc0.wait(dve, 0, 4)
            n = n_chunks(dve)
            with dve.Fori(0, n) as i:
                e = expert_of(dve, i)
                bc.done(dve.tensor_copy(bcur[:, :], bgu[:, :, bass.ds(e, 1)].rearrange("p j o -> p (j o)")))
                bc.wait(dve, i)
                for j in range(8):
                    clamp(i, j)
                    if j == 7:
                        gated(i, j)
                        w_lo(i, j + 4)
                    else:
                        w_lo(i, j + 4)
                        gated(i, j)
                    if j == 3:
                        take_slots(i)
                for s in range(3):
                    out_bias(i, 0, s)
                for k in range(4):
                    x_lo(i + 1, k)
                w_lo(i + 1, 0)
                w_lo(i + 1, 1)
                out_bias(i, 1, 0)
                for k in range(4, 8):
                    x_lo(i + 1, k)
                out_bias(i, 1, 1)
                out_bias(i, 1, 2)
                w_lo(i + 1, 2)
                w_lo(i + 1, 3)

        @block.gpsimd
        def _(pool):
            def load_slots(i):
                r = pool.value_load(tab[0:1, bass.ds(i + NTAB, 1)], min_val=0, max_val=SLOTS - CHUNK)
                for s, (s0, m) in enumerate(SUBS):
                    pool.dma_start(mnx[0:m, s, :], X["slots"][bass.ds(r + s0, m), :]).then_inc(meta_in, 16)

            def gather():
                for s, (s0, m) in enumerate(SUBS):
                    pool.indirect_dma_start(
                        xg[0:m, s, :], None, X["h"][:, :],
                        bass.IndirectOffsetOnAxis(mnx[0:m, s, 0:1].bitcast(U32), 0)).then_inc(x_in, 16)

            def act_lo(i, j):
                ahe.wait(pool, i, j + 1)
                for c in (slice(TAIL, CHUNK), slice(0, TAIL)):
                    low = CHUNK if c.start else CHUNK + MT
                    ins = pool.tensor_tensor(ahl[:, j, low:low + c.stop - c.start], a_[j % 2][:, c],
                                             ahl[:, j, c].bitcast(F32), ALU.subtract)
                ale.done(ins)

            def add_rows():
                for s, (s0, m) in enumerate(SUBS):
                    pool.indirect_dma_start(
                        X["y"][:, :], bass.IndirectOffsetOnAxis(mcur[0:m, s, 0:1].bitcast(U32), 0),
                        osb[0:m, s, :], None, compute_op=ALU.add).then_inc(sc, 16)

            load_slots(0)
            pool.wait_ge(meta_in, 48)
            gather()
            mc0.wait(pool, 0, 4)
            n = n_chunks(pool)
            with pool.Fori(0, n) as i:
                osc.wait(pool, i, 1)
                act_lo(i, 0)
                add_rows()
                act_lo(i, 1)
                act_lo(i, 2)
                act_lo(i, 3)
                mc.wait(pool, i)
                act_lo(i, 4)
                load_slots(i + 1)
                pool.wait_ge(meta_in, i * 48 + 96)
                trx.wait(pool, i)
                act_lo(i, 5)
                gather()
                act_lo(i, 6)
                act_lo(i, 7)
            osc.wait(pool, n, 1)
            mc.wait(pool, n - 1)
            last.done(pool.tensor_tensor(carry[:, :], carry[:, :], carry[:, :], ALU.add))
            add_rows()
            pool.wait_ge(sc, n * 48 + 48)
            pool.wait_ge(x_in, n * 48 + 48)

def final(nc, I, O, X):
    NB, LAG = 4, 2
    with ExitStack() as ctx:
        def sb(name, shape, dt=F32):
            return ctx.enter_context(nc.sbuf_tensor(name, shape, dt))

        def ev(name, per=1):
            return Event(ctx, nc, name, per)

        nf = sb("final_rows", [P, D])
        neghalf = sb("fneghalf", [P, 1])
        y = [sb(f"y{b}", [P, D]) for b in range(NB)]
        yo = [sb(f"yo{b}", [P, D]) for b in range(NB)]
        junk = sb("fjunk", [P, D])
        ss, ms, rs = ([sb(f"f{n}{b}", [P, 1]) for b in range(NB)] for n in ("ss", "ms", "rs"))
        y_in = [ctx.enter_context(nc.semaphore(f"y_in{b}")) for b in range(NB)]
        out_st = [ctx.enter_context(nc.semaphore(f"out_stored{b}")) for b in range(NB)]
        nf_in = ctx.enter_context(nc.semaphore("final_norm_in"))
        ess, ems, ers, eo = (ev(n) for n in ("f_ss", "f_ms", "f_rs", "f_out"))
        block = ctx.enter_context(nc.Block())

        def every(eng, f):
            for b in range(NB):
                f(0, b, P)
            with eng.Fori(1, PT // NB) as g:
                for b in range(NB):
                    f(g, b, P)
            f(PT // NB, 0, NS)

        @block.sync
        def _(sp):
            sp.dma_start(nf[:, :], I["final_norm"].partition_broadcast(P)).then_inc(nf_in, 16)

            def store(t, b, n):
                eo.wait(sp, t)
                dst = O["y_p"][0][bass.ds(t * P, P), :] if n == P else O["y_s"].rearrange("b l d -> (b l) d")
                sp.dma_start(dst, yo[b][0:n, :]).then_inc(out_st[b], 16)

            def tile(g, b, n):
                t = g * NB + b
                eo.wait(sp, t - NB)
                src = X["y"][bass.ds(t * P, P), :] if n == P else X["y"][SEQ:TOK, :]
                sp.dma_start(y[b][0:n, :], src).then_inc(y_in[b], 16)
                if not (isinstance(t, int) and t < LAG):
                    store(t - LAG, (b - LAG) % NB, P)

            every(sp, tile)
            for t in range(PT + 1 - LAG, PT + 1):
                store(t, t % NB, P if t < PT else NS)
            for b in range(NB):
                sp.wait_ge(out_st[b], 16 * len(range(b, PT + 1, NB)))

        @block.scalar
        def _(act):
            def square(g, b, n):
                t = g * NB + b
                act.wait_ge(y_in[b], g * 16 + 16)
                ems.wait(act, t - NB)
                ess.wait(act, t - 1)
                ess.done(act.activation(junk[0:n, :], y[b][0:n, :], ACT.Square, accum_out=ss[b][0:n, :]))
            every(act, square)

        @block.gpsimd
        def _(pool):
            pool.memset(neghalf[:, :], -0.5).then_inc(nf_in, 1)
            pool.wait_ge(nf_in, 17)

            def root(g, b, n):
                t = g * NB + b
                ems.wait(pool, t)
                eo.wait(pool, t - NB)
                ers.done(pool.tensor_tensor(rs[b][0:n, :], ms[b][0:n, :], neghalf[0:n, :], ALU.pow))
            every(pool, root)

        @block.vector
        def _(dve):
            dve.wait_ge(nf_in, 17)

            def mean(g, b, n):
                t = g * NB + b
                ess.wait(dve, t)
                ers.wait(dve, t - NB)
                ems.done(dve.tensor_scalar(ms[b][0:n, :], ss[b][0:n, :], 1.0 / D, EPS, ALU.mult, ALU.add))

            def norm(g, b, n):
                ers.wait(dve, g * NB + b)
                dve.wait_ge(y_in[b], g * 16 + 16)
                if not (isinstance(g, int) and g == 0):
                    dve.wait_ge(out_st[b], g * 16)
                eo.done(dve.scalar_tensor_tensor(yo[b][0:n, :], y[b][0:n, :], rs[b][0:n, 0:1],
                                                 nf[0:n, :], ALU.mult, ALU.mult))

            def tile(g, b, n):
                mean(g, b, n)
                norm(g, b, n)
            every(dve, tile)

def build(nc, I, O):
    X = {
        "slots": nc.dram_tensor("slot_rows", [SLOTS, 2], I32).ap(),
        "h": nc.dram_tensor("h_rows", [ROWS, D], F32).ap(),
        "y": nc.dram_tensor("y_rows", [ROWS, D], F32).ap(),
    }
    with nc.sbuf_tensor("chunk_table", [1, COUNT + 1], I32) as tab:
        mixer(nc, I, O, X, tab)
        experts(nc, I, X, tab)
    final(nc, I, O, X)

_INS = ["x_prompt", "x_sample", "state_gla", "state_pool", "norm1", "w_in", "w_gk2", "b_gk", "gla_norm", "w_pool",
        "pool_scale", "w_o", "norm2", "w_router", "b_router", "w_gate_up", "b_gate_up", "w_down", "b_down",
        "final_norm"]
_OUTS = {"y_p": (1, SEQ, D), "y_s": (NSEQ, LSEQ, D), "gla_p": (1, 1, H, DK, DV), "pool_p": (1, 1, BUF, PW),
         "gla_s": (1, NSEQ, H, DK, DV), "pool_s": (1, NSEQ, BUF, PW)}

def kernel(**inputs):
    import concourse.bacc as _bacc
    from concourse.bass_utils import run_bass_kernel_spmd as _run

    nc = _bacc.Bacc("TRN2", target_bir_lowering=False, num_devices=1)
    arrays = {f"in_{n}": np.ascontiguousarray(inputs[n]) for n in _INS}
    arrays.update({f"in_{n}": a for n, a in constants().items()})
    I = {n[3:]: nc.dram_tensor(n, a.shape, mybir.dt.from_np(a.dtype), kind="ExternalInput").ap()
         for n, a in arrays.items()}
    O = {n: nc.dram_tensor(f"out_{n}", s, F32, kind="ExternalOutput").ap() for n, s in _OUTS.items()}
    build(nc, I, O)
    r = _run(nc, [arrays], core_ids=[0])
    return tuple(r.results[0][f"out_{n}"] for n in _OUTS)
```
